# Optimizing a Trainium2 kernel written in Bass

```python
import math
import jax, jax.numpy as jnp
from jax import lax
import numpy as np
import jax
import jax.numpy as jnp

D_MODEL = 1024
BATCH = 1
SEQ = 256
DEPTH = 1

N_META = 16
CHUNK = 128
META_PAD = (-N_META) % CHUNK
RET_HEADS = 8
RET_DK = 64
RET_DV = 128
RET_QK_W = RET_HEADS * RET_DK
RET_V_W = RET_HEADS * RET_DV
MLA_HEADS = 8
MLA_Q_RANK = 384
MLA_KV_RANK = 256
MLA_NOPE = 64
MLA_ROPE = 32
MLA_DV = 64
MLA_QK = MLA_NOPE + MLA_ROPE
D_FF = ((-(-8 * D_MODEL // 3) + 255) // 256) * 256
ROPE_BASE = 10000.0
RMS_EPS = 1e-6
GN_EPS = 1e-5

SPLIT_SIZES = (RET_QK_W, RET_QK_W, RET_V_W, RET_V_W, MLA_Q_RANK, MLA_KV_RANK, MLA_ROPE, D_MODEL, D_MODEL)
SPLIT_IDX = tuple(int(s) for s in np.cumsum(SPLIT_SIZES)[:-1])
D_IN = int(sum(SPLIT_SIZES))


def _rmsnorm(x, w):
    xf = x.astype(jnp.float32)
    y = xf * lax.rsqrt(jnp.mean(xf * xf, axis=-1, keepdims=True) + RMS_EPS)
    return (y * w.astype(jnp.float32)).astype(x.dtype)

def _rope_tables(pos, dim):
    half = dim // 2
    inv = ROPE_BASE ** (-jnp.arange(half, dtype=jnp.float32) / half)
    ang = pos.astype(jnp.float32)[:, None] * inv[None, :]
    return jnp.cos(ang), jnp.sin(ang)

def _apply_rope(x, cos, sin):
    half = x.shape[-1] // 2
    xf = x.astype(jnp.float32)
    x1, x2 = xf[..., :half], xf[..., half:]
    return jnp.concatenate([x1 * cos - x2 * sin, x1 * sin + x2 * cos], axis=-1).astype(x.dtype)

def _retention_dir(q, k, v, log_gamma, inclusive):
    B, Lp, H, dk = q.shape
    dv = v.shape[-1]
    n = Lp // CHUNK
    qc = q.reshape(B, n, CHUNK, H, dk)
    kc = k.reshape(B, n, CHUNK, H, dk)
    vc = v.reshape(B, n, CHUNK, H, dv)
    lg = log_gamma.astype(jnp.float32)
    idx = jnp.arange(CHUNK, dtype=jnp.float32)
    rel = idx[:, None] - idx[None, :]
    mask = rel >= 0 if inclusive else rel > 0
    dmask = jnp.exp(jnp.where(mask[None], lg[:, None, None] * rel[None], -jnp.inf)).astype(q.dtype)
    scores = jnp.einsum('bnihd,bnjhd->bnhij', qc, kc) * dmask
    inner = jnp.einsum('bnhij,bnjhe->bnihe', scores, vc)
    w_k = jnp.exp(lg[None, :] * (CHUNK - 1 - idx)[:, None]).astype(q.dtype)
    incr = jnp.einsum('bnjhd,jh,bnjhe->nbhde', kc, w_k, vc)
    g_chunk = jnp.exp(lg * CHUNK).astype(incr.dtype)[None, :, None, None]

    def step(state, u):
        return g_chunk * state + u, state

    state0 = jnp.zeros((B, H, dk, dv), incr.dtype)
    _, states_prev = lax.scan(step, state0, incr)
    w_q = jnp.exp(lg[None, :] * (idx + 1.0)[:, None]).astype(q.dtype)
    cross = jnp.einsum('bnihd,ih,nbhde->bnihe', qc, w_q, states_prev)
    return (inner + cross).reshape(B, Lp, H, dv)

def _bidir_retention(q, k, v, decay_f, decay_b):
    lg_f = -jnp.exp(decay_f.astype(jnp.float32))
    lg_b = -jnp.exp(decay_b.astype(jnp.float32))
    pad = ((0, 0), (META_PAD, 0), (0, 0), (0, 0))
    qp, kp, vp = jnp.pad(q, pad), jnp.pad(k, pad), jnp.pad(v, pad)
    fwd = _retention_dir(qp, kp, vp, lg_f, True)
    bwd = jnp.flip(_retention_dir(jnp.flip(qp, 1), jnp.flip(kp, 1), jnp.flip(vp, 1), lg_b, False), 1)
    return (fwd + bwd)[:, META_PAD:]

def _head_group_norm(y, w):
    B, L, H, dv = y.shape
    yf = y.astype(jnp.float32)
    mu = jnp.mean(yf, axis=-1, keepdims=True)
    var = jnp.mean(jnp.square(yf - mu), axis=-1, keepdims=True)
    yn = ((yf - mu) * lax.rsqrt(var + GN_EPS)).reshape(B, L, H * dv)
    return (yn * w.astype(jnp.float32)).astype(y.dtype)

def _mla_attention(q_nope, q_rope, k_nope, k_rope, v):
    B, L, H, _ = q_nope.shape
    Lp = L + META_PAD
    nb = Lp // CHUNK
    scale = MLA_QK ** -0.5

    def to_blocks(t):
        t = jnp.pad(t, ((0, 0), (META_PAD, 0), (0, 0), (0, 0)))
        return t.reshape(B, nb, CHUNK, H, t.shape[-1]).swapaxes(0, 1)

    def attend(qb):
        qn, qr = qb
        s = jnp.einsum('bqhd,bkhd->bhqk', qn, k_nope) + jnp.einsum('bqhr,bkr->bhqk', qr, k_rope)
        p = jax.nn.softmax(s.astype(jnp.float32) * scale, axis=-1).astype(v.dtype)
        return jnp.einsum('bhqk,bkhd->bqhd', p, v)

    out = lax.map(attend, (to_blocks(q_nope), to_blocks(q_rope)))
    return out.swapaxes(0, 1).reshape(B, Lp, H, MLA_DV)[:, META_PAD:]

def _mixer(u, w_in, decay_f, decay_b, gn_w, w_ret_out, q_norm_w, w_uq, kv_norm_w, w_uk, w_uv,
           w_mla_out, w_o, ret_cos, ret_sin, mla_cos, mla_sin):
    B, L, _ = u.shape
    proj = u @ w_in
    rq, rk, rv, rg, a_cq, a_ckv, a_kr, a_gret, a_gmla = jnp.split(proj, SPLIT_IDX, axis=-1)

    rq = _apply_rope(rq.reshape(B, L, RET_HEADS, RET_DK), ret_cos[:, None, :], ret_sin[:, None, :])
    rk = _apply_rope(rk.reshape(B, L, RET_HEADS, RET_DK), ret_cos[:, None, :], ret_sin[:, None, :]) * (RET_DK ** -0.5)
    rv = rv.reshape(B, L, RET_HEADS, RET_DV)
    y_ret = _head_group_norm(_bidir_retention(rq, rk, rv, decay_f, decay_b), gn_w)
    y_ret = (jax.nn.silu(rg) * y_ret) @ w_ret_out

    c_q = _rmsnorm(a_cq, q_norm_w)
    q = (c_q @ w_uq).reshape(B, L, MLA_HEADS, MLA_QK)
    q_nope = q[..., :MLA_NOPE]
    q_rope = _apply_rope(q[..., MLA_NOPE:], mla_cos[:, None, :], mla_sin[:, None, :])
    c_kv = _rmsnorm(a_ckv, kv_norm_w)
    k_nope = (c_kv @ w_uk).reshape(B, L, MLA_HEADS, MLA_NOPE)
    v = (c_kv @ w_uv).reshape(B, L, MLA_HEADS, MLA_DV)
    k_rope = _apply_rope(a_kr, mla_cos, mla_sin)
    y_mla = _mla_attention(q_nope, q_rope, k_nope, k_rope, v).reshape(B, L, MLA_HEADS * MLA_DV) @ w_mla_out

    merged = jax.nn.sigmoid(a_gret) * y_ret + jax.nn.sigmoid(a_gmla) * y_mla
    return merged @ w_o

def _swiglu(u, w_gate, w_up, w_down):
    return (jax.nn.silu(u @ w_gate) * (u @ w_up)) @ w_down

def first_inputs(seed: int = 0) -> dict:
    key = jax.random.key(seed)
    ks = jax.random.split(key, 24)
    f32 = jnp.float32

    def nrm(k, shape, fan_in):
        return jax.random.normal(k, shape, f32) * (fan_in ** -0.5)

    def gain(k, shape):
        return 1.0 + 0.02 * jax.random.normal(k, shape, f32)

    h_idx = jnp.arange(RET_HEADS, dtype=f32)
    gamma = 1.0 - 2.0 ** (-5.0 - h_idx)
    decay_base = jnp.log(-jnp.log(gamma))
    return {
        'x': jax.random.normal(ks[0], (BATCH, SEQ, D_MODEL), f32),
        'meta_tokens': jax.random.normal(ks[1], (N_META, D_MODEL), f32),
        'norm_mix_w': gain(ks[2], (DEPTH, D_MODEL)),
        'w_in': nrm(ks[3], (DEPTH, D_MODEL, D_IN), D_MODEL),
        'ret_decay_fwd': decay_base[None] + 0.05 * jax.random.normal(ks[4], (DEPTH, RET_HEADS), f32),
        'ret_decay_bwd': decay_base[None] + 0.05 * jax.random.normal(ks[5], (DEPTH, RET_HEADS), f32),
        'ret_gn_w': gain(ks[6], (DEPTH, RET_V_W)),
        'w_ret_out': nrm(ks[7], (DEPTH, RET_V_W, D_MODEL), RET_V_W),
        'mla_q_norm_w': gain(ks[8], (DEPTH, MLA_Q_RANK)),
        'w_uq': nrm(ks[9], (DEPTH, MLA_Q_RANK, MLA_HEADS * MLA_QK), MLA_Q_RANK),
        'mla_kv_norm_w': gain(ks[10], (DEPTH, MLA_KV_RANK)),
        'w_uk': nrm(ks[11], (DEPTH, MLA_KV_RANK, MLA_HEADS * MLA_NOPE), MLA_KV_RANK),
        'w_uv': nrm(ks[12], (DEPTH, MLA_KV_RANK, MLA_HEADS * MLA_DV), MLA_KV_RANK),
        'w_mla_out': nrm(ks[13], (DEPTH, MLA_HEADS * MLA_DV, D_MODEL), MLA_HEADS * MLA_DV),
        'w_o': nrm(ks[14], (DEPTH, D_MODEL, D_MODEL), D_MODEL),
        'norm_ffn_w': gain(ks[15], (DEPTH, D_MODEL)),
        'w_ffn_gate': nrm(ks[16], (DEPTH, D_MODEL, D_FF), D_MODEL),
        'w_ffn_up': nrm(ks[17], (DEPTH, D_MODEL, D_FF), D_MODEL),
        'w_ffn_down': nrm(ks[18], (DEPTH, D_FF, D_MODEL), D_FF),
        'norm_final_w': gain(ks[19], (D_MODEL,)),
    }

def first_block(x, meta_tokens, norm_mix_w, w_in, ret_decay_fwd, ret_decay_bwd, ret_gn_w, w_ret_out,
              mla_q_norm_w, w_uq, mla_kv_norm_w, w_uk, w_uv, w_mla_out, w_o, norm_ffn_w,
              w_ffn_gate, w_ffn_up, w_ffn_down, norm_final_w):
    B, S, D = x.shape
    L = S + N_META
    meta = jnp.broadcast_to(meta_tokens.astype(x.dtype)[None], (B, N_META, D))
    h = jnp.concatenate([meta, x], axis=1)
    pos = jnp.arange(L)
    ret_cos, ret_sin = _rope_tables(pos, RET_DK)
    mla_cos, mla_sin = _rope_tables(pos, MLA_ROPE)
    for l in range(DEPTH):
        h = h + _mixer(_rmsnorm(h, norm_mix_w[l]), w_in[l], ret_decay_fwd[l], ret_decay_bwd[l], ret_gn_w[l],
                       w_ret_out[l], mla_q_norm_w[l], w_uq[l], mla_kv_norm_w[l], w_uk[l], w_uv[l],
                       w_mla_out[l], w_o[l], ret_cos, ret_sin, mla_cos, mla_sin)
        h = h + _swiglu(_rmsnorm(h, norm_ffn_w[l]), w_ffn_gate[l], w_ffn_up[l], w_ffn_down[l])
    h = _rmsnorm(h, norm_final_w)
    return h[:, N_META:]


DEPTH_2 = 2

N_EVEN = (DEPTH_2 + 1) // 2
N_ODD = DEPTH_2 // 2
MIX_W = D_MODEL
A_WIDTH = MIX_W // 2
A_GROUPS = 8
A_GDIM = A_WIDTH // A_GROUPS
B_WIDTH = MIX_W // 2
B_HEADS = 8
B_HDIM = B_WIDTH // B_HEADS
QBLOCK = 128
C_HEADS = 4
C_V = MIX_W // C_HEADS
C_QK = C_V // 2
C_CHUNK = 128
CONV_W = 4
D_FF_2 = 4 * D_MODEL
EV_IN = 2 * A_WIDTH + 3 * B_WIDTH
OD_IN = 2 * C_HEADS * C_QK + 2 * C_HEADS * C_V + 2 * C_HEADS
EPS = 1e-6


def _rmsnorm_2(x, g):
    xf = x.astype(jnp.float32)
    ms = jnp.mean(xf * xf, axis=-1, keepdims=True)
    return (xf * lax.rsqrt(ms + EPS) * g.astype(jnp.float32)).astype(x.dtype)

def _layernorm(x, g, b):
    xf = x.astype(jnp.float32)
    mu = jnp.mean(xf, axis=-1, keepdims=True)
    var = jnp.mean(jnp.square(xf - mu), axis=-1, keepdims=True)
    y = (xf - mu) * lax.rsqrt(var + EPS) * g.astype(jnp.float32) + b.astype(jnp.float32)
    return y.astype(x.dtype)

def _stick_breaking(q, k, v):
    seq = q.shape[2]
    scale = q.shape[-1] ** -0.5
    outs = []
    for blk in range(seq // QBLOCK):
        t0 = blk * QBLOCK
        t1 = t0 + QBLOCK
        z = jnp.einsum('bhtd,bhsd->bhts', q[:, :, t0:t1], k[:, :, :t1]) * scale
        mask = jnp.arange(t1)[None, :] < jnp.arange(t0, t1)[:, None]
        log1m = jnp.where(mask, -jax.nn.softplus(z), 0.0)
        suffix = lax.cumsum(log1m, axis=3, reverse=True)
        a = jnp.where(mask, jnp.exp(z + suffix), 0.0)
        outs.append(jnp.einsum('bhts,bhsd->bhtd', a, v[:, :, :t1]))
    return jnp.concatenate(outs, axis=2)

def _even_mixer(h, w_in, w_out, ln_g, ln_b, sg_w, sg_b, qn_g, kn_g):
    bsz, seq, _ = h.shape
    nc = seq // CHUNK
    p = h @ w_in
    za = jax.nn.gelu(p[..., :2 * A_WIDTH])
    zb = p[..., 2 * A_WIDTH:]
    u = za[..., :A_WIDTH].reshape(bsz, nc, CHUNK, A_GROUPS, A_GDIM)
    vg = _layernorm(za[..., A_WIDTH:], ln_g, ln_b).reshape(bsz, nc, CHUNK, A_GROUPS, A_GDIM)
    w_causal = sg_w * jnp.tril(jnp.ones((CHUNK, CHUNK), sg_w.dtype))
    mixed = jnp.einsum('gts,bnsgc->bntgc', w_causal, vg) + sg_b.T[:, :, None]
    y_a = (u * mixed).reshape(bsz, seq, A_WIDTH)
    q = _rmsnorm_2(zb[..., :B_WIDTH].reshape(bsz, seq, B_HEADS, B_HDIM), qn_g)
    k = _rmsnorm_2(zb[..., B_WIDTH:2 * B_WIDTH].reshape(bsz, seq, B_HEADS, B_HDIM), kn_g)
    v = zb[..., 2 * B_WIDTH:].reshape(bsz, seq, B_HEADS, B_HDIM)
    to_bhsd = lambda t: t.astype(jnp.float32).transpose(0, 2, 1, 3)
    o = _stick_breaking(to_bhsd(q), to_bhsd(k), to_bhsd(v))
    y_b = o.transpose(0, 2, 1, 3).reshape(bsz, seq, B_WIDTH).astype(h.dtype)
    return jnp.concatenate([y_a, y_b], axis=-1) @ w_out

def _causal_conv(x, w, b):
    ch = x.shape[-1]
    y = lax.conv_general_dilated(x, w[:, None, :], window_strides=(1,),
                                 padding=[(CONV_W - 1, 0)],
                                 dimension_numbers=('NWC', 'WIO', 'NWC'),
                                 feature_group_count=ch)
    return y + b

def _mlstm(q, k, v, i_pre, f_pre):
    bsz, seq, nh, dqk = q.shape
    dv = v.shape[-1]
    nc = seq // C_CHUNK
    f32 = jnp.float32
    q = q.astype(f32)
    k = k.astype(f32) * (dqk ** -0.5)
    v = v.astype(f32)
    logf = jax.nn.log_sigmoid(f_pre.astype(f32))
    logi = i_pre.astype(f32)

    def chunk4(a):
        return a.reshape(bsz, nc, C_CHUNK, nh, a.shape[-1]).transpose(1, 0, 3, 2, 4)

    def chunk3(a):
        return a.reshape(bsz, nc, C_CHUNK, nh).transpose(1, 0, 3, 2)

    tril = jnp.tril(jnp.ones((C_CHUNK, C_CHUNK), bool))

    def step(carry, inp):
        c_st, n_st, m_st = carry
        qc, kc, vc, lf, li = inp
        bcum = jnp.cumsum(lf, axis=-1)
        dmat = jnp.where(tril, bcum[..., :, None] - bcum[..., None, :] + li[..., None, :], -jnp.inf)
        g = bcum + m_st[..., None]
        m_t = jnp.maximum(g, jnp.max(dmat, axis=-1))
        wts = jnp.exp(dmat - m_t[..., None])
        inter = jnp.exp(g - m_t)
        s = jnp.einsum('bhtd,bhsd->bhts', qc, kc) * wts
        num = jnp.einsum('bhts,bhsv->bhtv', s, vc) + inter[..., None] * jnp.einsum('bhtd,bhdv->bhtv', qc, c_st)
        den = jnp.sum(s, axis=-1) + inter * jnp.einsum('bhtd,bhd->bht', qc, n_st)
        h = num / jnp.maximum(jnp.abs(den), jnp.exp(-m_t))[..., None]
        b_last = bcum[..., -1]
        wk = b_last[..., None] - bcum + li
        m_new = jnp.maximum(b_last + m_st, jnp.max(wk, axis=-1))
        decay = jnp.exp(b_last + m_st - m_new)
        wkx = jnp.exp(wk - m_new[..., None])
        c_new = decay[..., None, None] * c_st + jnp.einsum('bhs,bhsd,bhsv->bhdv', wkx, kc, vc)
        n_new = decay[..., None] * n_st + jnp.einsum('bhs,bhsd->bhd', wkx, kc)
        return (c_new, n_new, m_new), h

    init = (jnp.zeros((bsz, nh, dqk, dv), f32), jnp.zeros((bsz, nh, dqk), f32), jnp.zeros((bsz, nh), f32))
    _, hs = lax.scan(step, init, (chunk4(q), chunk4(k), chunk4(v), chunk3(logf), chunk3(logi)))
    return hs.transpose(1, 0, 3, 2, 4).reshape(bsz, seq, nh, dv)

def _odd_mixer(h, w_in, conv_w, conv_b, i_b, f_b, on_g, w_out):
    bsz, seq, _ = h.shape
    p = h @ w_in
    n_qk = 2 * C_HEADS * C_QK
    n_v = C_HEADS * C_V
    qk = jax.nn.silu(_causal_conv(p[..., :n_qk], conv_w, conv_b))
    q = qk[..., :C_HEADS * C_QK].reshape(bsz, seq, C_HEADS, C_QK)
    k = qk[..., C_HEADS * C_QK:].reshape(bsz, seq, C_HEADS, C_QK)
    v = p[..., n_qk:n_qk + n_v].reshape(bsz, seq, C_HEADS, C_V)
    og = p[..., n_qk + n_v:n_qk + 2 * n_v].reshape(bsz, seq, C_HEADS, C_V)
    gates = p[..., n_qk + 2 * n_v:]
    i_pre = gates[..., :C_HEADS] + i_b
    f_pre = gates[..., C_HEADS:] + f_b
    hc = _mlstm(q, k, v, i_pre, f_pre)
    hc = _rmsnorm_2(hc, on_g.reshape(C_HEADS, C_V)).astype(h.dtype)
    y = (hc * jax.nn.sigmoid(og)).reshape(bsz, seq, MIX_W)
    return y @ w_out

def _sqrelu_mlp(h, w1, w2):
    return jnp.square(jax.nn.relu(h @ w1)) @ w2

def second_inputs(seed: int = 0) -> dict:
    key = jax.random.key(seed)
    ks = jax.random.split(key, 24)
    nrm = lambda k, shape, s: jax.random.normal(k, shape, jnp.float32) * s
    gain = lambda k, shape: 1.0 + 0.05 * jax.random.normal(k, shape, jnp.float32)
    f_base = jnp.linspace(3.0, 6.0, C_HEADS, dtype=jnp.float32)
    return {
        'x': nrm(ks[0], (BATCH, SEQ, D_MODEL), 1.0),
        'mix_norm_g': gain(ks[1], (DEPTH_2, D_MODEL)),
        'mlp_norm_g': gain(ks[2], (DEPTH_2, D_MODEL)),
        'mlp_w1': nrm(ks[3], (DEPTH_2, D_MODEL, D_FF_2), D_MODEL ** -0.5),
        'mlp_w2': nrm(ks[4], (DEPTH_2, D_FF_2, D_MODEL), D_FF_2 ** -0.5),
        'ev_w_in': nrm(ks[5], (N_EVEN, D_MODEL, EV_IN), D_MODEL ** -0.5),
        'ev_w_out': nrm(ks[6], (N_EVEN, MIX_W, D_MODEL), MIX_W ** -0.5),
        'sg_ln_g': gain(ks[7], (N_EVEN, A_WIDTH)),
        'sg_ln_b': nrm(ks[8], (N_EVEN, A_WIDTH), 0.02),
        'sg_w': nrm(ks[9], (N_EVEN, A_GROUPS, CHUNK, CHUNK), CHUNK ** -0.5),
        'sg_b': 1.0 + nrm(ks[10], (N_EVEN, A_GROUPS, CHUNK), 0.1),
        'sb_q_norm_g': gain(ks[11], (N_EVEN, B_HDIM)),
        'sb_k_norm_g': gain(ks[12], (N_EVEN, B_HDIM)),
        'od_w_in': nrm(ks[13], (N_ODD, D_MODEL, OD_IN), D_MODEL ** -0.5),
        'od_conv_w': nrm(ks[14], (N_ODD, CONV_W, 2 * C_HEADS * C_QK), CONV_W ** -0.5),
        'od_conv_b': nrm(ks[15], (N_ODD, 2 * C_HEADS * C_QK), 0.02),
        'od_i_b': nrm(ks[16], (N_ODD, C_HEADS), 0.1),
        'od_f_b': f_base[None, :] + nrm(ks[17], (N_ODD, C_HEADS), 0.1),
        'od_out_norm_g': gain(ks[18], (N_ODD, MIX_W)),
        'od_w_out': nrm(ks[19], (N_ODD, MIX_W, D_MODEL), MIX_W ** -0.5),
    }

def second_block(x, mix_norm_g, mlp_norm_g, mlp_w1, mlp_w2, ev_w_in, ev_w_out,
              sg_ln_g, sg_ln_b, sg_w, sg_b, sb_q_norm_g, sb_k_norm_g,
              od_w_in, od_conv_w, od_conv_b, od_i_b, od_f_b, od_out_norm_g, od_w_out):
    for layer in range(DEPTH_2):
        h = _rmsnorm_2(x, mix_norm_g[layer])
        j = layer // 2
        if layer % 2 == 0:
            x = x + _even_mixer(h, ev_w_in[j], ev_w_out[j], sg_ln_g[j], sg_ln_b[j],
                                sg_w[j], sg_b[j], sb_q_norm_g[j], sb_k_norm_g[j])
        else:
            x = x + _odd_mixer(h, od_w_in[j], od_conv_w[j], od_conv_b[j], od_i_b[j],
                               od_f_b[j], od_out_norm_g[j], od_w_out[j])
        h = _rmsnorm_2(x, mlp_norm_g[layer])
        x = x + _sqrelu_mlp(h, mlp_w1[layer], mlp_w2[layer])
    return x


def setup_inputs(seed=0):
    out = dict(first_inputs(seed))
    for name, value in second_inputs(seed + 1).items():
        if name != "x":
            out[name + "_2"] = value
    return out


def reference(
    x, meta_tokens, norm_mix_w, w_in, ret_decay_fwd, ret_decay_bwd, ret_gn_w, w_ret_out,
    mla_q_norm_w, w_uq, mla_kv_norm_w, w_uk, w_uv, w_mla_out, w_o, norm_ffn_w, w_ffn_gate,
    w_ffn_up, w_ffn_down, norm_final_w, mix_norm_g_2, mlp_norm_g_2, mlp_w1_2, mlp_w2_2,
    ev_w_in_2, ev_w_out_2, sg_ln_g_2, sg_ln_b_2, sg_w_2, sg_b_2, sb_q_norm_g_2, sb_k_norm_g_2,
    od_w_in_2, od_conv_w_2, od_conv_b_2, od_i_b_2, od_f_b_2, od_out_norm_g_2, od_w_out_2,
):
    x = first_block(
        x, meta_tokens, norm_mix_w, w_in, ret_decay_fwd, ret_decay_bwd, ret_gn_w, w_ret_out,
        mla_q_norm_w, w_uq, mla_kv_norm_w, w_uk, w_uv, w_mla_out, w_o, norm_ffn_w, w_ffn_gate,
        w_ffn_up, w_ffn_down, norm_final_w,
    )
    return second_block(
        x, mix_norm_g_2, mlp_norm_g_2, mlp_w1_2, mlp_w2_2, ev_w_in_2, ev_w_out_2, sg_ln_g_2,
        sg_ln_b_2, sg_w_2, sg_b_2, sb_q_norm_g_2, sb_k_norm_g_2, od_w_in_2, od_conv_w_2,
        od_conv_b_2, od_i_b_2, od_f_b_2, od_out_norm_g_2, od_w_out_2,
    )


_drawn_inputs = setup_inputs


def setup_inputs(seed=0):
    import zlib

    import numpy as np

    out = dict(_drawn_inputs(seed))
    spreads = {}
    factors = {'norm_mix_w': 2.985,
     'ret_gn_w': 6.405,
     'mla_q_norm_w': 8.0,
     'mla_kv_norm_w': 8.0,
     'norm_ffn_w': 3.245,
     'sg_ln_g_2': 3.972,
     'sg_ln_b_2': 8.0,
     'sb_q_norm_g_2': 5.48,
     'sb_k_norm_g_2': 5.459,
     'od_conv_b_2': 8.0,
     'od_i_b_2': 64.0,
     'od_out_norm_g_2': 3.643}
    for name, (base, spread) in spreads.items():
        noise = np.random.default_rng([zlib.crc32(name.encode()), seed]).standard_normal(out[name].shape)
        drawn = base * np.exp(spread * noise) if base else spread * noise
        out[name] = jnp.asarray(drawn.astype(out[name].dtype))
    for name, factor in factors.items():
        out[name] = (out[name] * factor).astype(out[name].dtype)
    return out
```

```python
from contextlib import ExitStack

import concourse.bass as bass
from concourse import mybir

F32 = mybir.dt.float32
F32R = mybir.dt.float32r
ALU = mybir.AluOpType
ACT = mybir.ActivationFunctionType
AX_X = mybir.AxisListType.X

P = 128
D = 1024
KT = D // P
S = 256
META = 16
L = S + META
HEADS = 8
D_FF, D_MLP = 2816, 4096
W_CHUNK = 2048
RING = 4
AHEAD = 2
EPS, GN_EPS = 1e-6, 1e-5
KEY_BLOCKS = [(0, 128), (128, 128), (256, 16)]

CONST_COLS = {}
_at = 0
for _name, _w in (("ident", 128), ("ones", 128), ("ones_half", 128), ("neg_tri", 128), ("neg_ones", 128),
                  ("rot_ret", 128), ("rot_mla", 96), ("cos_ret", L), ("sin_ret", L), ("cos_mla", L),
                  ("sin_mla", L), ("rel", 3 * S)):
    CONST_COLS[_name] = (_at, _w)
    _at += _w
N_CONST = _at
LATE_COLS = {}
_at = 0
for _name, _w in (("mask_strict", 384), ("mask_causal", 384), ("pick_head", 512)):
    LATE_COLS[_name] = (_at, _w)
    _at += _w
N_LATE = _at

PAR_COLS = {}
_at = 0
for _name, _w in (("norm_mix", 8), ("gn", 8), ("q_norm", 3), ("kv_norm", 2), ("ffn", 8), ("final", 8),
                  ("mix2", 16), ("mlp2", 16), ("conv_w", 32), ("conv_b", 8), ("on", 8), ("sb_q", 1),
                  ("sb_k", 1), ("sg_b", 8), ("decay_f", 8), ("decay_b", 8), ("i_b", 4), ("f_b", 4)):
    PAR_COLS[_name] = (_at, _w)
    _at += _w
N_PAR = _at

REGION = {"f1": 3200, "f2": 2176, "f3": 2112, "f4": 2112, "f5": 2048, "f6": 2304}


class Lane:

    def __init__(self, engine, sems, step):
        self.engine, self.sems, self.step = engine, sems, step
        self.base, self.here, self.i, self.per = {}, {}, None, {}

    def value(self, name):
        v = self.base.get(name, 0) + self.here.get(name, 0)
        return v if self.i is None or not self.per.get(name) else self.i * self.per[name] + v

    def post(self, ins, name):
        ins.then_inc(self.sems[name], 1)
        self.here[name] = self.here.get(name, 0) + 1
        self.engine.wait_ge(self.sems[name], self.value(name))

    def run(self, ins):
        self.post(ins, self.step)

    def enter(self, i, per):
        self.flush()
        self.i, self.per = i, per

    def leave(self, turns):
        assert self.here == {k: v for k, v in self.per.items() if v}, (self.here, self.per)
        for k, v in self.per.items():
            self.base[k] = self.base.get(k, 0) + v * turns
        self.here, self.i, self.per = {}, None, {}

    def flush(self):
        for k, v in self.here.items():
            self.base[k] = self.base.get(k, 0) + v
        self.here = {}


class Sems(dict):
    def __init__(self, make):
        super().__init__()
        self.make = make

    def __missing__(self, name):
        self[name] = self.make(name)
        return self[name]


def at(f, n, i):
    return f(n) if i is None else i * (f(n + RING) - f(n)) + f(n)


def plan_chunks(w):
    chunks, index = [], {}

    def add(name, *parts):
        index[name] = len(chunks)
        chunks.append(parts)

    def cols(ap, c0, width, kt=KT):
        v = ap.rearrange("(k p) n -> p k n", p=P)
        return (lambda m: v[:, :, c0:c0 + width]), kt, width

    def stripe(name, ap, c0, n, width=256, kt=KT):
        for j in range(n):
            add(f"{name}{j}", cols(ap, c0 + j * width, width, kt))

    w_in = w["w_in"][0]
    stripe("rq", w_in, 0, 2)
    stripe("rk", w_in, 512, 2)
    stripe("rv", w_in, 1024, 4)
    add("c0", cols(w_in, 3072, 256))
    add("c1", cols(w_in, 3328, 256))
    add("c2", cols(w_in, 3584, 160))
    stripe("rg", w_in, 2048, 4)
    stripe("gm", w_in, 4768, 4)
    stripe("uq", w["w_uq"][0], 0, 2, 384, 3)
    add("ukv", cols(w["w_uk"][0], 0, 512, 2), cols(w["w_uv"][0], 0, 512, 2))
    stripe("ro", w["w_ret_out"][0], 0, 4)
    stripe("gr", w_in, 3744, 4)
    stripe("mo", w["w_mla_out"][0], 0, 2, 512, 4)
    stripe("wo", w["w_o"][0], 0, 4)

    def hidden_stream(tag, n, up, down):
        for k in range(n):
            add(f"{tag}A{k}", *up(k))
            if k >= 1:
                add(f"{tag}B{k - 1}", *down(k - 1))
        add(f"{tag}B{n - 1}", *down(n - 1))

    def up_cols(ap, width):
        v = ap.rearrange("(k p) n -> p k n", p=P)
        return lambda k: ((lambda c: v[:, :, bass.ds(c * width, width)]), KT, width, k)

    def down_rows(ap, kt):
        v = ap.rearrange("(b k p) n -> b p k n", p=P, k=kt)
        return lambda k: ((lambda c: v[bass.ds(c, 1)].rearrange("b p k n -> (b p) k n")), kt, D, k)

    gate, upp = up_cols(w["w_ffn_gate"][0], 128), up_cols(w["w_ffn_up"][0], 128)
    half = w["w_ffn_down"][0]
    ffn_down = down_rows(half, 1)
    hidden_stream("ffn", D_FF // P, lambda k: (gate(k), upp(k)), lambda k: (ffn_down(k),))

    ev = w["ev_w_in_2"][0]
    stripe("sq", ev, 1024, 2)
    stripe("sk", ev, 1536, 2)
    stripe("sv", ev, 2048, 2)
    stripe("za", ev, 0, 4)
    stripe("eo", w["ev_w_out_2"][0], 0, 4)
    m1, m2 = up_cols(w["mlp_w1_2"][0], 256), down_rows(w["mlp_w2_2"][0], 2)
    hidden_stream("m0", D_MLP // 256, lambda k: (m1(k),), lambda k: (m2(k),))
    od = w["od_w_in_2"][0]
    add("gates", cols(od, 3072, 8))
    stripe("qk", od, 0, 4)
    stripe("ov", od, 1024, 4)
    stripe("og", od, 2048, 4)
    stripe("oo", w["od_w_out_2"][0], 0, 4)
    n1, n2 = up_cols(w["mlp_w1_2"][1], 256), down_rows(w["mlp_w2_2"][1], 2)
    hidden_stream("m1", D_MLP // 256, lambda k: (n1(k),), lambda k: (n2(k),))
    return chunks, index


def build(nc, w, params, consts, late, ln_gb, out):
    chunks, index = plan_chunks(w)
    landed, total = [], [0] * RING
    for n, parts in enumerate(chunks):
        total[n % RING] += 16 * len(parts)
        landed.append(total[n % RING])

    def width_of(n):
        return sum(p[1] * p[2] for p in chunks[n])

    with ExitStack() as ctx:
        def sb(name, shape, dt=F32):
            return ctx.enter_context(nc.sbuf_tensor(name, shape, dt))

        sems = Sems(lambda name: ctx.enter_context(nc.semaphore(name)))

        raw = sb("raw", [P, RING, W_CHUNK])
        whi = sb("whi", [P, RING, W_CHUNK], F32R)
        wlo = sb("wlo", [P, RING, W_CHUNK], F32R)
        x_all = sb("x_all", [P, KT, L])
        x2 = x_all[:, :, META:L]
        u = sb("u", [P, 2, KT, L], F32R)
        v = sb("v", [P, 2, KT, S], F32R)
        cst = sb("cst", [P, N_CONST])
        par = sb("par", [P, N_PAR])
        r_all = sb("r_all", [P, 3, L])
        kr = sb("kr", [P, L])
        small = sb("small", [P, 64])
        reg = {k: sb(k, [P, n]) for k, n in REGION.items()}
        proj = ctx.enter_context(nc.psum_tensor("proj", [P, 4, 512], F32))
        aux = ctx.enter_context(nc.psum_tensor("aux", [P, 4, 512], F32))

        def C(name):
            a, n = CONST_COLS[name]
            return cst[:, a:a + n]

        def V(name, j=0):
            a, _ = PAR_COLS[name]
            return par[:, a + j:a + j + 1]

        late_at = CONST_COLS["rot_ret"][0]

        def LC(name):
            a, n = LATE_COLS[name]
            return cst[:, late_at + a:late_at + a + n]

        def f(name, a, *dims):
            n = 1
            for d in dims:
                n *= d
            ap = reg[name][:, a:a + n]
            if len(dims) == 1:
                return ap
            if len(dims) == 2:
                return ap.rearrange("p (a b) -> p a b", a=dims[0])
            return ap.rearrange("p (a b c) -> p a b c", a=dims[0], b=dims[1])

        def W(part, n, off, kt, cols):
            t = (whi, wlo)[part]
            return t[:, n % RING, off:off + kt * cols].rearrange("p (k n) -> p k n", k=kt)

        def bc(ap, n):
            return ap[:, None, :].to_broadcast([ap.shape[0], n, ap.shape[1]])

        eps, gn_eps, one = small[:, 0:1], small[:, 1:2], small[:, 2:3]
        lgf, lgb = small[:, 4:12], small[:, 12:20]
        mx, nb, sums, rs = small[:, 20:22], small[:, 22:24], small[:, 24:26], small[:, 26:28]
        r_tok = small[:, 28:30]
        qg8 = small[:, 30:31]
        gat = small[:, 32:48]
        stat = small[:, 48:54]

        x_tok = f("f1", 0, 3, D)
        sq = f("f2", 0, KT, L)
        preq, prek = f("f4", 0, 4, S), f("f4", 4 * S, 4, L)
        q_ret, k_ret = f("f3", 0, 4, S), f("f3", 4 * S, 4, L)
        rv_feat = f("f2", 0, 8, L)
        rv_tok = f("f1", 0, 3, D)
        low = f("f6", 0, 3 * S + 2 * L + L)
        acq, ackv, akr = f("f6", 0, 3, S), f("f6", 3 * S, 2, L), f("f6", 3 * S + 2 * L, L)
        low_sq = f("f5", 0, 3 * S + 2 * L)
        dec = f("f6", 0, 3, S)
        sd = f("f6", 3 * S, 2, 3, S)
        o_ret = f("f2", 0, 8, S)
        d_sq = f("f1", 0, 8, S)
        rg = f("f4", 0, 8, S)
        th_m = f("f5", 0, 8, S)
        q_all, q_pre = f("f1", 0, 8, S), f("f3", 0, 8, S)
        k_all = f("f2", 0, 8, L)
        v_feat = f("f6", 0, 4, L)
        v_tok = f("f4", 0, 3, 512)
        prob = f("f1", 2048, 2, 2, L)
        pt = f("f6", 0, 3, S)
        yr = f("f3", 0, 8, S)

        def o_mla(a):
            return f("f6", 768 + a * S, S) if a < 3 else f("f6", 1536, S)

        block = ctx.enter_context(nc.Block())

        FFN = dict(tag="ffn", n=D_FF // P, kt=1, k0=0)
        M0 = dict(tag="m0", n=D_MLP // 256, kt=2, k0=D_FF // P)
        M1 = dict(tag="m1", n=D_MLP // 256, kt=2, k0=D_FF // P + D_MLP // 256)
        loop_first = {d["tag"]: index[d["tag"] + "A0"] for d in (FFN, M0, M1)}
        in_loop = set()
        for d in (FFN, M0, M1):
            in_loop |= set(range(loop_first[d["tag"]], loop_first[d["tag"]] + 2 * d["n"]))
        order = {n: j for j, n in enumerate(m for m in range(len(chunks)) if m not in in_loop)}

        def ckv_split(a, k):
            flat = v[:, a, 3:8, :].rearrange("p k t -> p (k t)")
            return flat[:, k * L:(k + 1) * L]

        @block.sync
        def _(sp):
            def load(n, i=None):
                if n >= RING:
                    sp.wait_ge(sems["lo_ready"], at(lambda m: m - RING + 1, n, i))
                off = 0
                for part in chunks[n]:
                    src, kt, width = part[:3]
                    c = None if len(part) < 4 else (part[3] if i is None else i * 2 + part[3])
                    dst = raw[:, n % RING, off:off + kt * width].rearrange("p (k n) -> p k n", k=kt)
                    sp.dma_start(dst, src(c)).then_inc(sems[f"raw_landed{n % RING}"], 16)
                    off += kt * width

            x, meta = w["x"][0], w["meta_tokens"]
            sp.dma_start(cst[:, :], consts).then_inc(sems["const_in"], 16)
            sp.dma_start(x_tok[0:META, 0, :], meta).then_inc(sems["x_in"], 16)
            sp.dma_start(x_tok[META:P, 0, :], x[0:P - META, :]).then_inc(sems["x_in"], 16)
            sp.dma_start(x_tok[:, 1, :], x[P - META:2 * P - META, :]).then_inc(sems["x_in"], 16)
            sp.dma_start(x_tok[0:META, 2, :], x[S - META:S, :]).then_inc(sems["x_in"], 16)
            sp.dma_start(par[:, :], params).then_inc(sems["par_in"], 16)

            def stream(d):
                g = loop_first[d["tag"]]
                for n in range(g, g + 3):
                    load(n)
                turns = (d["n"] - 2) // 2
                with sp.Fori(0, turns) as i:
                    for j in range(4):
                        load(g + 3 + j, i)
                load(g + 2 * d["n"] - 1)

            n = 0
            for d, tag in ((FFN, "ffn"), (M0, "m0"), (M1, "m1")):
                while n < loop_first[tag]:
                    load(n)
                    n += 1
                if tag == "ffn":
                    sp.wait_ge(sems["q_mla_roped"], 1)
                    sp.dma_start(cst[:, late_at:late_at + N_LATE], late).then_inc(sems["late_in"], 16)
                stream(d)
                n += 2 * d["n"]
                if tag == "ffn":
                    sp.wait_ge(sems["merged"], 1)
                    sp.dma_start(f("f6", 0, 8, P), w["sg_w_2"][0].rearrange("g t s -> t g s")).then_inc(sems["sg_in"], 16)
                    sp.dma_start(f("f6", 1024, 2, 512), ln_gb).then_inc(sems["sg_in"], 16)
            for h in range(2):
                sp.wait_ge(sems["out_ready"], h + 1)
                sp.dma_start(out[0].rearrange("(b p) n -> p b n", p=P)[:, h, :], f("f1", h * D, D)).then_inc(sems["stored"], 16)
            sp.wait_ge(sems["stored"], 32)

        @block.tensor
        def _(pe):
            mm = nc.tensor.matmul

            def split_mm(o, w_of, x_of, kt, first=True, last=True, skip=False):
                ins = None
                for k in range(kt):
                    for j, (a, b) in enumerate(((0, 0), (0, 1), (1, 0))):
                        ins = mm(o, w_of(a, k), x_of(b, k), start=first and k == 0 and j == 0,
                                 stop=last and k == kt - 1 and j == 2, skip_group_check=skip)
                return ins

            def read_out(name):
                pe.wait_ge(sems["proj_free"], order[index[name]] + 1)

            def begin(n):
                pe.wait_ge(sems["lo_ready"], n + 1)
                m = order[n]
                if m >= 2:
                    pe.wait_ge(sems["proj_free"], m - 1)
                return m, 2 * (m % 2)

            def finish(ins):
                ins.then_inc(sems["chunk_used"], 1)

            def project(name, blocks=2, src=u, t0=0, t=L, kt=KT, width=256, m=P, step=P, off=0):
                n = index[name]
                _, b = begin(n)
                for j in range(blocks):
                    ins = split_mm(proj[0:m, b + j, 0:t],
                                   lambda a, k: W(a, n, off, kt, width)[:, k, j * step:j * step + m],
                                   lambda a, k: src[:, a, k, t0:t0 + t], kt)
                finish(ins)

            def project_tokens(name, width=256):
                n = index[name]
                _, b = begin(n)
                for j in range(2):
                    ins = split_mm(proj[:, b + j, 0:width],
                                   lambda a, k: u[:, a, k, META + j * P:META + (j + 1) * P],
                                   lambda a, k: W(a, n, 0, KT, width)[:, k, :], KT)
                finish(ins)

            def sum_squares(tokens, name, per_token=False):
                for k in range(KT):
                    ins = mm(aux[:, 0, 0:tokens], C("ones"), sq_of(tokens)[:, k, :], start=k == 0, stop=k == KT - 1)
                if per_token:
                    for b in range(2):
                        for k in range(KT):
                            ins = mm(aux[:, 1, b:b + 1], sq_of(tokens)[:, k, b * P:(b + 1) * P], C("ones")[:, 0:1],
                                     start=k == 0, stop=k == KT - 1)
                ins.then_inc(sems[name], 1)

            def sq_of(tokens):
                return sq if tokens == L else f("f2", 0, KT, S)

            pe.wait_ge(sems["const_in"], 16)
            pe.wait_ge(sems["x_in"], 64)
            for k in range(KT):
                bank = (proj if k < 4 else aux)[:, k % 4, :]
                for b, (t, m) in enumerate(KEY_BLOCKS):
                    ins = nc.tensor.transpose(bank[:, t:t + m], x_tok[0:m, b, k * P:(k + 1) * P], C("ident")[0:m, 0:m])
                ins.then_inc(sems["x_turned"], 1)
            pe.wait_ge(sems["x_ready"], KT)

            pe.wait_ge(sems["u_ready"], 1)
            project("rq0", t0=META, t=S)
            pe.wait_ge(sems["sq_ready"], 1)
            sum_squares(L, "sumsq")
            project("rq1", t0=META, t=S)
            project("rk0")
            read_out("rq1")
            pe.wait_ge(sems["rms_ready"], 1)
            for j in range(2):
                ins = mm(aux[:, j, :], C("rot_ret"), preq[:, 2 * j:2 * j + 2, :], start=True, stop=True)
            ins.then_inc(sems["q_rotated"], 1)
            project("rk1")
            project("rv0")
            read_out("rk1")
            pe.wait_ge(sems["q_roped"], 1)
            for j in range(4):
                ins = mm(aux[:, j, 0:L], C("rot_ret"), prek[:, j, :], start=True, stop=True)
            ins.then_inc(sems["k_rotated"], 1)
            for j in range(1, 4):
                project(f"rv{j}")
            pe.wait_ge(sems["k_roped"], 1)
            project("c0", t0=META, t=S)
            for b, (t, m) in enumerate(KEY_BLOCKS):
                for hh in range(2):
                    j = 2 * b + hh
                    if j == 0:
                        read_out("rv3")
                    if j >= 4:
                        pe.wait_ge(sems["rv_tok_ready"], j - 3)
                    for q in range(4):
                        ins = nc.tensor.transpose(aux[0:m, j % 4, q * P:(q + 1) * P], rv_feat[:, 4 * hh + q, t:t + m], C("ident"))
                    ins.then_inc(sems["rv_turned"], 1)
            n = index["c1"]
            _, b = begin(n)
            split_mm(proj[:, b, 0:S], lambda a, k: W(a, n, 0, KT, 256)[:, k, 0:P], lambda a, k: u[:, a, k, META:L], KT)
            finish(split_mm(proj[:, b + 1, 0:L], lambda a, k: W(a, n, 0, KT, 256)[:, k, P:2 * P], lambda a, k: u[:, a, k, :], KT))
            n2 = index["c2"]
            _, b = begin(n2)
            split_mm(proj[:, b, 0:L], lambda a, k: W(a, n2, 0, KT, 160)[:, k, 0:P], lambda a, k: u[:, a, k, :], KT)
            finish(split_mm(proj[0:96, b + 1, 0:L], lambda a, k: W(a, n2, 0, KT, 160)[:, k, 64:160], lambda a, k: u[:, a, k, :], KT))

            def ret_scores(h):
                b, p0 = 2 * (h % 2), 64 * (h % 2)
                if h >= 2:
                    pe.wait_ge(sems["o_ready"], h - 1)
                for j, (t, m) in enumerate(KEY_BLOCKS):
                    o = aux[:, b, j * S:(j + 1) * S] if j < 2 else aux[0:m, b + 1, 0:S]
                    ins = mm(o, k_ret[p0:p0 + 64, h // 2, t:t + m], q_ret[p0:p0 + 64, h // 2, :], start=True, stop=True)
                ins.then_inc(sems["ret_scores"], 1)

            def ret_values(h):
                pe.wait_ge(sems["sd_ready"], h + 1)
                for j, (t, m) in enumerate(KEY_BLOCKS):
                    ins = mm(aux[:, 2 * (h % 2) + 1, S:2 * S], rv_tok[0:m, j, h * P:(h + 1) * P], sd[0:m, h % 2, j, :],
                             start=j == 0, stop=j == 2)
                ins.then_inc(sems["ret_out"], 1)

            pe.wait_ge(sems["rv_tok_ready"], 6)
            pe.wait_ge(sems["low_sq_ready"], 1)
            for j in range(3):
                mm(aux[:, 0, 0:S], C("ones"), low_sq[:, j * S:(j + 1) * S], start=j == 0, stop=j == 2)
            for j in range(2):
                ins = mm(aux[:, 1, 0:L], C("ones"), low_sq[:, 3 * S + j * L:3 * S + (j + 1) * L], start=j == 0, stop=j == 1)
            ins.then_inc(sems["low_sumsq"], 1)
            mm(aux[0:96, 2, 0:L], C("rot_mla")[64:96, :], akr[64:96, :], start=True, stop=True).then_inc(sems["kr_rotated"], 1)
            pe.wait_ge(sems["low_done"], 1)
            ret_scores(0)
            for h in range(HEADS):
                project(f"rg{h}" if h < 4 else f"gm{h - 4}", t0=META, t=S)
                if h + 1 < HEADS:
                    ret_scores(h + 1)
                ret_values(h)
            pe.wait_ge(sems["o_ready"], 8)
            for j in range(4):
                ins = mm(aux[:, j, :], C("ones"), o_ret[:, 2 * j:2 * j + 2, :], start=True, stop=True)
            ins.then_inc(sems["gn_sum"], 1)

            def query_chunk(j):
                n = index[f"uq{j}"]
                _, b = begin(n)
                for q in range(4):
                    ins = split_mm(proj[0:96, b + q // 2, (q % 2) * S:(q % 2 + 1) * S],
                                   lambda a, k: W(a, n, 0, 3, 384)[:, k, 96 * q:96 * q + 96],
                                   lambda a, k: v[:, a, k, :], 3)
                finish(ins)

            query_chunk(0)
            query_chunk(1)
            pe.wait_ge(sems["d_sq_ready"], 1)
            for j in range(4):
                ins = mm(aux[:, j, :], C("ones"), d_sq[:, 2 * j:2 * j + 2, :], start=True, stop=True)
            ins.then_inc(sems["gn_var"], 1)
            n = index["ukv"]
            for half in range(4):
                if half == 0:
                    pe.wait_ge(sems["lo_ready"], n + 1)
                    pe.wait_ge(sems["proj_free"], order[n])
                if half >= 2:
                    pe.wait_ge(sems["kv_half"], half - 1)
                b = 2 * (half % 2)
                for j in range(2):
                    c = 2 * (half % 2) + j
                    ins = split_mm(proj[:, b + j, 0:L],
                                   lambda a, k: W(a, n, 1024 * (half // 2), 2, 512)[:, k, c * P:(c + 1) * P],
                                   lambda a, k: ckv_split(a, k), 2)
                if half < 3:
                    ins.then_inc(sems["kv_mm"], 1)
            finish(ins)
            read_out("uq1")
            pe.wait_ge(sems["gn_root"], 1)
            for j in range(4):
                ins = mm(aux[0:96, j, :], C("rot_mla")[0:96, :], q_pre[0:96, 2 * j:2 * j + 2, :], start=True, stop=True)
            ins.then_inc(sems["q_mla_rotated"], 1)
            pe.wait_ge(sems["q_mla_roped"], 1)
            read_out("ukv")
            for b, (t, m) in enumerate(KEY_BLOCKS):
                for q in range(4):
                    ins = nc.tensor.transpose(aux[0:m, b, q * P:(q + 1) * P], v_feat[:, q, t:t + m], C("ident"))
            ins.then_inc(sems["v_turned"], 1)
            pe.wait_ge(sems["v_tok_ready"], 1)

            def mla_scores(h):
                if h:
                    pe.wait_ge(sems["mla_exp"], h)
                for b in range(2):
                    ins = mm(aux[:, b, 0:L], q_all[0:96, h, b * P:(b + 1) * P], k_all[0:96, h, :], start=True, stop=True)
                ins.then_inc(sems["mla_scores"], 1)

            def mla_turn(h):
                pe.wait_ge(sems["prob_ready"], h + 1)
                if h:
                    pe.wait_ge(sems["o_mla_ready"], h)
                for j, (t, m) in enumerate(KEY_BLOCKS):
                    for b in range(2):
                        o = aux[:, 2, j * S + b * P:j * S + (b + 1) * P] if j < 2 else aux[0:m, 3, b * P:(b + 1) * P]
                        ins = nc.tensor.transpose(o, prob[:, h % 2, b, t:t + m], C("ident"))
                ins.then_inc(sems["prob_turned"], 1)

            def mla_values(h):
                pe.wait_ge(sems["pt_ready"], h + 1)
                p0 = 64 * (h % 2)
                for j, (t, m) in enumerate(KEY_BLOCKS):
                    ins = mm(aux[p0:p0 + 64, 3, S:2 * S], v_tok[0:m, j, 64 * h:64 * h + 64], pt[0:m, j, :],
                             start=j == 0, stop=j == 2)
                ins.then_inc(sems["mla_out"], 1)

            mla_scores(0)
            for h in range(HEADS):
                mla_turn(h)
                if h + 1 < HEADS:
                    mla_scores(h + 1)
                if h < 4:
                    if h == 0:
                        pe.wait_ge(sems["y_ret_ready"], 1)
                    project(f"ro{h}", src=v, t=S)
                else:
                    project(f"gr{h - 4}", t0=META, t=S)
                mla_values(h)
            pe.wait_ge(sems["y_mla_ready"], 1)
            for c in range(2):
                n = index[f"mo{c}"]
                _, b = begin(n)
                for j in range(4):
                    ins = split_mm(proj[:, b + j // 2, (j % 2) * S:(j % 2 + 1) * S],
                                   lambda a, k: W(a, n, 0, 4, 512)[:, k, j * P:(j + 1) * P],
                                   lambda a, k: v[:, a, k, :], 4)
                finish(ins)
            pe.wait_ge(sems["merged_ready"], 1)
            for c in range(4):
                project(f"wo{c}", t0=META, t=S)

            def hidden_layer(d, norm, split_no):
                tag, n_h, kt, k0 = d["tag"], d["n"], d["kt"], d["k0"]
                g = loop_first[tag]
                pe.wait_ge(sems["u_ready"], split_no)
                pe.wait_ge(sems["proj_free"], order[g - 1] + 1)

                def up(n, k, i=None):
                    pe.wait_ge(sems["lo_ready"], at(lambda m: m + 1, n, i))
                    if k0 + k >= 2:
                        pe.wait_ge(sems["hidden_val"], k0 + k - 1 if i is None else i * 2 + (k0 + k - 1))
                    for j in range(2):
                        if tag == "ffn":
                            ins = split_mm(proj[:, 2 * (k % 2) + j, 0:S], lambda a, q: W(a, n, 1024 * j, KT, P)[:, q, :],
                                           lambda a, q: u[:, a, q, META:L], KT)
                        else:
                            ins = split_mm(proj[:, 2 * (k % 2) + j, 0:S], lambda a, q: W(a, n, 0, KT, 256)[:, q, j * P:(j + 1) * P],
                                           lambda a, q: u[:, a, q, META:L], KT)
                    finish(ins)

                def down(n, k, i=None, first=False, last=False):
                    pe.wait_ge(sems["lo_ready"], at(lambda m: m + 1, n, i))
                    pe.wait_ge(sems["hidden_ready"], k0 + k + 1 if i is None else i * 2 + (k0 + k + 1))
                    for q in range(kt):
                        for j in range(8):
                            ins = None
                            for s, (a, b) in enumerate(((0, 0), (0, 1), (1, 0))):
                                ins = mm(aux[:, j // 2, (j % 2) * S:(j % 2 + 1) * S],
                                         W(a, n, 0, kt, D)[:, q, j * P:(j + 1) * P], v[:, b, 2 * (k % 2) + q, :],
                                         start=first and q == 0 and s == 0 and j % 2 == 0,
                                         stop=last and q == kt - 1 and s == 2, skip_group_check=True)
                    finish(ins)

                up(g, 0)
                up(g + 1, 1)
                pe.wait_ge(sems["rms_ready"], norm + 1)
                down(g + 2, 0, first=True)
                with pe.Fori(0, (n_h - 2) // 2) as i:
                    up(g + 3, 2, i)
                    down(g + 4, 1, i)
                    up(g + 5, 3, i)
                    down(g + 6, 2, i)
                down(g + 2 * n_h - 1, n_h - 1, last=True)

            pe.wait_ge(sems["sq_ready"], 2)
            sum_squares(S, "sumsq")
            hidden_layer(FFN, 1, 2)

            pe.wait_ge(sems["sq_ready"], 3)
            sum_squares(S, "sumsq")

            pe.wait_ge(sems["sq_ready"], 4)
            sum_squares(S, "sumsq", per_token=True)
            pe.wait_ge(sems["u_ready"], 3)
            pe.wait_ge(sems["hidden_val"], M0["k0"])
            for name in ("sq", "sk"):
                project(f"{name}0", t0=META, t=S)
                project(f"{name}1", t0=META, t=S)
            pe.wait_ge(sems["rms_ready"], 4)
            for j in range(2):
                pe.wait_ge(sems["sb_sq_ready"], j + 1)
                for q in range(2):
                    ins = mm(aux[:, 2 * j + q, :], C("ones_half"), f("f1", 0, 4, S)[:, 2 * q:2 * q + 2, :] if j == 0
                             else f("f1", 1024, 4, S)[:, 2 * q:2 * q + 2, :], start=True, stop=True)
                ins.then_inc(sems["sb_sumsq"], 1)
            project_tokens("sv0")
            project_tokens("sv1")
            pe.wait_ge(sems["sg_in"], 32)
            pe.wait_ge(sems["sb_qk_ready"], 1)
            for g in range(8):
                ins = nc.tensor.transpose(aux[:, g // 4, (g % 4) * P:(g % 4 + 1) * P], f("f6", 0, 8, P)[:, g, :], C("ident"))
            ins.then_inc(sems["sg_turned"], 1)
            pe.wait_ge(sems["sg_t_ready"], 1)

            sb_q, sb_k, sb_v = f("f3", 0, 4, S), f("f3", 1024, 4, S), f("f5", 0, 2, 512)

            def sb_scores(a):
                if a:
                    pe.wait_ge(sems["sb_out_ready"], a)
                for e in range(2):
                    p0 = 64 * e
                    mm(aux[:, e, 0:S], sb_k[p0:p0 + 64, a, 0:P], sb_q[p0:p0 + 64, a, :], start=True, stop=True)
                    ins = mm(aux[:, e, S:S + P], sb_k[p0:p0 + 64, a, P:S], sb_q[p0:p0 + 64, a, P:S], start=True, stop=True)
                ins.then_inc(sems["sb_scores"], 1)

            def sb_suffix(a):
                pe.wait_ge(sems["sb_soft"], a + 1)
                soft = f("f2", 768, 2, 384)
                for e in range(2):
                    mm(aux[:, 2 + e, 0:S], C("neg_tri"), soft[:, e, 0:S], start=True, stop=False, skip_group_check=True)
                    mm(aux[:, 2 + e, P:S], C("neg_ones"), soft[:, e, S:S + P], start=False, stop=True, skip_group_check=True)
                    ins = mm(aux[:, 2 + e, S:S + P], C("neg_tri"), soft[:, e, S:S + P], start=True, stop=True)
                ins.then_inc(sems["sb_suffix"], 1)

            def sb_values(a):
                pe.wait_ge(sems["sb_attn"], a + 1)
                attn = f("f2", 768, 2, 384)
                for e in range(2):
                    h = 2 * a + e
                    o = aux[64 * e:64 * e + 64, 0, :]
                    mm(o[:, 0:S], sb_v[:, 0, 64 * h:64 * h + 64], attn[:, e, 0:S], start=True, stop=False, skip_group_check=True)
                    ins = mm(o[:, P:S], sb_v[:, 1, 64 * h:64 * h + 64], attn[:, e, S:S + P], start=False, stop=True,
                             skip_group_check=True)
                ins.then_inc(sems["sb_out"], 1)

            read_out("sv1")
            for a in range(4):
                sb_scores(a)
                project_tokens(f"za{a}")
                sb_suffix(a)
                sb_values(a)
            pe.wait_ge(sems["vg_ready"], 1)
            pe.wait_ge(sems["sb_out_ready"], 4)
            vg = f("f1", 2048, 2, 512)
            wct = f("f6", 0, 8, P)
            for g in range(8):
                ins = mm(aux[:, g // 4, (g % 4) * P:(g % 4 + 1) * P], wct[:, g, :],
                         vg[:, :, g * 64:(g + 1) * 64], start=True, stop=True)
            ins.then_inc(sems["mixed"], 1)
            pe.wait_ge(sems["ya_ready"], 1)
            ya = f("f1", 2048, 2, 512)
            for q in range(4):
                for b in range(2):
                    ins = nc.tensor.transpose(aux[:, 2 + q // 2, (q % 2) * S + b * P:(q % 2) * S + (b + 1) * P],
                                              ya[:, b, q * P:(q + 1) * P], C("ident"))
            ins.then_inc(sems["ya_turned"], 1)
            pe.wait_ge(sems["y_even_ready"], 1)
            for c in range(4):
                project(f"eo{c}", src=v, t=S)
            pe.wait_ge(sems["sq_ready"], 5)
            sum_squares(S, "sumsq")
            hidden_layer(M0, 4, 4)

            pe.wait_ge(sems["sq_ready"], 6)
            sum_squares(S, "sumsq", per_token=True)
            pe.wait_ge(sems["u_ready"], 5)
            pe.wait_ge(sems["hidden_val"], M1["k0"])
            project_tokens("gates", 8)
            project("qk0", t0=META, t=S)
            pe.wait_ge(sems["gates_ready"], 1)
            for j in range(2):
                for b in range(2):
                    ins = nc.tensor.transpose(aux[0:4, 1 + j, b * P:(b + 1) * P], gat[:, 8 * b + 4 * j:8 * b + 4 * j + 4], C("ident"))
            ins.then_inc(sems["gates_turned"], 1)
            project("qk1", t0=META, t=S)
            rows = f("f6", 1536, 3, S)
            pe.wait_ge(sems["rows_ready"], 1)
            for b in range(2):
                ins = nc.tensor.transpose(aux[:, 0, 4 * b:4 * b + 4], rows[0:4, 0, b * P:(b + 1) * P], C("ident")[0:4, 0:4])
            ins.then_inc(sems["a_turned"], 1)
            project("qk2", t0=META, t=S)
            project("qk3", t0=META, t=S)
            for j in range(4):
                project_tokens(f"ov{j}")
            pe.wait_ge(sems["conv_done"], 1)
            read_out("ov3")
            pe.wait_ge(sems["a_cols_ready"], 1)
            oqk = f("f3", 0, 8, S)
            ov = f("f5", 0, 2, D)
            osd = f("f6", 384, 384)
            oh = f("f1", 0, 8, S)
            for h in range(4):
                if h:
                    pe.wait_ge(sems["oh_ready"], h)
                mm(aux[:, 0, 0:S], oqk[:, 4 + h, 0:P], oqk[:, h, :], start=True, stop=True)
                mm(aux[:, 0, S:S + P], oqk[:, 4 + h, P:S], oqk[:, h, P:S], start=True, stop=True)
                pick = LC("pick_head")[0:4, h * P:(h + 1) * P]
                mm(aux[:, 1, 0:S], pick, rows[0:4, 1, :], start=True, stop=True)
                mm(aux[:, 1, S:2 * S], pick, rows[0:4, 2, :], start=True, stop=True).then_inc(sems["o_scores"], 1)
                project(f"og{h}", t0=META, t=S)
                pe.wait_ge(sems["osd_ready"], h + 1)
                mm(aux[:, 2, 0:S], C("ones"), osd[:, 0:S], start=True, stop=False, skip_group_check=True)
                mm(aux[:, 2, P:S], C("ones"), osd[:, S:S + P], start=False, stop=True,
                   skip_group_check=True).then_inc(sems["o_den"], 1)
                for j in range(2):
                    c = 256 * h + 128 * j
                    mm(aux[:, 3, j * S:(j + 1) * S], ov[:, 0, c:c + P], osd[:, 0:S], start=True, stop=False, skip_group_check=True)
                    ins = mm(aux[:, 3, j * S + P:(j + 1) * S], ov[:, 1, c:c + P], osd[:, S:S + P], start=False, stop=True,
                             skip_group_check=True)
                ins.then_inc(sems["o_num"], 1)
            pe.wait_ge(sems["oh_sq_ready"], 1)
            osq = f("f2", 0, 8, S)
            for h in range(4):
                for j in range(2):
                    ins = mm(aux[:, h, 0:S], C("ones"), osq[:, 2 * h + j, :], start=j == 0, stop=j == 1)
            ins.then_inc(sems["oh_sumsq"], 1)
            pe.wait_ge(sems["y_odd_ready"], 1)
            for c in range(4):
                project(f"oo{c}", src=v, t=S)
            pe.wait_ge(sems["sq_ready"], 7)
            sum_squares(S, "sumsq")
            hidden_layer(M1, 6, 6)
            pe.wait_ge(sems["final_ready"], 1)
            for b in range(2):
                for k in range(KT):
                    bank = proj[:, 2 * b + k // 4, :]
                    ins = nc.tensor.transpose(bank[:, (k % 4) * P:(k % 4 + 1) * P], x2[:, k, b * P:(b + 1) * P], C("ident"))
                ins.then_inc(sems["out_turned"], 1)

        @block.scalar
        def _(eng):
            act = nc.scalar.activation
            A = Lane(eng, sems, "act_step")
            done = [0]

            def split(n, i=None):
                eng.wait_ge(sems[f"raw_landed{n % RING}"], at(lambda m: landed[m], n, i))
                if n >= RING:
                    eng.wait_ge(sems["chunk_used"], at(lambda m: m - RING + 1, n, i))
                wd = width_of(n)
                A.post(act(whi[:, n % RING, 0:wd], raw[:, n % RING, 0:wd], ACT.Copy), "hi_ready")

            def pump(n):
                while done[0] <= min(n + AHEAD, len(chunks) - 1):
                    split(done[0])
                    done[0] += 1

            def scaled_hi(k0, gain, tokens, x, dst=u, t0=0):
                for k in range(KT):
                    ins = act(dst[:, 0, k, t0:t0 + tokens], x[:, k, :], ACT.Copy, scale=V(gain, k0 + k))
                    A.post(ins, "u_hi")

            def root(src, dst, scale, eps_ap, name):
                A.post(act(dst, src, ACT.Sqrt, bias=eps_ap, scale=scale), name)

            def read_out(name):
                eng.wait_ge(sems["proj_free"], order[index[name]] + 1)

            split(0)
            split(1)
            done[0] = 2
            eng.wait_ge(sems["par_in"], 16)
            eng.wait_ge(sems["small_ready"], 1)
            for k in range(KT):
                eng.wait_ge(sems["x_ready"], k + 1)
                A.post(act(u[:, 0, k, :], x_all[:, k, :], ACT.Copy, scale=V("norm_mix", k)), "u_hi")
            A.post(act(sq, x_all[:, :, :], ACT.Square), "sq_ready")
            A.post(act(small[:, 4:20], par[:, PAR_COLS["decay_f"][0]:PAR_COLS["decay_f"][0] + 16], ACT.Exp), "lg_ready")
            eng.wait_ge(sems["sumsq"], 1)
            root(aux[:, 0, 0:L], r_all[:, 0, :], 1.0 / D, eps, "root_ready")
            for name in ("rq0", "rq1", "rk0", "rk1", "rv0", "rv1", "rv2", "rv3", "c0", "c1", "c2"):
                pump(index[name])
            read_out("c2")
            A.post(act(low_sq, low[:, 0:3 * S + 2 * L], ACT.Square), "low_sq_ready")
            eng.wait_ge(sems["low_sumsq"], 1)
            root(aux[:, 0, 0:S], r_all[:, 1, 0:S], 1.0 / 384, eps, "root_ready")
            root(aux[:, 1, 0:L], r_all[:, 2, :], 1.0 / 256, eps, "root_ready")
            for j in range(3):
                A.post(act(v[:, 0, j, :], acq[:, j, :], ACT.Copy, scale=V("q_norm", j)), "low_hi")
            for j in range(2):
                A.post(act(ckv_split(0, j), ackv[:, j, :], ACT.Copy, scale=V("kv_norm", j)), "low_hi")
            for h in range(HEADS):
                eng.wait_ge(sems["dec_arg"], h + 1)
                A.run(act(dec[:, 0:2, :], dec[:, 0:2, :], ACT.Exp))
                A.post(act(dec[0:META, 2, :], dec[0:META, 2, :], ACT.Exp), "dec_ready")
                name = f"rg{h}" if h < 4 else f"gm{h - 4}"
                pump(index[name])
                b = 2 * (order[index[name]] % 2)
                if h < 4:
                    eng.wait_ge(sems["gate_scaled"], h + 1)
                    A.post(act(proj[:, b:b + 2, 0:S], rg[:, 2 * h:2 * h + 2, :], ACT.Tanh, scale=0.5), "gate_tanh")
                else:
                    read_out(name)
                    t = th_m[:, 2 * (h - 4):2 * (h - 4) + 2, :]
                    A.post(act(t, t, ACT.Tanh, scale=0.5), "gate_tanh")
            pump(index["uq0"])
            pump(index["uq1"])
            eng.wait_ge(sems["d_ready"], 1)
            A.post(act(d_sq, o_ret, ACT.Square), "d_sq_ready")
            pump(index["ukv"])
            eng.wait_ge(sems["gn_var"], 1)
            A.post(act(d_sq, aux[:, :, :].rearrange("p a (b t) -> p (a b) t", b=2), ACT.Sqrt, bias=gn_eps, scale=1.0 / P), "gn_root")
            eng.wait_ge(sems["chunk_used"], index["ukv"] + 1)
            eng.wait_ge(sems["y_ret_val"], 1)
            A.post(act(v[:, 0, :, :], rg, ACT.Copy, scale=0.5), "y_ret_hi")

            def soft(h):
                eng.wait_ge(sems["neg_max"], h + 1)
                for b in range(2):
                    ins = act(prob[:, h % 2, b, :], aux[:, b, 0:L], ACT.Exp, bias=nb[:, b:b + 1], scale=96.0 ** -0.5,
                              accum_out=sums[:, b:b + 1])
                    if b == 0:
                        A.run(ins)
                A.post(ins, "mla_exp")

            soft(0)
            for h in range(HEADS):
                name = f"ro{h}" if h < 4 else f"gr{h - 4}"
                if h + 1 < HEADS:
                    soft(h + 1)
                pump(index[name])
                if h >= 4:
                    b = 2 * (order[index[name]] % 2)
                    eng.wait_ge(sems["gate_scaled"], h + 1)
                    A.post(act(proj[:, b:b + 2, 0:S], proj[:, b:b + 2, 0:S], ACT.Tanh, scale=0.5), "gate_tanh")
            eng.wait_ge(sems["o_mla_ready"], 8)
            for a in range(4):
                A.post(act(v[:, 0, a, :], o_mla(a), ACT.Copy), "y_mla_hi")
            pump(index["mo0"])
            pump(index["mo1"])
            eng.wait_ge(sems["merged"], 1)
            A.post(act(u[:, 0, :, META:L], yr, ACT.Copy, scale=0.5), "merged_hi")
            for c in range(4):
                pump(index[f"wo{c}"])

            def norm(x_ready, gain, k0, norm_no, per_token=False, hi=True):
                if isinstance(x_ready, str):
                    read_out(x_ready)
                else:
                    eng.wait_ge(sems["x_new"], x_ready)
                A.post(act(f("f2", 0, KT, S), x2, ACT.Square), "sq_ready")
                if hi:
                    scaled_hi(k0, gain, S, x2, t0=META)
                eng.wait_ge(sems["sumsq"], norm_no + 1)
                if per_token:
                    A.run(act(r_tok, aux[:, 1, 0:2], ACT.Sqrt, bias=eps, scale=1.0 / D))
                root(aux[:, 0, 0:S], r_all[:, 0, 0:S], 1.0 / D, eps, "root_ready")

            def hidden_layer(d):
                tag, n_h, k0 = d["tag"], d["n"], d["k0"]
                g = loop_first[tag]

                def step(n, k, i=None):
                    if i is None:
                        pump(n)
                    else:
                        split(n + AHEAD, i)
                    if k is None:
                        return
                    kk = (lambda c: k0 + k + c if i is None else i * 2 + (k0 + k + c))

                    def buffer_free():
                        if k >= 1:
                            eng.wait_ge(sems["chunk_used"], at(lambda m: m, g + 2 * k - 1, i))

                    if tag == "ffn":
                        eng.wait_ge(sems["ffn_gate_scaled"], kk(1))
                        A.post(act(proj[:, 2 * (k % 2), 0:S], f("f1", 0, S), ACT.Tanh, scale=0.5), "ffn_gate_tanh")
                        eng.wait_ge(sems["hidden_val"], kk(1))
                        buffer_free()
                        A.post(act(v[:, 0, 2 * (k % 2), :], f("f1", 256, S), ACT.Copy), "hidden_hi")
                    else:
                        eng.wait_ge(sems["hidden_val"], kk(1))
                        buffer_free()
                        A.post(act(v[:, 0, 2 * (k % 2):2 * (k % 2) + 2, :], f("f1", 512, 2, S), ACT.Copy), "hidden_hi")

                step(g, 0)
                turns = (n_h - 2) // 2
                with eng.Fori(0, turns) as i:
                    A.enter(i, {"hi_ready": 4, "hidden_hi": 2, "ffn_gate_tanh": 2 if tag == "ffn" else 0})
                    step(g + 1, 1, i)
                    step(g + 2, None, i)
                    step(g + 3, 2, i)
                    step(g + 4, None, i)
                A.leave(turns)
                done[0] += 4 * turns
                step(g + 2 * n_h - 3, n_h - 1)
                pump(g + 2 * n_h - 2)
                pump(g + 2 * n_h - 1)

            norm("wo3", "ffn", 0, 1)
            hidden_layer(FFN)
            norm(1, None, 0, 2, hi=False)
            norm(2, "mix2", 0, 3, per_token=True)
            sbq = f("f4", 0, 4, S)
            sbk = f("f4", 1024, 4, S)
            for j, (name, buf) in enumerate((("sq", sbq), ("sk", sbk))):
                pump(index[f"{name}0"])
                pump(index[f"{name}1"])
                read_out(f"{name}1")
                A.post(act(f("f1", 1024 * j, 4, S), buf, ACT.Square), "sb_sq_ready")
            for j in range(2):
                eng.wait_ge(sems["sb_sumsq"], j + 1)
                A.post(act(f("f1", 1024 * j, 4, S), aux[:, 2 * j:2 * j + 2, :].rearrange("p a (b t) -> p (a b) t", b=2),
                           ACT.Sqrt, bias=eps, scale=1.0 / 64), "sb_root")
            pump(index["sv0"])
            pump(index["sv1"])
            zm, soft_b, e_b = f("f2", 0, 2, 384), f("f2", 768, 2, 384), f("f1", 2048, 2, 384)
            for a in range(4):
                pump(index[f"za{a}"])
                eng.wait_ge(sems["sb_z"], a + 1)
                A.run(act(e_b, zm, ACT.Abs))
                A.run(act(e_b, e_b, ACT.Exp, scale=-1.0))
                A.post(act(e_b, e_b, ACT.Ln, bias=one), "sb_log")
                eng.wait_ge(sems["sb_arg"], a + 1)
                A.post(act(soft_b, zm, ACT.Exp), "sb_exp")
            za = f("f4", 0, 2, D)
            read_out("za3")
            A.post(act(za, za, ACT.Gelu_apprx_tanh), "gelu_ready")
            eng.wait_ge(sems["vg_centred"], 1)
            for b in range(2):
                A.run(act(f("f2", 1536, 512), f("f1", 2048, 2, 512)[:, b, :], ACT.Square, accum_out=stat[:, 2 + b:3 + b]))
            A.post(act(stat[:, 4:6], stat[:, 2:4], ACT.Sqrt, bias=eps, scale=1.0 / 512), "vg_root")
            eng.wait_ge(sems["ya_feat"], 1)
            A.run(act(v[:, 0, 0:4, :], f("f1", 0, 4, S), ACT.Copy))
            A.post(act(v[:, 0, 4:8, :], f("f1", 1024, 4, S), ACT.Copy), "y_even_hi")
            for c in range(4):
                pump(index[f"eo{c}"])
            norm("eo3", "mlp2", 0, 4)
            hidden_layer(M0)

            norm(3, "mix2", 8, 5, per_token=True)
            pump(index["gates"])
            fg = gat.rearrange("p (b c) -> p b c", b=2)[:, :, 4:8]
            ftmp = stat[:, 0:6]
            ab = f("f6", 0, 8)
            eng.wait_ge(sems["gates_raw"], 1)
            A.run(act(ab.rearrange("p (b c) -> p b c", b=2), fg, ACT.Abs))
            A.run(act(ab, ab, ACT.Exp, scale=-1.0))
            A.post(act(ab, ab, ACT.Ln, bias=one), "gates_log")
            conv_in, conv_out = f("f1", 0, 8, S + 3), f("f3", 0, 8, S)
            th = f("f2", 0, 8, S)
            for c in range(4):
                pump(index[f"qk{c}"])
            for j in range(4):
                pump(index[f"ov{j}"])
            eng.wait_ge(sems["conv_ready"], 1)
            A.post(act(th, conv_out, ACT.Tanh, scale=0.5), "conv_tanh")
            ow = f("f6", 0, 384)
            for h in range(4):
                pump(index[f"og{h}"])
                eng.wait_ge(sems["ow_arg"], h + 1)
                A.post(act(ow, ow, ACT.Exp, scale=-1.0), "ow_exp")
                A.post(act(f("f6", 768, S), aux[:, 1, S:2 * S], ACT.Exp, scale=-1.0), "em_ready")
                read_out(f"og{h}")
                t = f("f4", 0, 8, S)[:, 2 * h:2 * h + 2, :]
                A.post(act(t, t, ACT.Tanh, scale=0.5), "gate_tanh")
            eng.wait_ge(sems["oh_ready"], 4)
            A.post(act(f("f2", 0, 8, S), f("f1", 0, 8, S), ACT.Square), "oh_sq_ready")
            eng.wait_ge(sems["oh_sumsq"], 1)
            A.post(act(f("f2", 0, 4, S), aux[:, :, 0:S], ACT.Sqrt, bias=eps, scale=1.0 / 256), "oh_root")
            eng.wait_ge(sems["y_odd_val"], 1)
            A.post(act(v[:, 0, :, :], f("f1", 0, 8, S), ACT.Copy, scale=0.5), "y_odd_hi")
            for c in range(4):
                pump(index[f"oo{c}"])
            norm("oo3", "mlp2", 8, 6)
            hidden_layer(M1)

        @block.vector
        def _(eng):
            ve = nc.vector
            B = Lane(eng, sems, "dve_step")
            done = [0]
            free = [0]

            def tt(o, a, b, op):
                return ve.tensor_tensor(o, a, b, op)

            def stt(o, a, s, b, op0, op1):
                return ve.scalar_tensor_tensor(out=o, in0=a, scalar=s, in1=b, op0=op0, op1=op1)

            def ts(o, a, s, op, s2=None, op2=None):
                return ve.tensor_scalar(o, a, s, s2, op) if op2 is None else ve.tensor_scalar(o, a, s, s2, op, op2)

            def split(n, i=None):
                eng.wait_ge(sems["hi_ready"], at(lambda m: m + 1, n, i))
                wd = width_of(n)
                s = n % RING
                B.post(tt(wlo[:, s, 0:wd], raw[:, s, 0:wd], whi[:, s, 0:wd].bitcast(F32), ALU.subtract), "lo_ready")

            def pump(n):
                while done[0] <= min(n + AHEAD, len(chunks) - 1):
                    split(done[0])
                    done[0] += 1

            def arrive(name):
                n = index[name]
                pump(n)
                eng.wait_ge(sems["chunk_used"], n + 1)
                return 2 * (order[n] % 2)

            def freed(ins):
                B.post(ins, "proj_free")

            def hi32(ap):
                return ap.bitcast(F32)

            B.run(ve.memset(eps, EPS))
            B.run(ve.memset(gn_eps, GN_EPS))
            B.post(ve.memset(one, 1.0), "small_ready")
            for k in range(KT):
                bank = (proj if k < 4 else aux)[:, k % 4, 0:L]
                eng.wait_ge(sems["x_turned"], k + 1)
                B.post(ve.tensor_copy(x_all[:, k, :], bank), "x_ready")
            split(0)
            split(1)
            done[0] = 2
            eng.wait_ge(sems["par_in"], 16)

            def scaled_lo(gain, k0, x, tokens, count, t0=0):
                for k in range(KT):
                    eng.wait_ge(sems["u_hi"], count + k + 1)
                    o = u[:, 1, k, t0:t0 + tokens]
                    ins = stt(o, x[:, k, :], V(gain, k0 + k), hi32(u[:, 0, k, t0:t0 + tokens]), ALU.mult, ALU.subtract)
                    if k < KT - 1:
                        B.run(ins)
                B.post(ins, "u_ready")

            scaled_lo("norm_mix", 0, x_all, L, 0)
            eng.wait_ge(sems["lg_ready"], 1)
            B.run(ts(small[:, 4:12], small[:, 4:12], -1.0, ALU.mult))
            pump(index["rq0"])
            eng.wait_ge(sems["root_ready"], 1)
            r1 = r_all[:, 0, :]
            B.post(ve.reciprocal(r1, r1), "rms_ready")
            rq = r1[:, META:L]
            for c in range(2):
                b = arrive(f"rq{c}")
                freed(tt(preq[:, 2 * c:2 * c + 2, :], proj[:, b:b + 2, 0:S], bc(rq, 2), ALU.mult))
            b = arrive("rk0")
            freed(tt(prek[:, 0:2, :], proj[:, b:b + 2, 0:L], bc(r1, 2), ALU.mult))
            eng.wait_ge(sems["q_rotated"], 1)
            rot = aux[:, 0:2, :].rearrange("p a (b t) -> p (a b) t", b=2)
            B.run(tt(q_ret, rot, bc(C("sin_ret")[:, META:L], 4), ALU.mult))
            B.run(tt(preq, preq, bc(C("cos_ret")[:, META:L], 4), ALU.mult))
            B.post(tt(q_ret, q_ret, preq, ALU.add), "q_roped")
            b = arrive("rk1")
            freed(tt(prek[:, 2:4, :], proj[:, b:b + 2, 0:L], bc(r1, 2), ALU.mult))
            b = arrive("rv0")
            freed(tt(rv_feat[:, 0:2, :], proj[:, b:b + 2, 0:L], bc(r1, 2), ALU.mult))
            eng.wait_ge(sems["k_rotated"], 1)
            B.run(tt(k_ret, aux[:, :, 0:L], bc(C("sin_ret"), 4), ALU.mult))
            B.run(tt(prek, prek, bc(C("cos_ret"), 4), ALU.mult))
            B.post(tt(k_ret, k_ret, prek, ALU.add), "k_roped")
            for c in range(1, 4):
                b = arrive(f"rv{c}")
                freed(tt(rv_feat[:, 2 * c:2 * c + 2, :], proj[:, b:b + 2, 0:L], bc(r1, 2), ALU.mult))
            b = arrive("c0")
            freed(tt(acq[:, 0:2, :], proj[:, b:b + 2, 0:S], bc(rq, 2), ALU.mult))
            for j in range(6):
                m = KEY_BLOCKS[j // 2][1]
                eng.wait_ge(sems["rv_turned"], j + 1)
                B.post(ve.tensor_copy(rv_tok[0:m, j // 2, 512 * (j % 2):512 * (j % 2 + 1)], aux[0:m, j % 4, :]), "rv_tok_ready")
            b = arrive("c1")
            B.run(tt(acq[:, 2, :], proj[:, b, 0:S], rq, ALU.mult))
            freed(tt(ackv[:, 0, :], proj[:, b + 1, 0:L], r1, ALU.mult))
            b = arrive("c2")
            B.run(tt(ackv[:, 1, :], proj[:, b, 0:L], r1, ALU.mult))
            freed(tt(akr[64:96, :], proj[64:96, b + 1, 0:L], r1[64:96, :], ALU.mult))
            eng.wait_ge(sems["kr_rotated"], 1)
            krr = kr[64:96, :]
            B.run(tt(krr, aux[64:96, 2, 0:L], C("sin_mla")[64:96, :], ALU.mult))
            B.run(tt(akr[64:96, :], akr[64:96, :], C("cos_mla")[64:96, :], ALU.mult))
            B.run(tt(krr, krr, akr[64:96, :], ALU.add))
            eng.wait_ge(sems["root_ready"], 3)
            B.run(ve.reciprocal(r_all[:, 1, 0:S], r_all[:, 1, 0:S]))
            B.run(ve.reciprocal(r_all[:, 2, :], r_all[:, 2, :]))
            for j in range(3):
                eng.wait_ge(sems["low_hi"], j + 1)
                B.run(stt(v[:, 1, j, :], acq[:, j, :], V("q_norm", j), hi32(v[:, 0, j, :]), ALU.mult, ALU.subtract))
            for j in range(2):
                eng.wait_ge(sems["low_hi"], j + 4)
                (B.run if j == 0 else lambda ins: B.post(ins, "low_done"))(stt(ckv_split(1, j), ackv[:, j, :], V("kv_norm", j), hi32(ckv_split(0, j)), ALU.mult, ALU.subtract))

            rel = C("rel").rearrange("p (a t) -> p a t", a=3)

            def decay_arg(h):
                B.run(ts(dec[:, 0:2, :], rel[:, 0:2, :], lgf[:, h:h + 1], ALU.mult))
                B.run(ts(dec[0:META, 2, :], rel[0:META, 2, :], lgf[0:META, h:h + 1], ALU.mult))
                B.run(stt(dec[:, 0:2, :], rel[:, 0:2, :], lgb[:, h:h + 1], dec[:, 0:2, :], ALU.mult, ALU.min))
                B.post(stt(dec[0:META, 2, :], rel[0:META, 2, :], lgb[0:META, h:h + 1], dec[0:META, 2, :], ALU.mult, ALU.min), "dec_arg")

            for h in range(HEADS):
                decay_arg(h)
                eng.wait_ge(sems["dec_ready"], h + 1)
                eng.wait_ge(sems["ret_scores"], h + 1)
                b = 2 * (h % 2)
                B.run(stt(sd[:, h % 2, 0:2, :], aux[:, b, :].rearrange("p (a t) -> p a t", a=2), 0.125, dec[:, 0:2, :],
                          ALU.mult, ALU.mult))
                B.post(stt(sd[0:META, h % 2, 2, :], aux[0:META, b + 1, 0:S], 0.125, dec[0:META, 2, :], ALU.mult, ALU.mult), "sd_ready")
                if h < 4:
                    pb = arrive(f"rg{h}")
                    g2 = rg[:, 2 * h:2 * h + 2, :]
                    B.post(tt(g2, proj[:, pb:pb + 2, 0:S], bc(rq, 2), ALU.mult), "gate_scaled")
                    eng.wait_ge(sems["gate_tanh"], h + 1)
                    freed(stt(g2, proj[:, pb:pb + 2, 0:S], 1.0, g2, ALU.add, ALU.mult))
                else:
                    pb = arrive(f"gm{h - 4}")
                    freed(tt(th_m[:, 2 * (h - 4):2 * (h - 4) + 2, :], proj[:, pb:pb + 2, 0:S], bc(rq, 2), ALU.mult))
                eng.wait_ge(sems["ret_out"], h + 1)
                B.post(ve.tensor_copy(o_ret[:, h, :], aux[:, 2 * (h % 2) + 1, S:2 * S]), "o_ready")
            eng.wait_ge(sems["gn_sum"], 1)
            auxh = aux[:, :, :].rearrange("p a (b t) -> p (a b) t", b=2)
            B.post(stt(o_ret, auxh, -1.0 / P, o_ret, ALU.mult, ALU.add), "d_ready")

            def query_part(j):
                pb = arrive(f"uq{j}")
                src = proj[0:96, pb:pb + 2, :].rearrange("p a (b t) -> p (a b) t", b=2)
                freed(tt(q_pre[0:96, 4 * j:4 * j + 4, :], src, bc(r_all[0:96, 1, 0:S], 4), ALU.mult))

            query_part(0)
            query_part(1)
            eng.wait_ge(sems["gn_root"], 1)
            B.run(ve.reciprocal(d_sq, d_sq))
            B.run(tt(o_ret, o_ret, d_sq, ALU.mult))
            for h in range(HEADS):
                ins = stt(rg[:, h, :], o_ret[:, h, :], V("gn", h), rg[:, h, :], ALU.mult, ALU.mult)
                if h < HEADS - 1:
                    B.run(ins)
            B.post(ins, "y_ret_val")
            pump(index["ukv"])
            rkv = r_all[:, 2, :]
            pairs = k_all.rearrange("p (a e) t -> p e a t", e=2)
            for half in range(4):
                if half < 3:
                    eng.wait_ge(sems["kv_mm"], half + 1)
                else:
                    eng.wait_ge(sems["chunk_used"], index["ukv"] + 1)
                b = 2 * (half % 2)
                if half < 2:
                    for e in range(2):
                        ins = tt(pairs[0:64, e, 2 * half:2 * half + 2, :], proj[64 * e:64 * e + 64, b:b + 2, 0:L],
                                 bc(rkv[64 * e:64 * e + 64, :], 2), ALU.mult)
                        if e == 0:
                            B.run(ins)
                    B.post(ins, "kv_half")
                elif half == 2:
                    B.post(tt(v_feat[:, 0:2, :], proj[:, b:b + 2, 0:L], bc(rkv, 2), ALU.mult), "kv_half")
                else:
                    freed(tt(v_feat[:, 2:4, :], proj[:, b:b + 2, 0:L], bc(rkv, 2), ALU.mult))
            B.run(ve.tensor_copy(k_all[64:96, :, :], bc(kr[64:96, :], 8)))
            eng.wait_ge(sems["q_mla_rotated"], 1)
            B.run(tt(q_all[0:96], auxh[0:96], bc(C("sin_mla")[0:96, META:L], 8), ALU.mult))
            B.run(tt(q_pre[0:96], q_pre[0:96], bc(C("cos_mla")[0:96, META:L], 8), ALU.mult))
            B.post(tt(q_all[0:96], q_all[0:96], q_pre[0:96], ALU.add), "q_mla_roped")
            eng.wait_ge(sems["y_ret_hi"], 1)
            B.post(stt(v[:, 1, :, :], rg, 0.5, hi32(v[:, 0, :, :]), ALU.mult, ALU.subtract), "y_ret_ready")
            eng.wait_ge(sems["v_turned"], 1)
            B.run(ve.tensor_copy(v_tok[:, 0:2, :], aux[:, 0:2, :]))
            B.post(ve.tensor_copy(v_tok[0:META, 2, :], aux[0:META, 2, :]), "v_tok_ready")

            def soft_max(h):
                eng.wait_ge(sems["mla_scores"], h + 1)
                B.run(ve.reduce_max(mx, aux[:, 0:2, 0:L], AX_X))
                B.post(ts(nb, mx, -(96.0 ** -0.5), ALU.mult), "neg_max")
                eng.wait_ge(sems["mla_exp"], h + 1)
                B.run(ve.reciprocal(rs, sums))
                for b in range(2):
                    ins = ts(prob[:, h % 2, b, :], prob[:, h % 2, b, :], rs[:, b:b + 1], ALU.mult)
                    if b == 0:
                        B.run(ins)
                B.post(ins, "prob_ready")

            soft_max(0)
            for h in range(HEADS):
                eng.wait_ge(sems["prob_turned"], h + 1)
                B.run(ve.tensor_copy(pt[:, 0:2, :], aux[:, 2, :].rearrange("p (a t) -> p a t", a=2)))
                B.post(ve.tensor_copy(pt[0:META, 2, :], aux[0:META, 3, 0:S]), "pt_ready")
                if h + 1 < HEADS:
                    soft_max(h + 1)
                if h < 4:
                    b = arrive(f"ro{h}")
                    freed(ve.tensor_copy(yr[:, 2 * h:2 * h + 2, :], proj[:, b:b + 2, 0:S]))
                else:
                    b = arrive(f"gr{h - 4}")
                    y2 = yr[:, 2 * (h - 4):2 * (h - 4) + 2, :]
                    B.post(tt(proj[:, b:b + 2, 0:S], proj[:, b:b + 2, 0:S], bc(rq, 2), ALU.mult), "gate_scaled")
                    eng.wait_ge(sems["gate_tanh"], h + 5)
                    freed(stt(y2, proj[:, b:b + 2, 0:S], 1.0, y2, ALU.add, ALU.mult))
                eng.wait_ge(sems["mla_out"], h + 1)
                p0 = 64 * (h % 2)
                B.post(ve.tensor_copy(o_mla(h // 2)[p0:p0 + 64, :], aux[p0:p0 + 64, 3, S:2 * S]), "o_mla_ready")
            for a in range(4):
                eng.wait_ge(sems["y_mla_hi"], a + 1)
                ins = tt(v[:, 1, a, :], o_mla(a), hi32(v[:, 0, a, :]), ALU.subtract)
                if a < 3:
                    B.run(ins)
            B.post(ins, "y_mla_ready")
            for c in range(2):
                b = arrive(f"mo{c}")
                t = th_m[:, 4 * c:4 * c + 4, :]
                freed(stt(t, t, 1.0, proj[:, b:b + 2, :].rearrange("p a (b t) -> p (a b) t", b=2), ALU.add, ALU.mult))
            B.post(tt(yr, yr, th_m, ALU.add), "merged")
            eng.wait_ge(sems["merged_hi"], 1)
            B.post(stt(u[:, 1, :, META:L], yr, 0.5, hi32(u[:, 0, :, META:L]), ALU.mult, ALU.subtract), "merged_ready")

            def add_blocks(name):
                for c in range(4):
                    b = arrive(f"{name}{c}")
                    t = x2[:, 2 * c:2 * c + 2, :]
                    freed(tt(t, t, proj[:, b:b + 2, 0:S], ALU.add))

            add_blocks("wo")
            rms = r_all[:, 0, 0:S]

            def norm(gain, k0, norm_no, hi_count, per_token=False):
                if gain:
                    scaled_lo(gain, k0, x2, S, hi_count, t0=META)
                eng.wait_ge(sems["root_ready"], norm_no + 3)
                if per_token:
                    B.run(ve.reciprocal(r_tok, r_tok))
                B.post(ve.reciprocal(rms, rms), "rms_ready")

            def hidden_layer(d):
                tag, n_h, k0 = d["tag"], d["n"], d["k0"]
                g = loop_first[tag]

                def step(n, k, i=None):
                    if i is None:
                        pump(n)
                    else:
                        split(n + AHEAD, i)
                    if k is None:
                        return
                    kk = (lambda c: k0 + k + c if i is None else i * 2 + (k0 + k + c))
                    eng.wait_ge(sems["chunk_used"], at(lambda m: m + 1, n, i))
                    b, slot = 2 * (k % 2), 2 * (k % 2)
                    if tag == "ffn":
                        g0, hid = f("f1", 0, S), f("f1", 256, S)
                        B.post(tt(g0, proj[:, b, 0:S], rms, ALU.mult), "ffn_gate_scaled")
                        eng.wait_ge(sems["ffn_gate_tanh"], kk(1))
                        B.run(stt(g0, proj[:, b, 0:S], 1.0, g0, ALU.add, ALU.mult))
                        B.post(tt(hid, g0, proj[:, b + 1, 0:S], ALU.mult), "hidden_val")
                        eng.wait_ge(sems["hidden_hi"], kk(1))
                        B.post(tt(v[:, 1, slot, :], hid, hi32(v[:, 0, slot, :]), ALU.subtract), "hidden_ready")
                    else:
                        rl, hid = f("f1", 0, 2, S), f("f1", 512, 2, S)
                        B.run(ts(rl, proj[:, b:b + 2, 0:S], 0.0, ALU.max))
                        B.post(tt(hid, rl, rl, ALU.mult), "hidden_val")
                        eng.wait_ge(sems["hidden_hi"], kk(1))
                        B.post(tt(v[:, 1, slot:slot + 2, :], hid, hi32(v[:, 0, slot:slot + 2, :]), ALU.subtract), "hidden_ready")

                step(g, 0)
                turns = (n_h - 2) // 2
                with eng.Fori(0, turns) as i:
                    B.enter(i, {"lo_ready": 4, "hidden_val": 2, "hidden_ready": 2, "dve_step": 2,
                                "ffn_gate_scaled": 2 if tag == "ffn" else 0})
                    step(g + 1, 1, i)
                    step(g + 2, None, i)
                    step(g + 3, 2, i)
                    step(g + 4, None, i)
                B.leave(turns)
                done[0] += 4 * turns
                step(g + 2 * n_h - 3, n_h - 1)
                pump(g + 2 * n_h - 2)
                pump(g + 2 * n_h - 1)
                eng.wait_ge(sems["chunk_used"], g + 2 * n_h)
                t = f("f1", 0, KT, S)
                if tag == "ffn":
                    B.run(stt(t, auxh, 0.5, bc(rms, KT), ALU.mult, ALU.mult))
                else:
                    B.run(tt(rms, rms, rms, ALU.mult))
                    B.run(tt(t, auxh, bc(rms, KT), ALU.mult))
                B.post(tt(x2, x2, t, ALU.add), "final_ready" if tag == "m1" else "x_new")

            norm("ffn", 0, 1, 8)
            hidden_layer(FFN)
            norm(None, 0, 2, 0)
            for k in range(KT):
                ins = stt(x2[:, k, :], x2[:, k, :], V("final", k), rms, ALU.mult, ALU.mult)
                if k < KT - 1:
                    B.run(ins)
            B.post(ins, "x_new")

            norm("mix2", 0, 3, 16, per_token=True)
            pre = (f("f4", 0, 4, S), f("f4", 1024, 4, S))
            root = (f("f1", 0, 4, S), f("f1", 1024, 4, S))
            fin = (f("f3", 0, 4, S), f("f3", 1024, 4, S))
            B.run(ts(qg8, V("sb_q"), 0.125, ALU.mult))
            for j, name in enumerate(("sq", "sk")):
                for c in range(2):
                    b = arrive(f"{name}{c}")
                    freed(tt(pre[j][:, 2 * c:2 * c + 2, :], proj[:, b:b + 2, 0:S], bc(rms, 2), ALU.mult))
            for j in range(2):
                eng.wait_ge(sems["sb_root"], j + 1)
                B.run(ve.reciprocal(root[j], root[j]))
                ins = stt(fin[j], pre[j], qg8 if j == 0 else V("sb_k"), root[j], ALU.mult, ALU.mult)
                if j == 0:
                    B.run(ins)
            B.post(ins, "sb_qk_ready")

            def per_token(name, dst, width=256):
                b = arrive(name)
                for j in range(2):
                    ins = ts(dst(j), proj[:, b + j, 0:width], r_tok[:, j:j + 1], ALU.mult)
                    if j == 0:
                        B.run(ins)
                freed(ins)

            sb_v = f("f5", 0, 2, 512)
            for c in range(2):
                per_token(f"sv{c}", lambda j: sb_v[:, j, c * 256:(c + 1) * 256])
            eng.wait_ge(sems["late_in"], 16)
            eng.wait_ge(sems["sg_turned"], 1)
            causal = LC("mask_causal")[:, 0:P]
            B.post(tt(f("f6", 0, 8, P), aux[:, 0:2, :].rearrange("p a (g t) -> p (a g) t", g=4), bc(causal, 8), ALU.mult), "sg_t_ready")
            zm, soft_b, e_b = f("f2", 0, 2, 384), f("f2", 768, 2, 384), f("f1", 2048, 2, 384)
            strict = bc(LC("mask_strict"), 2)
            za = f("f4", 0, 2, D)
            for a in range(4):
                eng.wait_ge(sems["sb_scores"], a + 1)
                B.post(tt(zm, aux[:, 0:2, 0:384], strict, ALU.mult), "sb_z")
                per_chunk = lambda j: za[:, j, a * 256:(a + 1) * 256]
                pump(index[f"za{a}"])
                eng.wait_ge(sems["sb_log"], a + 1)
                B.run(stt(soft_b, zm, 0.0, e_b, ALU.max, ALU.add))
                B.post(tt(soft_b, soft_b, strict, ALU.mult), "sb_soft")
                per_token(f"za{a}", per_chunk)
                eng.wait_ge(sems["sb_suffix"], a + 1)
                B.post(tt(zm, zm, aux[:, 2:4, 0:384], ALU.add), "sb_arg")
                eng.wait_ge(sems["sb_exp"], a + 1)
                B.post(tt(soft_b, soft_b, strict, ALU.mult), "sb_attn")
                eng.wait_ge(sems["sb_out"], a + 1)
                B.post(ve.tensor_copy(f("f1", 1024, 4, S)[:, a, :], aux[:, 0, 0:S]), "sb_out_ready")
            vg = f("f1", 2048, 2, 512)
            eng.wait_ge(sems["gelu_ready"], 1)
            B.run(ve.reduce_sum(stat[:, 0:2], za[:, :, 512:1024], AX_X))
            B.run(ts(stat[:, 0:2], stat[:, 0:2], 1.0 / 512, ALU.mult))
            for b in range(2):
                ins = ts(vg[:, b, :], za[:, b, 512:1024], stat[:, b:b + 1], ALU.subtract)
                if b == 0:
                    B.run(ins)
            B.post(ins, "vg_centred")
            eng.wait_ge(sems["vg_root"], 1)
            eng.wait_ge(sems["sg_in"], 32)
            B.run(ve.reciprocal(stat[:, 4:6], stat[:, 4:6]))
            ln = f("f6", 1024, 2, 512)
            for b in range(2):
                B.run(stt(vg[:, b, :], vg[:, b, :], stat[:, 4 + b:5 + b], ln[:, 0, :], ALU.mult, ALU.mult))
            B.post(tt(vg, vg, bc(ln[:, 1, :], 2), ALU.add), "vg_ready")
            eng.wait_ge(sems["mixed"], 1)
            for g in range(8):
                c = slice(g * 64, (g + 1) * 64)
                m = aux[:, g // 4, (g % 4) * P:(g % 4 + 1) * P].rearrange("p (b c) -> p b c", b=2)
                ins = stt(vg[:, :, c], m, V("sg_b", g), za[:, :, c], ALU.add, ALU.mult)
                if g < 7:
                    B.run(ins)
            B.post(ins, "ya_ready")
            eng.wait_ge(sems["ya_turned"], 1)
            B.post(ve.tensor_copy(f("f1", 0, 4, S), aux[:, 2:4, :].rearrange("p a (b t) -> p (a b) t", b=2)), "ya_feat")
            eng.wait_ge(sems["y_even_hi"], 1)
            B.run(tt(v[:, 1, 0:4, :], f("f1", 0, 4, S), hi32(v[:, 0, 0:4, :]), ALU.subtract))
            B.post(tt(v[:, 1, 4:8, :], f("f1", 1024, 4, S), hi32(v[:, 0, 4:8, :]), ALU.subtract), "y_even_ready")
            add_blocks("eo")
            norm("mlp2", 0, 4, 24)
            hidden_layer(M0)

            norm("mix2", 8, 5, 32, per_token=True)
            b = arrive("gates")
            B.run(ts(gat[:, 0:8], proj[:, b, 0:8], r_tok[:, 0:1], ALU.mult))
            freed(ts(gat[:, 8:16], proj[:, b + 1, 0:8], r_tok[:, 1:2], ALU.mult))
            ga = gat.rearrange("p (b c) -> p b c", b=2)
            ib = PAR_COLS["i_b"][0]
            B.post(tt(ga, ga, bc(par[:, ib:ib + 8], 2), ALU.add), "gates_raw")
            eng.wait_ge(sems["gates_log"], 1)
            ab = f("f6", 0, 8).rearrange("p (b c) -> p b c", b=2)
            B.post(stt(ga[:, :, 4:8], ga[:, :, 4:8], 0.0, ab, ALU.min, ALU.subtract), "gates_ready")
            rows, cum, ones_row = f("f6", 1536, 3, S)[0:4], f("f6", 1280, S)[0:4], f("f6", 1024, S)[0:4]
            conv_in, conv_out = f("f1", 0, 8, S + 3), f("f3", 0, 8, S)
            B.run(ve.memset(ones_row, 1.0))
            B.run(ve.memset(conv_in[:, :, 0:3], 0.0))
            eng.wait_ge(sems["gates_turned"], 1)
            B.run(ve.tensor_copy(rows[:, 1, :], aux[0:4, 2, 0:S]))
            B.run(ve.tensor_tensor_scan(cum, ones_row, rows[:, 1, :], 0.0, ALU.mult, ALU.add))
            B.run(tt(rows[:, 0, :], aux[0:4, 1, 0:S], cum, ALU.subtract))
            B.run(ve.tensor_tensor_scan(rows[:, 1, :], rows[:, 0, :], rows[:, 0, :], 0.0, ALU.max, ALU.max))
            B.post(tt(rows[:, 2, :], cum, rows[:, 1, :], ALU.add), "rows_ready")

            def conv(c):
                for k in range(KT // 4 * c, KT // 4 * (c + 1)):
                    o = conv_out[:, k, :]
                    B.run(ts(o, conv_in[:, k, 0:S], V("conv_w", k), ALU.mult, V("conv_b", k), ALU.add))
                    for q in range(1, 4):
                        ins = stt(o, conv_in[:, k, q:q + S], V("conv_w", 8 * q + k), o, ALU.mult, ALU.add)
                        if q < 3 or k < KT - 1:
                            B.run(ins)
                return ins

            b = arrive("qk0")
            freed(tt(conv_in[:, 0:2, 3:S + 3], proj[:, b:b + 2, 0:S], bc(rms, 2), ALU.mult))
            a_cols = small[:, 54:62]
            eng.wait_ge(sems["a_turned"], 1)
            B.post(ve.tensor_copy(a_cols, aux[:, 0, 0:8]), "a_cols_ready")
            for c in range(1, 4):
                b = arrive(f"qk{c}")
                freed(tt(conv_in[:, 2 * c:2 * c + 2, 3:S + 3], proj[:, b:b + 2, 0:S], bc(rms, 2), ALU.mult))
            ov = f("f5", 0, 2, D)
            for c in range(4):
                ins = conv(c)
                if c == 3:
                    B.post(ins, "conv_ready")
                per_token(f"ov{c}", lambda j: ov[:, j, c * 256:(c + 1) * 256])
            eng.wait_ge(sems["conv_tanh"], 1)
            B.post(stt(conv_out, f("f2", 0, 8, S), 1.0, conv_out, ALU.add, ALU.mult), "conv_done")
            ow, osd, em, r_h = f("f6", 0, 384), f("f6", 384, 384), f("f6", 768, S), f("f6", 1024, S)
            oh, og = f("f1", 0, 8, S), f("f4", 0, 8, S)
            for h in range(4):
                eng.wait_ge(sems["o_scores"], h + 1)
                B.run(ts(ow[:, 0:S], aux[:, 1, 0:S], a_cols[:, h:h + 1], ALU.subtract, 0.0, ALU.max))
                B.post(ts(ow[:, S:384], aux[:, 1, P:S], a_cols[:, 4 + h:5 + h], ALU.subtract, 0.0, ALU.max), "ow_arg")
                pump(index[f"og{h}"])
                eng.wait_ge(sems["ow_exp"], h + 1)
                B.run(stt(osd, aux[:, 0, 0:384], 0.25 * 128.0 ** -0.5, ow, ALU.mult, ALU.mult))
                B.post(tt(osd, osd, LC("mask_causal"), ALU.mult), "osd_ready")
                b = arrive(f"og{h}")
                freed(tt(og[:, 2 * h:2 * h + 2, :], proj[:, b:b + 2, 0:S], bc(rms, 2), ALU.mult))
                eng.wait_ge(sems["em_ready"], h + 1)
                eng.wait_ge(sems["o_den"], h + 1)
                B.run(stt(r_h, aux[:, 2, 0:S], -1.0, em, ALU.mult, ALU.max))
                B.run(tt(r_h, aux[:, 2, 0:S], r_h, ALU.max))
                B.run(ve.reciprocal(r_h, r_h))
                eng.wait_ge(sems["o_num"], h + 1)
                B.post(tt(oh[:, 2 * h:2 * h + 2, :], aux[:, 3, :].rearrange("p (a t) -> p a t", a=2), bc(r_h, 2), ALU.mult), "oh_ready")
            eng.wait_ge(sems["oh_root"], 1)
            rt = f("f2", 0, 4, S)
            B.run(ve.reciprocal(rt, rt))
            for k in range(KT):
                B.run(stt(oh[:, k, :], oh[:, k, :], V("on", k), rt[:, k // 2, :], ALU.mult, ALU.mult))
            eng.wait_ge(sems["gate_tanh"], 16)
            B.post(stt(oh, og, 1.0, oh, ALU.add, ALU.mult), "y_odd_val")
            eng.wait_ge(sems["y_odd_hi"], 1)
            B.post(stt(v[:, 1, :, :], oh, 0.5, hi32(v[:, 0, :, :]), ALU.mult, ALU.subtract), "y_odd_ready")
            add_blocks("oo")
            norm("mlp2", 8, 6, 40)
            hidden_layer(M1)
            for b in range(2):
                eng.wait_ge(sems["out_turned"], b + 1)
                B.post(ve.tensor_copy(f("f1", b * D, D), proj[:, 2 * b:2 * b + 2, :].rearrange("p a n -> p (a n)")), "out_ready")


def host_constants():
    import numpy as np

    def rope(half, rows):
        inv = np.float32(10000.0) ** (-np.arange(half, dtype=np.float32) / np.float32(half))
        ang = np.arange(L, dtype=np.float32)[None, :] * inv[rows % half][:, None]
        return np.cos(ang), np.sin(ang)

    def rotation(size, starts, half):
        m = np.zeros((P, size), np.float32)
        for s in starts:
            for j in range(half):
                m[s + half + j, s + j] = -1.0
                m[s + j, s + half + j] = 1.0
        return m

    p = np.arange(P)
    one = np.ones((P, P), np.float32)
    cr, sr = rope(32, p)
    cm, sm = rope(16, p[:32])
    cos_m, sin_m = np.ones((P, L), np.float32), np.zeros((P, L), np.float32)
    cos_m[64:96], sin_m[64:96] = cm, sm
    half_block = (p[:, None] // 64 == p[None, :] // 64).astype(np.float32)
    rel = np.stack([META + np.arange(S)[None, :] - (p[:, None] + t) for t, _ in KEY_BLOCKS], 1)
    parts = {"ident": np.eye(P), "ones": one, "ones_half": half_block, "neg_tri": -np.tril(one), "neg_ones": -one,
             "rot_ret": rotation(P, (0, 64), 32), "rot_mla": rotation(96, (64,), 16), "cos_ret": cr, "sin_ret": sr,
             "cos_mla": cos_m, "sin_mla": sin_m, "rel": rel.reshape(P, 3 * S)}
    consts = np.concatenate([np.asarray(parts[k], np.float32) for k in CONST_COLS], 1)
    t = np.concatenate([np.arange(S), np.arange(P)])[None, :]
    pick = np.zeros((P, 4, P), np.float32)
    for h in range(4):
        pick[h, h] = 1.0
    lates = {"mask_strict": p[:, None] < t, "mask_causal": p[:, None] <= t, "pick_head": pick.reshape(P, 512)}
    late = np.concatenate([np.asarray(lates[k], np.float32) for k in LATE_COLS], 1)
    return np.ascontiguousarray(consts), np.ascontiguousarray(late)


def packed_vectors(a):
    import numpy as np

    def col(x):
        return np.reshape(x, (-1, P)).T

    def rows(x):
        return np.broadcast_to(np.reshape(x, (1, -1)), (P, np.size(x)))

    parts = {"norm_mix": col(a["norm_mix_w"]), "gn": col(a["ret_gn_w"]), "q_norm": col(a["mla_q_norm_w"]),
             "kv_norm": col(a["mla_kv_norm_w"]), "ffn": col(a["norm_ffn_w"]), "final": col(a["norm_final_w"]),
             "mix2": col(a["mix_norm_g_2"]), "mlp2": col(a["mlp_norm_g_2"]), "conv_w": col(a["od_conv_w_2"]),
             "conv_b": col(a["od_conv_b_2"]), "on": col(a["od_out_norm_g_2"]),
             "sb_q": col(np.tile(np.ravel(a["sb_q_norm_g_2"]), 2)), "sb_k": col(np.tile(np.ravel(a["sb_k_norm_g_2"]), 2)),
             "sg_b": col(a["sg_b_2"]), "decay_f": rows(a["ret_decay_fwd"]), "decay_b": rows(a["ret_decay_bwd"]),
             "i_b": rows(a["od_i_b_2"]), "f_b": rows(a["od_f_b_2"])}
    params = np.ascontiguousarray(np.concatenate([parts[k] for k in PAR_COLS], 1))
    ln_gb = np.ascontiguousarray(np.stack([rows(a["sg_ln_g_2"]), rows(a["sg_ln_b_2"])], 1))
    return params, ln_gb


_WHOLE = ["x", "meta_tokens", "w_in", "w_ret_out", "w_uq", "w_uk", "w_uv", "w_mla_out", "w_o", "w_ffn_gate", "w_ffn_up",
          "w_ffn_down", "mlp_w1_2", "mlp_w2_2", "ev_w_in_2", "ev_w_out_2", "sg_w_2", "od_w_in_2", "od_w_out_2"]


def kernel(**inputs):
    import numpy as _np
    import concourse.bacc as _bacc
    from concourse import mybir as _mybir
    from concourse.bass_utils import run_bass_kernel_spmd as _run

    nc = _bacc.Bacc("TRN2", target_bir_lowering=False, num_devices=1)
    host = {k: _np.asarray(v) for k, v in inputs.items()}
    arrays, w = {}, {}

    def give(name, a):
        a = _np.ascontiguousarray(a)
        arrays[f"in_{name}_dram"] = a
        return nc.dram_tensor(f"in_{name}_dram", a.shape, _mybir.dt.from_np(a.dtype), kind="ExternalInput").ap()

    for name in _WHOLE:
        w[name] = give(name, host[name])
    params, ln_gb = packed_vectors(host)
    consts, late = host_constants()
    extra = [give(n, a) for n, a in (("params", params), ("consts", consts), ("late", late), ("ln_gb", ln_gb))]
    out = nc.dram_tensor("out_0_dram", (1, S, D), _mybir.dt.float32, kind="ExternalOutput").ap()
    build(nc, w, *extra, out)
    r = _run(nc, [arrays], core_ids=[0])
    return r.results[0]["out_0_dram"]
```

```python
from contextlib import ExitStack

import concourse.bass as bass
from concourse import mybir

F32 = mybir.dt.float32
F32R = mybir.dt.float32r
ALU = mybir.AluOpType
ACT = mybir.ActivationFunctionType
AX_X = mybir.AxisListType.X

P = 128
D = 1024
KT = D // P
S = 256
META = 16
L = S + META
HEADS = 8
D_FF, D_MLP = 2816, 4096
W_CHUNK = 2048
RING = 4
AHEAD = 3
EPS, GN_EPS = 1e-6, 1e-5
KEY_BLOCKS = [(0, 128), (128, 128), (256, 16)]

CONST_COLS = {}
_at = 0
for _name, _w in (("ident", 128), ("ones", 128), ("pick16", 30), ("neg_tri", 128), ("neg_ones", 128),
                  ("rot_ret", 128), ("rot_mla", 96), ("cos_ret", L), ("sin_ret", L), ("cos_mla", L),
                  ("sin_mla", L), ("rel", 3 * S), ("pick8", 16)):
    CONST_COLS[_name] = (_at, _w)
    _at += _w
N_CONST = _at
LATE_COLS = {}
_at = 0
for _name, _w in (("mask_strict", 384), ("mask_causal", 384), ("pick_head", 512)):
    LATE_COLS[_name] = (_at, _w)
    _at += _w
N_LATE = _at

PAR_COLS = {}
_at = 0
for _name, _w in (("norm_mix", 8), ("gn", 8), ("q_norm", 3), ("kv_norm", 2), ("ffn", 8), ("final", 8),
                  ("mix2", 16), ("mlp2", 16), ("conv_w", 32), ("conv_b", 8), ("on", 8), ("sb_q", 1),
                  ("sb_k", 1), ("sg_b", 8), ("decay_f", 8), ("decay_b", 8), ("i_b", 4), ("f_b", 4)):
    PAR_COLS[_name] = (_at, _w)
    _at += _w
N_PAR = _at

REGION = {"f1": 3200, "f2": 2176, "f3": 2112, "f4": 2112, "f5": 2048, "f6": 2304}


class Lane:

    def __init__(self, engine, sems, step):
        self.engine, self.sems, self.step = engine, sems, step
        self.base, self.here, self.i, self.per = {}, {}, None, {}

    def value(self, name):
        v = self.base.get(name, 0) + self.here.get(name, 0)
        return v if self.i is None or not self.per.get(name) else self.i * self.per[name] + v

    def post(self, ins, name):
        ins.then_inc(self.sems[name], 1)
        self.here[name] = self.here.get(name, 0) + 1
        self.engine.wait_ge(self.sems[name], self.value(name))

    def run(self, ins):
        self.post(ins, self.step)

    def enter(self, i, per):
        self.flush()
        self.i, self.per = i, per

    def leave(self, turns):
        assert self.here == {k: v for k, v in self.per.items() if v}, (self.here, self.per)
        for k, v in self.per.items():
            self.base[k] = self.base.get(k, 0) + v * turns
        self.here, self.i, self.per = {}, None, {}

    def flush(self):
        for k, v in self.here.items():
            self.base[k] = self.base.get(k, 0) + v
        self.here = {}


class Sems(dict):
    def __init__(self, make):
        super().__init__()
        self.make = make

    def __missing__(self, name):
        self[name] = self.make(name)
        return self[name]


def at(f, n, i):
    return f(n) if i is None else i * (f(n + RING) - f(n)) + f(n)


def plan_chunks(w):
    chunks, index = [], {}

    def add(name, *parts):
        index[name] = len(chunks)
        chunks.append(parts)

    def cols(ap, c0, width, kt=KT):
        v = ap.rearrange("(k p) n -> p k n", p=P)
        return (lambda m: v[:, :, c0:c0 + width]), kt, width

    def stripe(name, ap, c0, n, width=256, kt=KT):
        for j in range(n):
            add(f"{name}{j}", cols(ap, c0 + j * width, width, kt))

    w_in = w["w_in"][0]
    stripe("rq", w_in, 0, 2)
    stripe("rk", w_in, 512, 2)
    stripe("rv", w_in, 1024, 4)
    add("c0", cols(w_in, 3072, 256))
    add("c1", cols(w_in, 3328, 256))
    add("c2", cols(w_in, 3584, 160))
    stripe("rg", w_in, 2048, 4)
    stripe("gm", w_in, 4768, 4)
    stripe("uq", w["w_uq"][0], 0, 2, 384, 3)
    add("ukv", cols(w["w_uk"][0], 0, 512, 2), cols(w["w_uv"][0], 0, 512, 2))
    stripe("gr", w_in, 3744, 4)
    stripe("ro", w["w_ret_out"][0], 0, 4)
    stripe("mo", w["w_mla_out"][0], 0, 2, 512, 4)
    stripe("wo", w["w_o"][0], 0, 4)

    def hidden_stream(tag, n, up, down):
        for k in range(n):
            add(f"{tag}A{k}", *up(k))
            if k >= 1:
                add(f"{tag}B{k - 1}", *down(k - 1))
        add(f"{tag}B{n - 1}", *down(n - 1))

    def up_cols(ap, width):
        v = ap.rearrange("(k p) n -> p k n", p=P)
        return lambda k: ((lambda c: v[:, :, bass.ds(c * width, width)]), KT, width, k)

    def down_rows(ap, kt):
        v = ap.rearrange("(b k p) n -> b p k n", p=P, k=kt)
        return lambda k: ((lambda c: v[bass.ds(c, 1)].rearrange("b p k n -> (b p) k n")), kt, D, k)

    gate, upp = up_cols(w["w_ffn_gate"][0], 128), up_cols(w["w_ffn_up"][0], 128)
    half = w["w_ffn_down"][0]
    ffn_down = down_rows(half, 1)
    hidden_stream("ffn", D_FF // P, lambda k: (gate(k), upp(k)), lambda k: (ffn_down(k),))

    ev = w["ev_w_in_2"][0]
    stripe("sq", ev, 1024, 2)
    stripe("sk", ev, 1536, 2)
    stripe("za", ev, 0, 4)
    stripe("sv", ev, 2048, 2)
    stripe("eo", w["ev_w_out_2"][0], 0, 4)
    m1, m2 = up_cols(w["mlp_w1_2"][0], 256), down_rows(w["mlp_w2_2"][0], 2)
    hidden_stream("m0", D_MLP // 256, lambda k: (m1(k),), lambda k: (m2(k),))
    od = w["od_w_in_2"][0]
    add("gates", cols(od, 3072, 8))
    stripe("qk", od, 0, 4)
    stripe("ov", od, 1024, 4)
    stripe("og", od, 2048, 4)
    stripe("oo", w["od_w_out_2"][0], 0, 4)
    n1, n2 = up_cols(w["mlp_w1_2"][1], 256), down_rows(w["mlp_w2_2"][1], 2)
    hidden_stream("m1", D_MLP // 256, lambda k: (n1(k),), lambda k: (n2(k),))
    return chunks, index


def build(nc, w, params, consts, late, ln_gb, out):
    chunks, index = plan_chunks(w)
    in_halves = index[f"ffnB{D_FF // P - 1}"]
    landed, total = [], [0] * RING
    for n, parts in enumerate(chunks):
        total[n % RING] += 32 if n == in_halves else 16 * len(parts)
        landed.append(total[n % RING])

    def width_of(n):
        return sum(p[1] * p[2] for p in chunks[n])

    with ExitStack() as ctx:
        def sb(name, shape, dt=F32):
            return ctx.enter_context(nc.sbuf_tensor(name, shape, dt))

        sems = Sems(lambda name: ctx.enter_context(nc.semaphore(name)))

        raw = sb("raw", [P, RING, W_CHUNK])
        whi = sb("whi", [P, RING, W_CHUNK], F32R)
        wlo = sb("wlo", [P, RING, W_CHUNK], F32R)
        x_all = sb("x_all", [P, KT, L])
        x2 = x_all[:, :, META:L]
        u = sb("u", [P, 2, KT, L], F32R)
        v = sb("v", [P, 2, KT, S], F32R)
        cst = sb("cst", [P, N_CONST])
        par = sb("par", [P, N_PAR])
        r_all = sb("r_all", [P, 3, L])
        kr = sb("kr", [P, L])
        small = sb("small", [P, 72])
        reg = {k: sb(k, [P, n]) for k, n in REGION.items()}
        proj = ctx.enter_context(nc.psum_tensor("proj", [P, 4, 512], F32))
        aux = ctx.enter_context(nc.psum_tensor("aux", [P, 4, 512], F32))

        def C(name):
            a, n = CONST_COLS[name]
            return cst[:, a:a + n]

        def V(name, j=0):
            a, _ = PAR_COLS[name]
            return par[:, a + j:a + j + 1]

        late_at = CONST_COLS["rot_ret"][0]

        def LC(name):
            a, n = LATE_COLS[name]
            return cst[:, late_at + a:late_at + a + n]

        def f(name, a, *dims):
            n = 1
            for d in dims:
                n *= d
            ap = reg[name][:, a:a + n]
            if len(dims) == 1:
                return ap
            if len(dims) == 2:
                return ap.rearrange("p (a b) -> p a b", a=dims[0])
            return ap.rearrange("p (a b c) -> p a b c", a=dims[0], b=dims[1])

        def W(part, n, off, kt, cols):
            t = (whi, wlo)[part]
            return t[:, n % RING, off:off + kt * cols].rearrange("p (k n) -> p k n", k=kt)

        def bc(ap, n):
            return ap[:, None, :].to_broadcast([ap.shape[0], n, ap.shape[1]])

        eps, gn_eps, one = small[:, 0:1], small[:, 1:2], small[:, 2:3]
        lgf, lgb = small[:, 4:12], small[:, 12:20]
        mx, nb, sums, rs = small[:, 20:22], small[:, 22:24], small[:, 24:26], small[:, 26:28]
        r_tok = small[:, 28:30]
        qg8 = small[:, 30:31]
        gat = small[:, 32:48]
        stat = small[:, 48:54]
        both_gains = small[:, 64:72]

        x_tok = f("f1", 0, 3, D)
        sq = f("f2", 0, KT, L)
        preq, prek = f("f4", 0, 4, S), f("f4", 4 * S, 4, L)
        q_ret, k_ret = f("f3", 0, 4, S), f("f3", 4 * S, 4, L)
        rv_feat = f("f2", 0, 8, L)
        rv_tok = f("f1", 0, 3, D)
        low = f("f5", 0, 3 * S + 2 * L + L)
        acq, ackv, akr = f("f5", 0, 3, S), f("f5", 3 * S, 2, L), f("f5", 3 * S + 2 * L, L)
        low_sq = f("f4", 800, 3 * S + 2 * L)
        dec = f("f6", 0, 3, S)
        sd = f("f6", 3 * S, 2, 3, S)
        rows16 = f("f6", 2048, S)[0:16]
        o_ret = f("f2", 0, 8, S)
        d_sq = f("f1", 0, 8, S)
        rg = f("f4", 0, 8, S)
        th_m = f("f5", 0, 8, S)
        q_all, q_pre = f("f1", 0, 8, S), f("f3", 0, 8, S)
        k_all = f("f2", 0, 8, L)
        v_feat = f("f1", 2048, 4, L)
        v_tok = f("f6", 0, 3, 512)
        prob = f("f1", 2048, 2, 2, L)
        pt = f("f6", 1536, 3, S)
        rows8 = f("f6", 0, S)[0:8]
        yr = f("f3", 0, 8, S)

        def o_mla(a):
            return C("rel")[:, a * S:(a + 1) * S] if a < 3 else kr[:, 0:S]

        block = ctx.enter_context(nc.Block())

        FFN = dict(tag="ffn", n=D_FF // P, kt=1, k0=0)
        M0 = dict(tag="m0", n=D_MLP // 256, kt=2, k0=D_FF // P)
        M1 = dict(tag="m1", n=D_MLP // 256, kt=2, k0=D_FF // P + D_MLP // 256)
        loop_first = {d["tag"]: index[d["tag"] + "A0"] for d in (FFN, M0, M1)}
        loop_last = [index[f"{d['tag']}B{d['n'] - 1}"] for d in (FFN, M0, M1)]
        in_loop = set()
        for d in (FFN, M0, M1):
            in_loop |= set(range(loop_first[d["tag"]], loop_first[d["tag"]] + 2 * d["n"]))
        turns_of_banks = []
        for n in range(len(chunks)):
            if n not in in_loop:
                turns_of_banks.append(n)
                turns_of_banks += ["mixed", "ya_turn"] if n == index["sv1"] else ["low_norm"] if n == index["rg0"] else []
        order = {n: j for j, n in enumerate(turns_of_banks)}

        def ckv_split(a, k):
            flat = v[:, a, 3:8, :].rearrange("p k t -> p (k t)")
            return flat[:, k * L:(k + 1) * L]

        @block.sync
        def _(sp):
            def load(n, i=None):
                if n >= RING:
                    sp.wait_ge(sems["lo_ready"], at(lambda m: m - RING + 1, n, i))
                off = 0
                for part in chunks[n]:
                    src, kt, width = part[:3]
                    c = None if len(part) < 4 else (part[3] if i is None else i * 2 + part[3])
                    dst = raw[:, n % RING, off:off + kt * width].rearrange("p (k n) -> p k n", k=kt)
                    for rows in ((0, P),) if n != in_halves else ((0, P // 2), (P // 2, P)):
                        rows = slice(*rows)
                        sp.dma_start(dst[rows], src(c)[rows]).then_inc(sems[f"raw_landed{n % RING}"], 16)
                    off += kt * width

            x, meta = w["x"][0], w["meta_tokens"]
            sp.dma_start(cst[:, 0:P], consts[:, 0:P]).then_inc(sems["ident_in"], 16)
            sp.dma_start(x_tok[0:META, 0, :], meta).then_inc(sems["x_in"], 16)
            sp.dma_start(x_tok[META:P, 0, :], x[0:P - META, :]).then_inc(sems["x_in"], 16)
            sp.dma_start(x_tok[:, 1, :], x[P - META:2 * P - META, :]).then_inc(sems["x_in"], 16)
            sp.dma_start(x_tok[0:META, 2, :], x[S - META:S, :]).then_inc(sems["x_in"], 16)
            sp.dma_start(par[:, :], params).then_inc(sems["par_in"], 16)
            load(0)
            load(1)
            sp.dma_start(cst[:, P:N_CONST], consts[:, P:N_CONST]).then_inc(sems["const_in"], 16)

            def stream(d):
                g = loop_first[d["tag"]]
                for n in range(g, g + 3):
                    load(n)
                turns = (d["n"] - 2) // 2
                with sp.Fori(0, turns) as i:
                    for j in range(4):
                        load(g + 3 + j, i)
                load(g + 2 * d["n"] - 1)

            n = 2
            for d, tag in ((FFN, "ffn"), (M0, "m0"), (M1, "m1")):
                while n < loop_first[tag]:
                    load(n)
                    n += 1
                if tag == "ffn":
                    sp.wait_ge(sems["q_mla_roped"], 1)
                    sp.dma_start(cst[:, late_at:late_at + N_LATE], late).then_inc(sems["late_in"], 16)
                stream(d)
                n += 2 * d["n"]
                if tag == "ffn":
                    sp.wait_ge(sems["merged"], 1)
                    sp.dma_start(f("f6", 0, 8, P), w["sg_w_2"][0].rearrange("g t s -> t g s")).then_inc(sems["sg_in"], 16)
                    sp.dma_start(f("f6", 1024, 2, 512), ln_gb).then_inc(sems["sg_in"], 16)
            for j in range(4):
                c, b = j // 2 * 512, j % 2
                sp.wait_ge(sems["out_ready"], j + 1)
                sp.dma_start(out[0, b * P:(b + 1) * P, c:c + 512], f("f4", 512 * j, 512)).then_inc(sems["stored"], 16)
            sp.wait_ge(sems["stored"], 64)

        @block.tensor
        def _(pe):
            mm = nc.tensor.matmul

            def split_mm(o, w_of, x_of, kt, first=True, last=True, skip=False, gate=None):
                ins = None
                for k in range(kt):
                    if gate:
                        gate(k)
                    for j, (a, b) in enumerate(((0, 0), (0, 1), (1, 0))):
                        ins = mm(o, w_of(a, k), x_of(b, k), start=first and k == 0 and j == 0,
                                 stop=last and k == kt - 1 and j == 2, skip_group_check=skip)
                return ins

            def read_out(name):
                pe.wait_ge(sems["proj_free"], order[index.get(name, name)] + 1)

            def begin(n):
                if not isinstance(n, str):
                    pe.wait_ge(sems["lo_ready"], n + 1)
                m = order[n]
                if m >= 2:
                    pe.wait_ge(sems["proj_free"], m - 1)
                return m, 2 * (m % 2)

            def finish(ins):
                ins.then_inc(sems["chunk_used"], 1)

            def by_pair(norm_no, **sums):
                def gate(k):
                    if k % 2 == 0:
                        if norm_no and k:
                            square_pair(k // 2 - 1, norm_no, **sums)
                        if norm_no and k == 6:
                            square_pair(3, norm_no, **sums)
                        pe.wait_ge(sems["u_ready"], 4 * norm_no + k // 2 + 1)
                return gate

            def project(name, blocks=2, src=u, t0=0, t=L, kt=KT, width=256, m=P, step=P, off=0, gate=None, between=None):
                n = index[name]
                _, b = begin(n)
                for j in range(blocks):
                    ins = split_mm(proj[0:m, b + j, 0:t],
                                   lambda a, k: W(a, n, off, kt, width)[:, k, j * step:j * step + m],
                                   lambda a, k: src[:, a, k, t0:t0 + t], kt, gate=gate if j == 0 else None)
                    if between and j == 0:
                        between()
                finish(ins)

            def project_tokens(name, width=256, gate=None):
                n = index[name]
                _, b = begin(n)
                for j in range(2):
                    ins = split_mm(proj[:, b + j, 0:width],
                                   lambda a, k: u[:, a, k, META + j * P:META + (j + 1) * P],
                                   lambda a, k: W(a, n, 0, KT, width)[:, k, :], KT, gate=gate if j == 0 else None)
                finish(ins)

            def square_pair(c, norm_no, tokens=S, second=False):
                pe.wait_ge(sems["sq_ready"], 4 * norm_no + c + 1)
                for k in (2 * c, 2 * c + 1):
                    ins = mm(aux[:, 0, 0:tokens], C("ones"), sq_of(tokens)[:, k, :], start=k == 0, stop=k == KT - 1,
                             skip_group_check=True)
                if second and c:
                    for k in range(0 if c == 1 else 2 * c, 2 * c + 2):
                        ins = mm(aux[:, 1, 0:S], C("ones"), f("f3", 0, KT, S)[:, k, :], start=k == 0, stop=k == KT - 1,
                                 skip_group_check=True)
                if c == 3:
                    ins.then_inc(sems["sumsq"], 1)

            def turn_norm(norm_no):
                pe.wait_ge(sems["rms_ready"], norm_no + 1)
                for b in range(2):
                    ins = mm(aux[:, 0, b:b + 1], r_all[0:1, 0, b * P:(b + 1) * P], C("ones")[0:1, 0:1], start=True, stop=True)
                ins.then_inc(sems["r_turned"], 1)

            def sq_of(tokens):
                return sq if tokens == L else f("f2", 0, KT, S)

            pe.wait_ge(sems["ident_in"], 16)
            pe.wait_ge(sems["x_in"], 64)
            for k in range(KT):
                bank = (proj if k < 4 else aux)[:, k % 4, :]
                for b, (t, m) in enumerate(KEY_BLOCKS):
                    ins = nc.tensor.transpose(bank[:, t:t + m], x_tok[0:m, b, k * P:(k + 1) * P], C("ident")[0:m, 0:m])
                ins.then_inc(sems["x_turned"], 1)
            pe.wait_ge(sems["x_ready"], 2)
            project("rq0", t0=META, t=S, gate=by_pair(0))
            pe.wait_ge(sems["const_in"], 16)
            pe.wait_ge(sems["x_ready"], KT)
            for c in range(4):
                square_pair(c, 0, L)
            project("rq1", t0=META, t=S)
            project("rk0")
            read_out("rq1")
            pe.wait_ge(sems["rms_ready"], 1)
            for j in range(2):
                ins = mm(aux[:, j, :], C("rot_ret"), preq[:, 2 * j:2 * j + 2, :], start=True, stop=True)
            ins.then_inc(sems["q_rotated"], 1)
            project("rk1")
            project("rv0")
            read_out("rk1")
            pe.wait_ge(sems["q_roped"], 1)
            for j in range(4):
                ins = mm(aux[:, j, 0:L], C("rot_ret"), prek[:, j, :], start=True, stop=True)
            ins.then_inc(sems["k_rotated"], 1)
            for j in range(1, 4):
                project(f"rv{j}")
            pe.wait_ge(sems["k_roped"], 1)
            project("c0", t0=META, t=S)
            for b, (t, m) in enumerate(KEY_BLOCKS):
                for hh in range(2):
                    j = 2 * b + hh
                    if j == 0:
                        read_out("rv3")
                    if j >= 4:
                        pe.wait_ge(sems["rv_tok_ready"], j - 3)
                    for q in range(4):
                        ins = nc.tensor.transpose(aux[0:m, j % 4, q * P:(q + 1) * P], rv_feat[:, 4 * hh + q, t:t + m], C("ident"))
                    ins.then_inc(sems["rv_turned"], 1)
            n = index["c1"]
            _, b = begin(n)
            split_mm(proj[:, b, 0:S], lambda a, k: W(a, n, 0, KT, 256)[:, k, 0:P], lambda a, k: u[:, a, k, META:L], KT)
            finish(split_mm(proj[:, b + 1, 0:L], lambda a, k: W(a, n, 0, KT, 256)[:, k, P:2 * P], lambda a, k: u[:, a, k, :], KT))
            n2 = index["c2"]
            _, b = begin(n2)
            split_mm(proj[:, b, 0:L], lambda a, k: W(a, n2, 0, KT, 160)[:, k, 0:P], lambda a, k: u[:, a, k, :], KT)
            finish(split_mm(proj[0:96, b + 1, 0:L], lambda a, k: W(a, n2, 0, KT, 160)[:, k, 64:160], lambda a, k: u[:, a, k, :], KT))

            def ret_scores(h):
                b, p0 = 2 * (h % 2), 64 * (h % 2)
                if h >= 2:
                    pe.wait_ge(sems["o_ready"], h - 1)
                for j, (t, m) in enumerate(KEY_BLOCKS):
                    o = aux[:, b, j * S:(j + 1) * S] if j < 2 else aux[0:m, b + 1, 0:S]
                    ins = mm(o, k_ret[p0:p0 + 64, h // 2, t:t + m], q_ret[p0:p0 + 64, h // 2, :], start=True, stop=True)
                ins.then_inc(sems["ret_scores"], 1)

            def ret_values(h):
                pe.wait_ge(sems["sd_ready"], h + 1)
                for j, (t, m) in enumerate(KEY_BLOCKS):
                    ins = mm(aux[:, 2 * (h % 2) + 1, S:2 * S], rv_tok[0:m, j, h * P:(h + 1) * P], sd[0:m, h % 2, j, :],
                             start=j == 0, stop=j == 2)
                ins.then_inc(sems["ret_out"], 1)

            read_out("c2")
            pe.wait_ge(sems["rv_tok_ready"], 5)
            mm(aux[0:96, 2, 0:L], C("rot_mla")[64:96, :], akr[64:96, :], start=True, stop=True).then_inc(sems["kr_rotated"], 1)
            pe.wait_ge(sems["rv_tok_ready"], 6)
            ret_scores(0)
            for h in range(HEADS):
                def heads():
                    ret_values(h)
                    if h + 1 < HEADS:
                        if h == 0:
                            pe.wait_ge(sems["kr_roped"], 1)
                        ret_scores(h + 1)
                project(f"rg{h}" if h < 4 else f"gm{h - 4}", t0=META, t=S, between=heads)
                if h == 0:
                    _, b = begin("low_norm")
                    pe.wait_ge(sems["low_sq_ready"], 1)
                    for j in range(3):
                        mm(proj[:, b, 0:S], C("ones"), low_sq[:, j * S:(j + 1) * S], start=j == 0, stop=j == 2)
                    for j in range(2):
                        ins = mm(proj[:, b + 1, 0:L], C("ones"), low_sq[:, 3 * S + j * L:3 * S + (j + 1) * L], start=j == 0, stop=j == 1)
                    ins.then_inc(sems["low_sumsq"], 1)
            pe.wait_ge(sems["o_ready"], 8)
            for j in range(4):
                ins = mm(aux[:, j, :], C("ones"), o_ret[:, 2 * j:2 * j + 2, :], start=True, stop=True)
            ins.then_inc(sems["gn_sum"], 1)

            def query_chunk(j):
                n = index[f"uq{j}"]
                _, b = begin(n)
                for q in range(4):
                    ins = split_mm(proj[0:96, b + q // 2, (q % 2) * S:(q % 2 + 1) * S],
                                   lambda a, k: W(a, n, 0, 3, 384)[:, k, 96 * q:96 * q + 96],
                                   lambda a, k: v[:, a, k, :], 3)
                finish(ins)

            pe.wait_ge(sems["low_done"], 1)
            query_chunk(0)
            query_chunk(1)
            pe.wait_ge(sems["d_sq_ready"], 1)
            for h in range(HEADS):
                ins = mm(aux[0:8, 0, 0:S], C("pick8")[:, 7 - h:15 - h], d_sq[:, h, :], start=h == 0, stop=h == HEADS - 1)
            ins.then_inc(sems["gn_var"], 1)

            def kv_half(half):
                n = index["ukv"]
                if half == 0:
                    pe.wait_ge(sems["lo_ready"], n + 1)
                    pe.wait_ge(sems["proj_free"], order[n])
                if half >= 2:
                    pe.wait_ge(sems["kv_half"], half - 1)
                b = 2 * (half % 2)
                for j in range(2):
                    c = 2 * (half % 2) + j
                    ins = split_mm(proj[:, b + j, 0:L],
                                   lambda a, k: W(a, n, 1024 * (half // 2), 2, 512)[:, k, c * P:(c + 1) * P],
                                   lambda a, k: ckv_split(a, k), 2)
                if half < 3:
                    ins.then_inc(sems["kv_mm"], 1)
                else:
                    finish(ins)

            kv_half(0)
            kv_half(1)
            read_out("uq1")
            pe.wait_ge(sems["gn_root"], 1)
            for j in range(4):
                ins = mm(aux[0:96, j, :], C("rot_mla")[0:96, :], q_pre[0:96, 2 * j:2 * j + 2, :], start=True, stop=True)
                if j % 2:
                    ins.then_inc(sems["q_mla_rotated"], 1)
            kv_half(2)
            kv_half(3)
            pe.wait_ge(sems["gn_factor"], 1)
            for h in range(HEADS):
                if h % 4 == 0:
                    pe.wait_ge(sems["q_sin"], h // 4 + 1)
                ins = mm(aux[:, h // 2, (h % 2) * S:(h % 2 + 1) * S], C("ident")[0:8, h:h + 1].to_broadcast([8, P]), rows8,
                         start=True, stop=True)
                if h % 4 == 3:
                    ins.then_inc(sems["gn_spread"], 1)
            pe.wait_ge(sems["y_ret_val"], 1)
            for b, (t, m) in enumerate(KEY_BLOCKS):
                for q in range(4):
                    ins = nc.tensor.transpose(aux[0:m, b, q * P:(q + 1) * P], v_feat[:, q, t:t + m], C("ident"))
            ins.then_inc(sems["v_turned"], 1)
            pe.wait_ge(sems["v_tok_ready"], 1)
            pe.wait_ge(sems["q_mla_roped"], 1)
            pe.wait_ge(sems["kr_copied"], 1)

            def mla_scores(h):
                if h:
                    pe.wait_ge(sems["mla_exp"], h)
                for b in range(2):
                    ins = mm(aux[:, b, 0:L], q_all[0:96, h, b * P:(b + 1) * P], k_all[0:96, h, :], start=True, stop=True)
                ins.then_inc(sems["mla_scores"], 1)

            def mla_turn(h):
                pe.wait_ge(sems["prob_ready"], h + 1)
                if h:
                    pe.wait_ge(sems["o_mla_ready"], h)
                for j, (t, m) in enumerate(KEY_BLOCKS):
                    for b in range(2):
                        o = aux[:, 2, j * S + b * P:j * S + (b + 1) * P] if j < 2 else aux[0:m, 3, b * P:(b + 1) * P]
                        ins = nc.tensor.transpose(o, prob[:, h % 2, b, t:t + m], C("ident"))
                ins.then_inc(sems["prob_turned"], 1)

            def mla_values(h):
                pe.wait_ge(sems["pt_ready"], h + 1)
                p0 = 64 * (h % 2)
                for j, (t, m) in enumerate(KEY_BLOCKS):
                    ins = mm(aux[p0:p0 + 64, 3, S:2 * S], v_tok[0:m, j, 64 * h:64 * h + 64], pt[0:m, j, :],
                             start=j == 0, stop=j == 2)
                ins.then_inc(sems["mla_out"], 1)

            mla_scores(0)
            for h in range(HEADS):
                mla_turn(h)
                if h + 1 < HEADS:
                    mla_scores(h + 1)
                if h < 4:
                    project(f"gr{h}", t0=META, t=S, between=lambda: mla_values(h))
                else:
                    if h == 4:
                        pe.wait_ge(sems["y_ret_ready"], 1)
                    project(f"ro{h - 4}", src=v, t=S, between=lambda: mla_values(h))
            pe.wait_ge(sems["y_mla_ready"], 4)
            for c in range(2):
                n = index[f"mo{c}"]
                _, b = begin(n)
                for j in range(4):
                    ins = split_mm(proj[:, b + j // 2, (j % 2) * S:(j % 2 + 1) * S],
                                   lambda a, k: W(a, n, 0, 4, 512)[:, k, j * P:(j + 1) * P],
                                   lambda a, k: u[:, a, k, META:L], 4)
                finish(ins)
            def project_late(names, cut, ready, per=2):
                for k0, k1 in ((0, cut), (cut, KT)):
                    for name in names:
                        n = index[name]
                        b = begin(n)[1] if k0 == 0 else 2 * (order[n] % 2)
                        for j in range(2):
                            for k in range(k0, k1, 2):
                                if name == names[0] and j == 0:
                                    pe.wait_ge(sems[ready], k // per + 1)
                                ins = split_mm(proj[:, b + j, 0:S],
                                               lambda a, q: W(a, n, 0, KT, 256)[:, k + q, j * P:(j + 1) * P],
                                               lambda a, q: v[:, a, k + q, :], 2, first=k == 0, last=k == 6, skip=True)
                        if k1 == KT:
                            finish(ins)

            project_late(["wo0"], 4, "merged_ready")
            for c in range(1, 4):
                project(f"wo{c}", src=v, t=S)

            def hidden_layer(d, norm_no):
                tag, n_h, kt, k0 = d["tag"], d["n"], d["kt"], d["k0"]
                g = loop_first[tag]

                def up(n, k, i=None, gate=None):
                    pe.wait_ge(sems["lo_ready"], at(lambda m: m + 1, n, i))
                    if k0 + k >= 2:
                        pe.wait_ge(sems["hidden_val"], k0 + k - 1 if i is None else i * 2 + (k0 + k - 1))
                    for j in range(2):
                        first_gate = gate if j == 0 else None
                        if tag == "ffn":
                            ins = split_mm(proj[:, 2 * (k % 2) + j, 0:S], lambda a, q: W(a, n, 1024 * j, KT, P)[:, q, :],
                                           lambda a, q: u[:, a, q, META:L], KT, gate=first_gate)
                        else:
                            ins = split_mm(proj[:, 2 * (k % 2) + j, 0:S], lambda a, q: W(a, n, 0, KT, 256)[:, q, j * P:(j + 1) * P],
                                           lambda a, q: u[:, a, q, META:L], KT, gate=first_gate)
                    finish(ins)

                def down(n, k, i=None, first=False, last=False):
                    pe.wait_ge(sems["lo_ready"], at(lambda m: m + 1, n, i))
                    pe.wait_ge(sems["hidden_ready"], k0 + k + 1 if i is None else i * 2 + (k0 + k + 1))
                    for q in range(kt):
                        for j in range(8):
                            ins = None
                            for s, (a, b) in enumerate(((0, 0), (0, 1), (1, 0))):
                                ins = mm(aux[:, j // 2, (j % 2) * S:(j % 2 + 1) * S],
                                         W(a, n, 0, kt, D)[:, q, j * P:(j + 1) * P], v[:, b, 2 * (k % 2) + q, :],
                                         start=first and q == 0 and s == 0 and j % 2 == 0,
                                         stop=last and q == kt - 1 and s == 2, skip_group_check=True)
                            if last and q == kt - 1 and j in (1, 3, 5):
                                ins.then_inc(sems["down_bank"], 1)
                    finish(ins)

                pe.wait_ge(sems["proj_free"], order[g - 1] if order[g - 1] % 2 else order[g - 1] + 1)
                up(g, 0, gate=by_pair(norm_no))
                pe.wait_ge(sems["proj_free"], order[g - 1] + 1)
                up(g + 1, 1)
                pe.wait_ge(sems["rms_ready"], norm_no + 1)
                down(g + 2, 0, first=True)
                with pe.Fori(0, (n_h - 2) // 2) as i:
                    up(g + 3, 2, i)
                    down(g + 4, 1, i)
                    up(g + 5, 3, i)
                    down(g + 6, 2, i)
                down(g + 2 * n_h - 1, n_h - 1, last=True)

            hidden_layer(FFN, 1)

            pe.wait_ge(sems["hidden_val"], M0["k0"])
            project("sq0", t0=META, t=S, gate=by_pair(2, second=True))
            for name in ("sq1", "sk0", "sk1"):
                project(name, t0=META, t=S)
            turn_norm(2)
            pe.wait_ge(sems["sg_in"], 32)
            for g in range(8):
                ins = nc.tensor.transpose(aux[:, 2 + g // 4, (g % 4) * P:(g % 4 + 1) * P], f("f6", 0, 8, P)[:, g, :], C("ident"))
            ins.then_inc(sems["sg_turned"], 1)
            project_tokens("za0")
            for i in range(8):
                if i % 4 == 0:
                    pe.wait_ge(sems["sb_sq_ready"], i // 4 + 1)
                if i == 0:
                    pe.wait_ge(sems["r_tok_ready"], 1)
                ins = mm(aux[0:16, 0, 0:S], C("pick16")[:, 14 - 2 * i:30 - 2 * i], f("f2", 0, 8, S)[:, i, :], start=i == 0, stop=i == 7)
            ins.then_inc(sems["sb_sumsq"], 1)
            project_tokens("za1")
            pe.wait_ge(sems["sb_factor"], 1)
            pe.wait_ge(sems["sg_t_ready"], 1)
            for i in range(8):
                ins = mm(aux[:, i // 2, (i % 2) * S:(i % 2 + 1) * S], f("f5", 0, 8, P)[0:16, i, :], rows16, start=True, stop=True)
                if i % 4 == 3:
                    ins.then_inc(sems["sb_spread"], 1)
            project_tokens("za2")

            sb_q, sb_k, sb_v = f("f3", 0, 4, S), f("f3", 1024, 4, S), f("f5", 0, 2, 512)

            def sb_scores(a):
                if a >= 2:
                    pe.wait_ge(sems["sb_arg"], a - 1)
                b = 2 * (a % 2)
                for e in range(2):
                    p0 = 64 * e
                    mm(aux[:, b + e, 0:S], sb_k[p0:p0 + 64, a, 0:P], sb_q[p0:p0 + 64, a, :], start=True, stop=True)
                    ins = mm(aux[:, b + e, S:S + P], sb_k[p0:p0 + 64, a, P:S], sb_q[p0:p0 + 64, a, P:S], start=True, stop=True)
                ins.then_inc(sems["sb_scores"], 1)

            def sb_suffix(a):
                pe.wait_ge(sems["sb_soft"], a + 1)
                b = 2 * (a % 2)
                soft = f("f1", 768 * a, 2, 384)
                for e in range(2):
                    mm(aux[:, b + e, 0:S], C("neg_tri"), soft[:, e, 0:S], start=True, stop=False, skip_group_check=True)
                    mm(aux[:, b + e, P:S], C("neg_ones"), soft[:, e, S:S + P], start=False, stop=True, skip_group_check=True)
                    ins = mm(aux[:, b + e, S:S + P], C("neg_tri"), soft[:, e, S:S + P], start=True, stop=True)
                ins.then_inc(sems["sb_suffix"], 1)

            def sb_values(a):
                if a == 0:
                    pe.wait_ge(sems["sb_arg"], 3)
                pe.wait_ge(sems["sb_attn"], a + 1)
                attn = f("f1", 768 * a, 2, 384)
                for e in range(2):
                    h = 2 * a + e
                    o = aux[64 * e:64 * e + 64, a // 2, (a % 2) * S:(a % 2 + 1) * S]
                    mm(o[:, 0:S], sb_v[:, 0, 64 * h:64 * h + 64], attn[:, e, 0:S], start=True, stop=False, skip_group_check=True)
                    ins = mm(o[:, P:S], sb_v[:, 1, 64 * h:64 * h + 64], attn[:, e, S:S + P], start=False, stop=True,
                             skip_group_check=True)
                ins.then_inc(sems["sb_out"], 1)

            pe.wait_ge(sems["sb_qk_ready"], 1)
            sb_scores(0)
            sb_scores(1)
            project_tokens("za3")
            project_tokens("sv0")
            sb_suffix(0)
            sb_suffix(1)
            sb_scores(2)
            sb_scores(3)
            project_tokens("sv1")
            _, b = begin("mixed")
            pe.wait_ge(sems["vg_ready"], 1)
            vg = f("f5", 1024, 2, 512)
            wct = f("f6", 0, 8, P)
            for g in range(8):
                ins = mm(proj[:, b + g // 4, (g % 4) * P:(g % 4 + 1) * P], wct[:, g, :],
                         vg[:, :, g * 64:(g + 1) * 64], start=True, stop=True)
            ins.then_inc(sems["mixed"], 1)
            sb_suffix(2)
            sb_suffix(3)
            _, b = begin("ya_turn")
            read_out("mixed")
            for q in range(4):
                for j in range(2):
                    ins = nc.tensor.transpose(proj[:, b + q // 2, (q % 2) * S + j * P:(q % 2) * S + (j + 1) * P],
                                              vg[:, j, q * P:(q + 1) * P], C("ident"))
            ins.then_inc(sems["ya_turned"], 1)
            for a in range(4):
                sb_values(a)
            project_late(["eo0"], 4, "y_even_ready", 4)
            for c in range(1, 4):
                project(f"eo{c}", src=v, t=S)
            hidden_layer(M0, 3)

            pe.wait_ge(sems["hidden_val"], M1["k0"])
            project_tokens("gates", 8, gate=by_pair(4))
            project("qk0", t0=META, t=S, between=lambda: turn_norm(4))
            pe.wait_ge(sems["gates_ready"], 1)
            for j in range(2):
                for b in range(2):
                    ins = nc.tensor.transpose(aux[0:4, 1 + j, b * P:(b + 1) * P], gat[:, 8 * b + 4 * j:8 * b + 4 * j + 4], C("ident"))
            ins.then_inc(sems["gates_turned"], 1)
            project("qk1", t0=META, t=S)
            rows = f("f6", 1536, 3, S)
            pe.wait_ge(sems["rows_ready"], 1)
            for b in range(2):
                ins = nc.tensor.transpose(aux[:, 0, 4 * b:4 * b + 4], rows[0:4, 0, b * P:(b + 1) * P], C("ident")[0:4, 0:4])
            ins.then_inc(sems["a_turned"], 1)
            project("qk2", t0=META, t=S)
            pe.wait_ge(sems["a_cols_ready"], 1)
            for h in range(4):
                pick = LC("pick_head")[0:4, h * P:(h + 1) * P]
                mm(aux[:, h, 0:S], pick, rows[0:4, 1, :], start=True, stop=True)
                ins = mm(aux[:, h, S:2 * S], pick, rows[0:4, 2, :], start=True, stop=True)
            ins.then_inc(sems["o_spread"], 1)
            project("qk3", t0=META, t=S)
            project_tokens("ov0")
            project_tokens("ov1")
            oqk = f("f3", 0, 8, S)
            ov = f("f5", 0, 2, D)
            osq = f("f2", 0, 8, S)

            def o_scores(h):
                if h >= 2:
                    pe.wait_ge(sems["o_mean"], h - 1)
                bank = aux[:, h % 2, :]
                mm(bank[:, 0:S], oqk[:, 4 + h, 0:P], oqk[:, h, :], start=True, stop=True)
                mm(bank[:, S:S + P], oqk[:, 4 + h, P:S], oqk[:, h, P:S], start=True, stop=True).then_inc(sems["o_scores"], 1)

            def o_values(h):
                pe.wait_ge(sems["osd_ready"], h + 1)
                if h:
                    pe.wait_ge(sems["o_max"], h)
                osd = f("f6", 1536 + 384 * (h % 2), 384)
                mm(aux[:, 2, 0:S], C("ones"), osd[:, 0:S], start=True, stop=False, skip_group_check=True)
                mm(aux[:, 2, P:S], C("ones"), osd[:, S:S + P], start=False, stop=True,
                   skip_group_check=True).then_inc(sems["o_den"], 1)
                if h:
                    pe.wait_ge(sems["o_squares"], h)
                read_out(f"ov{h}")
                for j in range(2):
                    c = 256 * h + 128 * j
                    mm(aux[:, 3, j * S:(j + 1) * S], ov[:, 0, c:c + P], osd[:, 0:S], start=True, stop=False, skip_group_check=True)
                    ins = mm(aux[:, 3, j * S + P:(j + 1) * S], ov[:, 1, c:c + P], osd[:, S:S + P], start=False, stop=True,
                             skip_group_check=True)
                ins.then_inc(sems["o_num"], 1)

            def o_sum(h):
                pe.wait_ge(sems["o_squares"], h + 1)
                for j in range(2):
                    ins = mm(aux[:, h % 2, 0:S], C("ones"), osq[:, 2 * h + j, :], start=j == 0, stop=j == 1)
                ins.then_inc(sems["o_sum"], 1)

            pe.wait_ge(sems["conv_done"], 4)
            pe.wait_ge(sems["em_ready"], 1)
            o_scores(0)
            project_tokens("ov2")
            o_values(0)
            o_scores(1)
            project_tokens("ov3")
            o_sum(0)
            o_values(1)
            o_scores(2)
            project("og0", t0=META, t=S)
            o_sum(1)
            o_values(2)
            o_scores(3)
            project("og1", t0=META, t=S)
            o_sum(2)
            o_values(3)
            project("og2", t0=META, t=S)
            o_sum(3)
            project("og3", t0=META, t=S)
            project_late(["oo0", "oo1"], 6, "y_odd_ready")
            for c in range(2, 4):
                project(f"oo{c}", src=v, t=S)
            hidden_layer(M1, 5)
            pe.wait_ge(sems["hidden_val"], M1["k0"] + M1["n"])
            for k in range(KT):
                if k % 2 == 0:
                    pe.wait_ge(sems["final_ready"], k // 2 + 1)
                for b in range(2):
                    bank = proj[:, 2 * b + k // 4, :]
                    ins = nc.tensor.transpose(bank[:, (k % 4) * P:(k % 4 + 1) * P], x2[:, k, b * P:(b + 1) * P], C("ident"))
                    if k % 4 == 3:
                        ins.then_inc(sems["out_turned"], 1)

        @block.scalar
        def _(eng):
            act = nc.scalar.activation
            A = Lane(eng, sems, "act_step")
            done = [0]

            def split(n, i=None):
                eng.wait_ge(sems[f"raw_landed{n % RING}"], at(lambda m: landed[m], n, i))
                if n >= RING:
                    eng.wait_ge(sems["chunk_used"], at(lambda m: m - RING + 1, n, i))
                wd = width_of(n)
                A.post(act(whi[:, n % RING, 0:wd], raw[:, n % RING, 0:wd], ACT.Copy), "hi_ready")

            def pump(n):
                while done[0] <= min(n + AHEAD, len(chunks) - 1):
                    split(done[0])
                    done[0] += 1

            def root(src, dst, scale, eps_ap, name):
                A.post(act(dst, src, ACT.Sqrt, bias=eps_ap, scale=scale), name)

            def read_out(name):
                eng.wait_ge(sems["proj_free"], order[index.get(name, name)] + 1)

            eng.wait_ge(sems["par_in"], 16)
            eng.wait_ge(sems["small_ready"], 1)
            for k in range(KT):
                eng.wait_ge(sems["x_ready"], k + 1)
                A.post(act(u[:, 0, k, :], x_all[:, k, :], ACT.Copy, scale=V("norm_mix", k)), "u_hi")
                if k == 3:
                    split(0)
            done[0] = 1
            for c in range(4):
                A.post(act(sq[:, 2 * c:2 * c + 2, :], x_all[:, 2 * c:2 * c + 2, :], ACT.Square), "sq_ready")
            pump(index["rq0"])
            A.post(act(small[:, 4:20], par[:, PAR_COLS["decay_f"][0]:PAR_COLS["decay_f"][0] + 16], ACT.Exp), "lg_ready")
            eng.wait_ge(sems["sumsq"], 1)
            root(aux[:, 0, 0:L], r_all[:, 0, :], 1.0 / D, eps, "root_ready")
            for name in ("rq0", "rq1", "rk0", "rk1", "rv0", "rv1", "rv2", "rv3", "c0", "c1", "c2"):
                pump(index[name])
            read_out("c2")
            A.post(act(low_sq, low[:, 0:3 * S + 2 * L], ACT.Square), "low_sq_ready")
            def decay(h):
                eng.wait_ge(sems["dec_arg"], h + 1)
                A.run(act(dec[:, 0:2, :], dec[:, 0:2, :], ACT.Exp))
                A.post(act(dec[0:META, 2, :], dec[0:META, 2, :], ACT.Exp), "dec_ready")

            def low_norm(b):
                eng.wait_ge(sems["low_sumsq"], 1)
                root(proj[:, b, 0:S], r_all[:, 1, 0:S], 1.0 / 384, eps, "root_ready")
                root(proj[:, b + 1, 0:L], r_all[:, 2, :], 1.0 / 256, eps, "root_ready")
                for j in range(3):
                    A.post(act(v[:, 0, j, :], acq[:, j, :], ACT.Copy, scale=V("q_norm", j)), "low_hi")
                for j in range(2):
                    A.post(act(ckv_split(0, j), ackv[:, j, :], ACT.Copy, scale=V("kv_norm", j)), "low_hi")

            decay(0)
            for h in range(HEADS):
                if h + 1 < HEADS:
                    decay(h + 1)
                name = f"rg{h}" if h < 4 else f"gm{h - 4}"
                pump(index[name])
                b = 2 * (order[index.get(name, name)] % 2)
                if h == 1:
                    low_norm(2 * (order["low_norm"] % 2))
                if h < 4:
                    eng.wait_ge(sems["gate_scaled"], h + 1)
                    A.post(act(proj[:, b:b + 2, 0:S], rg[:, 2 * h:2 * h + 2, :], ACT.Tanh, scale=0.5), "gate_tanh")
                else:
                    read_out(name)
                    t = th_m[:, 2 * (h - 4):2 * (h - 4) + 2, :]
                    A.post(act(t, t, ACT.Tanh, scale=0.5), "gate_tanh")
            pump(index["uq0"])
            pump(index["uq1"])
            eng.wait_ge(sems["d_ready"], 1)
            A.post(act(d_sq, o_ret, ACT.Square), "d_sq_ready")
            pump(index["ukv"])
            eng.wait_ge(sems["gn_var"], 1)
            A.post(act(rows8, aux[0:8, 0, 0:S], ACT.Sqrt, bias=gn_eps[0:8], scale=1.0 / P), "gn_root")

            eng.wait_ge(sems["v_turned"], 1)
            A.run(act(v_tok[:, 0:2, :], aux[:, 0:2, :], ACT.Copy))
            A.post(act(v_tok[0:META, 2, :], aux[0:META, 2, :], ACT.Copy), "v_tok_ready")

            def soft(h):
                eng.wait_ge(sems["neg_max"], h + 1)
                for b in range(2):
                    ins = act(prob[:, h % 2, b, :], aux[:, b, 0:L], ACT.Exp, bias=nb[:, b:b + 1], scale=96.0 ** -0.5,
                              accum_out=sums[:, b:b + 1])
                    if b == 0:
                        A.run(ins)
                A.post(ins, "mla_exp")

            soft(0)
            for h in range(HEADS):
                name = f"gr{h}" if h < 4 else f"ro{h - 4}"
                if h + 1 < HEADS:
                    soft(h + 1)
                pump(index[name])
                if h == 0:
                    eng.wait_ge(sems["chunk_used"], index["ukv"] + 1)
                    eng.wait_ge(sems["y_ret_val"], 1)
                    A.post(act(v[:, 0, :, :], rg, ACT.Copy, scale=0.5), "y_ret_hi")
                if h < 4:
                    read_out(name)
                    t = yr[:, 2 * h:2 * h + 2, :]
                    A.post(act(t, t, ACT.Tanh, scale=0.5), "gate_tanh")
                if h >= 5:
                    eng.wait_ge(sems["chunk_used"], index["gr3"] + 1)
                    for a in (0, 1) if h == 5 else (h - 4,):
                        eng.wait_ge(sems["o_mla_ready"], 2 * a + 2)
                        A.post(act(u[:, 0, a, META:L], o_mla(a), ACT.Copy), "y_mla_hi")
            pump(index["mo0"])
            pump(index["mo1"])
            for j in range(4):
                eng.wait_ge(sems["merged"], j + 1)
                A.post(act(v[:, 0, 2 * j:2 * j + 2, :], yr[:, 2 * j:2 * j + 2], ACT.Copy, scale=0.5), "merged_hi")

            def norm(source, gain, norm_no, second=False):
                for c in range(4):
                    if isinstance(source, str):
                        pump(index[f"{source}{min(c + 1, 3)}"])
                        read_out(f"{source}{c}")
                    else:
                        eng.wait_ge(sems["x_new"], 4 * source + c + 1)
                    pair = x2[:, 2 * c:2 * c + 2, :]
                    for k in (2 * c, 2 * c + 1):
                        A.post(act(u[:, 0, k, META:L], x2[:, k, :], ACT.Copy, scale=gain(k)), "u_hi")
                    ins = act(f("f2", 0, KT, S)[:, 2 * c:2 * c + 2, :], pair, ACT.Square)
                    if second:
                        A.run(ins)
                        for k in (2 * c, 2 * c + 1):
                            ins = act(f("f3", 0, KT, S)[:, k, :], x2[:, k, :], ACT.Square, scale=V("final", k))
                            if k % 2 == 0:
                                A.run(ins)
                    A.post(ins, "sq_ready")
                if not isinstance(source, str):
                    pump(loop_last[source] - 1)
                eng.wait_ge(sems["sumsq"], norm_no + 1)
                root(aux[:, 0, 0:S], r_all[:, 0, 0:S], 1.0 / D, eps, "root_ready")

            def hidden_layer(d):
                tag, n_h, k0 = d["tag"], d["n"], d["k0"]
                g = loop_first[tag]

                def step(n, k, i=None):
                    if i is not None:
                        split(n + AHEAD, i)
                    elif k != n_h - 1:
                        pump(n)
                    if k is None:
                        return
                    kk = (lambda c: k0 + k + c if i is None else i * 2 + (k0 + k + c))

                    def buffer_free():
                        if k >= 1:
                            eng.wait_ge(sems["chunk_used"], at(lambda m: m, g + 2 * k - 1, i))

                    if tag == "ffn":
                        eng.wait_ge(sems["ffn_gate_scaled"], kk(1))
                        A.post(act(proj[:, 2 * (k % 2), 0:S], f("f1", 0, S), ACT.Tanh, scale=0.5), "ffn_gate_tanh")
                        eng.wait_ge(sems["hidden_val"], kk(1))
                        buffer_free()
                        A.post(act(v[:, 0, 2 * (k % 2), :], f("f1", 256, S), ACT.Copy), "hidden_hi")
                    else:
                        eng.wait_ge(sems["hidden_val"], kk(1))
                        buffer_free()
                        A.post(act(v[:, 0, 2 * (k % 2):2 * (k % 2) + 2, :], f("f1", 512, 2, S), ACT.Copy), "hidden_hi")

                step(g, 0)
                turns = (n_h - 2) // 2
                with eng.Fori(0, turns) as i:
                    A.enter(i, {"hi_ready": 4, "hidden_hi": 2, "ffn_gate_tanh": 2 if tag == "ffn" else 0})
                    step(g + 1, 1, i)
                    step(g + 2, None, i)
                    step(g + 3, 2, i)
                    step(g + 4, None, i)
                A.leave(turns)
                done[0] += 4 * turns
                step(g + 2 * n_h - 3, n_h - 1)
                pump(g + 2 * n_h - 3)

            norm("wo", lambda k: V("ffn", k), 1)
            hidden_layer(FFN)
            norm(0, lambda k: both_gains[:, k:k + 1], 2, second=True)
            eng.wait_ge(sems["second_mean"], 1)
            A.post(act(r_all[:, 2, 0:S], r_all[:, 2, 0:S], ACT.Sqrt, bias=eps, scale=1.0 / D), "second_root")
            for j, name in enumerate(("sq", "sk")):
                pump(index[f"{name}0"])
                pump(index[f"{name}1"])
                read_out(f"{name}1")
                A.post(act(f("f2", 1024 * j, 4, S), f("f1", 1024 * j, 4, S), ACT.Square), "sb_sq_ready")
            pump(index["za0"])
            eng.wait_ge(sems["sb_sumsq"], 1)
            A.post(act(rows16, aux[0:16, 0, 0:S], ACT.Sqrt, bias=eps[0:16], scale=1.0 / 64), "sb_root")
            pump(index["za1"])
            pump(index["za2"])

            def sb_log(*pairs):
                for a in pairs:
                    zm, soft = f("f2", 768 * (a % 2), 2, 384), f("f1", 768 * a, 2, 384)
                    eng.wait_ge(sems["sb_z"], a + 1)
                    A.run(act(soft, zm, ACT.Abs))
                    A.run(act(soft, soft, ACT.Exp, scale=-1.0))
                for a in pairs:
                    soft = f("f1", 768 * a, 2, 384)
                    A.post(act(soft, soft, ACT.Ln, bias=one), "sb_log")

            def sb_exp(a):
                zm, attn = f("f2", 768 * (a % 2), 2, 384), f("f1", 768 * a, 2, 384)
                eng.wait_ge(sems["sb_arg"], a + 1)
                A.post(act(attn, zm, ACT.Exp), "sb_exp")

            za = f("f4", 0, 2, D)
            sb_log(0, 1)
            pump(index["za3"])
            read_out("za3")
            A.post(act(za, za, ACT.Gelu_apprx_tanh), "gelu_ready")
            pump(index["sv0"])
            sb_exp(0)
            sb_exp(1)
            eng.wait_ge(sems["vg_centred"], 1)
            for b in range(2):
                A.run(act(f("f2", 1536, 512), f("f5", 1024, 2, 512)[:, b, :], ACT.Square, accum_out=stat[:, 2 + b:3 + b]))
            A.post(act(stat[:, 4:6], stat[:, 2:4], ACT.Sqrt, bias=eps, scale=1.0 / 512), "vg_root")
            pump(index["sv1"])
            sb_log(2, 3)
            sb_exp(2)
            sb_exp(3)
            read_out("ya_turn")
            A.post(act(v[:, 0, 0:4, :], f("f4", 0, 4, S), ACT.Copy), "y_even_hi")
            eng.wait_ge(sems["sb_out_ready"], 2)
            A.post(act(v[:, 0, 4:8, :], f("f2", 0, 4, S), ACT.Copy), "y_even_hi")
            norm("eo", lambda k: V("mlp2", k), 3)
            hidden_layer(M0)

            norm(1, lambda k: V("mix2", 8 + k), 4)
            pump(index["gates"])
            fg = gat.rearrange("p (b c) -> p b c", b=2)[:, :, 4:8]
            ftmp = stat[:, 0:6]
            ab = f("f6", 0, 8)
            eng.wait_ge(sems["gates_raw"], 1)
            A.run(act(ab.rearrange("p (b c) -> p b c", b=2), fg, ACT.Abs))
            A.run(act(ab, ab, ACT.Exp, scale=-1.0))
            A.post(act(ab, ab, ACT.Ln, bias=one), "gates_log")
            conv_out, th = f("f3", 0, 8, S), f("f2", 0, 8, S)
            ow_all, em_all = f("f6", 0, 1536), f("f1", 2072, 4, S)
            for c in range(4):
                pump(index[f"qk{c}"] + 1)
                if c == 3:
                    eng.wait_ge(sems["ow_arg"], 1)
                    A.post(act(ow_all, ow_all, ACT.Exp, scale=-1.0), "ow_exp")
                    A.post(act(em_all, aux[:, :, S:2 * S], ACT.Exp, scale=-1.0), "em_ready")
                eng.wait_ge(sems["conv_ready"], c + 1)
                A.post(act(th[:, 2 * c:2 * c + 2, :], conv_out[:, 2 * c:2 * c + 2, :], ACT.Tanh, scale=0.5), "conv_tanh")

            def o_squares(h):
                eng.wait_ge(sems["o_num"], h + 1)
                for k in (2 * h, 2 * h + 1):
                    A.run(act(f("f1", 0, 8, S)[:, k, :], aux[:, 3, (k % 2) * S:(k % 2 + 1) * S], ACT.Copy, scale=V("on", k)))
                A.post(act(f("f2", 0, 8, S)[:, 2 * h:2 * h + 2, :], aux[:, 3, :].rearrange("p (a t) -> p a t", a=2), ACT.Square), "o_squares")

            def o_root(h):
                eng.wait_ge(sems["o_mean"], h + 1)
                A.post(act(r_all[:, 2, 0:S], r_all[:, 2, 0:S], ACT.Sqrt), "o_root")

            def o_gate(h):
                read_out(f"og{h}")
                t = f("f4", 0, 8, S)[:, 2 * h:2 * h + 2, :]
                A.post(act(t, t, ACT.Tanh, scale=0.5), "gate_tanh")

            def y_hi(h):
                eng.wait_ge(sems["y_odd_val"], h + 1)
                A.post(act(v[:, 0, 2 * h:2 * h + 2, :], f("f1", 0, 8, S)[:, 2 * h:2 * h + 2, :], ACT.Copy, scale=0.5), "y_odd_hi")

            pump(index["ov0"])
            pump(index["ov1"])
            pump(index["ov2"])
            o_squares(0)
            pump(index["ov3"])
            o_root(0)
            o_squares(1)
            pump(index["og0"])
            o_root(1)
            o_squares(2)
            pump(index["og1"])
            o_root(2)
            o_squares(3)
            pump(index["og2"])
            o_root(3)
            for h in range(3):
                o_gate(h)
            for h in range(3):
                y_hi(h)
            pump(index["og3"])
            o_gate(3)
            y_hi(3)
            norm("oo", lambda k: V("mlp2", 8 + k), 5)
            hidden_layer(M1)
            for j in range(4):
                eng.wait_ge(sems["out_turned"], j + 1)
                A.post(act(f("f4", 512 * j, 512), proj[:, 2 * (j % 2) + j // 2, :], ACT.Copy), "out_ready")

        @block.gpsimd
        def _(eng):
            G = Lane(eng, sems, "pool_step")
            gp = nc.gpsimd
            eng.wait_ge(sems["kr_roped"], 1)
            eng.wait_ge(sems["kv_half"], 1)
            G.post(gp.tensor_copy(k_all[64:96, :, :], bc(kr[64:96, :], 8)), "kr_copied")
            eng.wait_ge(sems["q_mla_rotated"], 2)
            G.post(gp.tensor_tensor(q_pre[0:96], q_pre[0:96], bc(C("cos_mla")[0:96, META:L], 8), ALU.mult), "q_cos")

        @block.vector
        def _(eng):
            ve = nc.vector
            B = Lane(eng, sems, "dve_step")
            done = [0]
            free = [0]

            def tt(o, a, b, op):
                return ve.tensor_tensor(o, a, b, op)

            def stt(o, a, s, b, op0, op1):
                return ve.scalar_tensor_tensor(out=o, in0=a, scalar=s, in1=b, op0=op0, op1=op1)

            def ts(o, a, s, op, s2=None, op2=None):
                return ve.tensor_scalar(o, a, s, s2, op) if op2 is None else ve.tensor_scalar(o, a, s, s2, op, op2)

            def split(n, i=None):
                eng.wait_ge(sems["hi_ready"], at(lambda m: m + 1, n, i))
                wd = width_of(n)
                s = n % RING
                B.post(tt(wlo[:, s, 0:wd], raw[:, s, 0:wd], whi[:, s, 0:wd].bitcast(F32), ALU.subtract), "lo_ready")

            def pump(n):
                while done[0] <= min(n + AHEAD, len(chunks) - 1):
                    split(done[0])
                    done[0] += 1

            def arrive(name, urgent=False):
                n = index[name]
                if not urgent:
                    pump(n)
                eng.wait_ge(sems["chunk_used"], n + 1)
                return 2 * (order[n] % 2)

            def freed(ins):
                B.post(ins, "proj_free")

            def hi32(ap):
                return ap.bitcast(F32)

            B.run(ve.memset(eps, EPS))
            B.run(ve.memset(gn_eps, GN_EPS))
            B.post(ve.memset(one, 1.0), "small_ready")
            for k in range(KT):
                bank = (proj if k < 4 else aux)[:, k % 4, 0:L]
                eng.wait_ge(sems["x_turned"], k + 1)
                B.post(ve.tensor_copy(x_all[:, k, :], bank), "x_ready")
            eng.wait_ge(sems["par_in"], 16)

            def lo_pair(c, gain, norm_no, x=x2, t0=META):
                for k in (2 * c, 2 * c + 1):
                    eng.wait_ge(sems["u_hi"], 8 * norm_no + k + 1)
                    ins = stt(u[:, 1, k, t0:L], x[:, k, :], gain(k), hi32(u[:, 0, k, t0:L]), ALU.mult, ALU.subtract)
                    if k % 2 == 0:
                        B.run(ins)
                B.post(ins, "u_ready")

            lo_pair(0, lambda k: V("norm_mix", k), 0, x_all, 0)
            lo_pair(1, lambda k: V("norm_mix", k), 0, x_all, 0)
            split(0)
            done[0] = 1
            lo_pair(2, lambda k: V("norm_mix", k), 0, x_all, 0)
            lo_pair(3, lambda k: V("norm_mix", k), 0, x_all, 0)
            B.run(tt(both_gains, par[:, PAR_COLS["final"][0]:PAR_COLS["final"][0] + KT],
                     par[:, PAR_COLS["mix2"][0]:PAR_COLS["mix2"][0] + KT], ALU.mult))
            eng.wait_ge(sems["lg_ready"], 1)
            B.run(ts(small[:, 4:12], small[:, 4:12], -1.0, ALU.mult))
            pump(index["rq0"])
            eng.wait_ge(sems["root_ready"], 1)
            r1 = r_all[:, 0, :]
            B.post(ve.reciprocal(r1, r1), "rms_ready")
            rq = r1[:, META:L]
            for c in range(2):
                b = arrive(f"rq{c}")
                freed(tt(preq[:, 2 * c:2 * c + 2, :], proj[:, b:b + 2, 0:S], bc(rq, 2), ALU.mult))
            b = arrive("rk0")
            freed(tt(prek[:, 0:2, :], proj[:, b:b + 2, 0:L], bc(r1, 2), ALU.mult))
            eng.wait_ge(sems["q_rotated"], 1)
            rot = aux[:, 0:2, :].rearrange("p a (b t) -> p (a b) t", b=2)
            B.run(tt(q_ret, rot, bc(C("sin_ret")[:, META:L], 4), ALU.mult))
            B.run(tt(preq, preq, bc(C("cos_ret")[:, META:L], 4), ALU.mult))
            B.post(tt(q_ret, q_ret, preq, ALU.add), "q_roped")
            b = arrive("rk1")
            freed(tt(prek[:, 2:4, :], proj[:, b:b + 2, 0:L], bc(r1, 2), ALU.mult))
            b = arrive("rv0")
            freed(tt(rv_feat[:, 0:2, :], proj[:, b:b + 2, 0:L], bc(r1, 2), ALU.mult))
            eng.wait_ge(sems["k_rotated"], 1)
            B.run(tt(k_ret, aux[:, :, 0:L], bc(C("sin_ret"), 4), ALU.mult))
            B.run(tt(prek, prek, bc(C("cos_ret"), 4), ALU.mult))
            B.post(tt(k_ret, k_ret, prek, ALU.add), "k_roped")
            for c in range(1, 4):
                b = arrive(f"rv{c}")
                freed(tt(rv_feat[:, 2 * c:2 * c + 2, :], proj[:, b:b + 2, 0:L], bc(r1, 2), ALU.mult))
            b = arrive("c0")
            freed(tt(acq[:, 0:2, :], proj[:, b:b + 2, 0:S], bc(rq, 2), ALU.mult))
            for j in range(6):
                m = KEY_BLOCKS[j // 2][1]
                eng.wait_ge(sems["rv_turned"], j + 1)
                B.post(ve.tensor_copy(rv_tok[0:m, j // 2, 512 * (j % 2):512 * (j % 2 + 1)], aux[0:m, j % 4, :]), "rv_tok_ready")
            b = arrive("c1")
            B.run(tt(acq[:, 2, :], proj[:, b, 0:S], rq, ALU.mult))
            freed(tt(ackv[:, 0, :], proj[:, b + 1, 0:L], r1, ALU.mult))
            b = arrive("c2")
            B.run(tt(ackv[:, 1, :], proj[:, b, 0:L], r1, ALU.mult))
            freed(tt(akr[64:96, :], proj[64:96, b + 1, 0:L], r1[64:96, :], ALU.mult))
            eng.wait_ge(sems["kr_rotated"], 1)
            krr = kr[64:96, :]
            B.run(tt(krr, aux[64:96, 2, 0:L], C("sin_mla")[64:96, :], ALU.mult))
            B.run(tt(akr[64:96, :], akr[64:96, :], C("cos_mla")[64:96, :], ALU.mult))
            B.post(tt(krr, krr, akr[64:96, :], ALU.add), "kr_roped")

            def low_norm():
                eng.wait_ge(sems["root_ready"], 3)
                B.run(ve.reciprocal(r_all[:, 1, 0:S], r_all[:, 1, 0:S]))
                freed(ve.reciprocal(r_all[:, 2, :], r_all[:, 2, :]))

            def low_lo():
                for j in range(3):
                    eng.wait_ge(sems["low_hi"], j + 1)
                    B.run(stt(v[:, 1, j, :], acq[:, j, :], V("q_norm", j), hi32(v[:, 0, j, :]), ALU.mult, ALU.subtract))
                for j in range(2):
                    eng.wait_ge(sems["low_hi"], j + 4)
                    ins = stt(ckv_split(1, j), ackv[:, j, :], V("kv_norm", j), hi32(ckv_split(0, j)), ALU.mult, ALU.subtract)
                    if j == 0:
                        B.run(ins)
                B.post(ins, "low_done")

            rel = C("rel").rearrange("p (a t) -> p a t", a=3)

            def decay_arg(h):
                B.run(ts(dec[:, 0:2, :], rel[:, 0:2, :], lgf[:, h:h + 1], ALU.mult))
                B.run(ts(dec[0:META, 2, :], rel[0:META, 2, :], lgf[0:META, h:h + 1], ALU.mult))
                B.run(stt(dec[:, 0:2, :], rel[:, 0:2, :], lgb[:, h:h + 1], dec[:, 0:2, :], ALU.mult, ALU.min))
                B.post(stt(dec[0:META, 2, :], rel[0:META, 2, :], lgb[0:META, h:h + 1], dec[0:META, 2, :], ALU.mult, ALU.min), "dec_arg")

            def decayed(h):
                eng.wait_ge(sems["dec_ready"], h + 1)
                eng.wait_ge(sems["ret_scores"], h + 1)
                b = 2 * (h % 2)
                B.run(stt(sd[:, h % 2, 0:2, :], aux[:, b, :].rearrange("p (a t) -> p a t", a=2), 0.125, dec[:, 0:2, :],
                          ALU.mult, ALU.mult))
                B.post(stt(sd[0:META, h % 2, 2, :], aux[0:META, b + 1, 0:S], 0.125, dec[0:META, 2, :], ALU.mult, ALU.mult), "sd_ready")

            decay_arg(0)
            decayed(0)
            decay_arg(1)
            for h in range(HEADS):
                eng.wait_ge(sems["ret_out"], h + 1)
                B.post(ve.tensor_copy(o_ret[:, h, :], aux[:, 2 * (h % 2) + 1, S:2 * S]), "o_ready")
                if h + 1 < HEADS:
                    decayed(h + 1)
                if h == 1:
                    low_norm()
                if h == 2:
                    low_lo()
                if h < 4:
                    pb = arrive(f"rg{h}")
                    g2 = rg[:, 2 * h:2 * h + 2, :]
                    B.post(tt(g2, proj[:, pb:pb + 2, 0:S], bc(rq, 2), ALU.mult), "gate_scaled")
                    eng.wait_ge(sems["gate_tanh"], h + 1)
                    freed(stt(g2, proj[:, pb:pb + 2, 0:S], 1.0, g2, ALU.add, ALU.mult))
                else:
                    pb = arrive(f"gm{h - 4}")
                    freed(tt(th_m[:, 2 * (h - 4):2 * (h - 4) + 2, :], proj[:, pb:pb + 2, 0:S], bc(rq, 2), ALU.mult))
                if h + 2 < HEADS:
                    decay_arg(h + 2)
            eng.wait_ge(sems["gn_sum"], 1)
            auxh = aux[:, :, :].rearrange("p a (b t) -> p (a b) t", b=2)
            B.post(stt(o_ret, auxh, -1.0 / P, o_ret, ALU.mult, ALU.add), "d_ready")

            def query_part(j):
                pb = arrive(f"uq{j}")
                src = proj[0:96, pb:pb + 2, :].rearrange("p a (b t) -> p (a b) t", b=2)
                freed(tt(q_pre[0:96, 4 * j:4 * j + 4, :], src, bc(r_all[0:96, 1, 0:S], 4), ALU.mult))

            def kv_part(half):
                if half == 0:
                    pump(index["ukv"])
                if half < 3:
                    eng.wait_ge(sems["kv_mm"], half + 1)
                else:
                    eng.wait_ge(sems["chunk_used"], index["ukv"] + 1)
                b = 2 * (half % 2)
                if half < 2:
                    for e in range(2):
                        ins = tt(pairs[0:64, e, 2 * half:2 * half + 2, :], proj[64 * e:64 * e + 64, b:b + 2, 0:L],
                                 bc(rkv[64 * e:64 * e + 64, :], 2), ALU.mult)
                        if e == 0:
                            B.run(ins)
                    B.post(ins, "kv_half")
                elif half == 2:
                    B.post(tt(v_feat[:, 0:2, :], proj[:, b:b + 2, 0:L], bc(rkv, 2), ALU.mult), "kv_half")
                else:
                    freed(tt(v_feat[:, 2:4, :], proj[:, b:b + 2, 0:L], bc(rkv, 2), ALU.mult))

            rkv = r_all[:, 2, :]
            pairs = k_all.rearrange("p (a e) t -> p e a t", e=2)
            query_part(0)
            for h in range(HEADS):
                B.run(stt(rg[:, h, :], o_ret[:, h, :], V("gn", h), rg[:, h, :], ALU.mult, ALU.mult))
            query_part(1)
            eng.wait_ge(sems["d_sq_ready"], 1)
            kv_part(0)
            eng.wait_ge(sems["gn_root"], 1)
            B.post(ve.reciprocal(rows8, rows8), "gn_factor")
            kv_part(1)
            for e in range(2):
                heads = slice(4 * e, 4 * e + 4)
                eng.wait_ge(sems["q_mla_rotated"], e + 1)
                B.post(tt(q_all[0:96, heads], auxh[0:96, heads], bc(C("sin_mla")[0:96, META:L], 4), ALU.mult), "q_sin")
            kv_part(2)
            kv_part(3)
            for e in range(2):
                heads = slice(4 * e, 4 * e + 4)
                eng.wait_ge(sems["gn_spread"], e + 1)
                ins = tt(rg[:, heads], rg[:, heads], auxh[:, heads], ALU.mult)
                if e == 0:
                    B.run(ins)
            B.post(ins, "y_ret_val")
            eng.wait_ge(sems["q_cos"], 1)
            B.post(tt(q_all[0:96], q_all[0:96], q_pre[0:96], ALU.add), "q_mla_roped")

            def soft_max(h):
                eng.wait_ge(sems["mla_scores"], h + 1)
                B.run(ve.reduce_max(mx, aux[:, 0:2, 0:L], AX_X))
                B.post(ts(nb, mx, -(96.0 ** -0.5), ALU.mult), "neg_max")
                eng.wait_ge(sems["mla_exp"], h + 1)
                B.run(ve.reciprocal(rs, sums))
                for b in range(2):
                    ins = ts(prob[:, h % 2, b, :], prob[:, h % 2, b, :], rs[:, b:b + 1], ALU.mult)
                    if b == 0:
                        B.run(ins)
                B.post(ins, "prob_ready")

            soft_max(0)
            for h in range(HEADS):
                eng.wait_ge(sems["prob_turned"], h + 1)
                B.run(ve.tensor_copy(pt[:, 0:2, :], aux[:, 2, :].rearrange("p (a t) -> p a t", a=2)))
                B.post(ve.tensor_copy(pt[0:META, 2, :], aux[0:META, 3, 0:S]), "pt_ready")
                if h + 1 < HEADS:
                    soft_max(h + 1)
                eng.wait_ge(sems["mla_out"], h + 1)
                p0 = 64 * (h % 2)
                B.post(ve.tensor_copy(o_mla(h // 2)[p0:p0 + 64, :], aux[p0:p0 + 64, 3, S:2 * S]), "o_mla_ready")
                y2 = yr[:, 2 * (h % 4):2 * (h % 4) + 2, :]
                if h < 4:
                    b = arrive(f"gr{h}")
                    freed(tt(y2, proj[:, b:b + 2, 0:S], bc(rq, 2), ALU.mult))
                else:
                    b = arrive(f"ro{h - 4}")
                    eng.wait_ge(sems["gate_tanh"], h + 5)
                    freed(stt(y2, y2, 1.0, proj[:, b:b + 2, 0:S], ALU.add, ALU.mult))
                if h >= 5:
                    for a in (0, 1) if h == 5 else (h - 4,):
                        eng.wait_ge(sems["y_mla_hi"], a + 1)
                        B.post(tt(u[:, 1, a, META:L], o_mla(a), hi32(u[:, 0, a, META:L]), ALU.subtract), "y_mla_ready")
                if h == 1:
                    eng.wait_ge(sems["y_ret_hi"], 1)
                    B.post(stt(v[:, 1, :, :], rg, 0.5, hi32(v[:, 0, :, :]), ALU.mult, ALU.subtract), "y_ret_ready")
            for c in range(2):
                b = arrive(f"mo{c}")
                for e in range(2):
                    j = 2 * c + e
                    pair = slice(2 * j, 2 * j + 2)
                    ins = stt(th_m[:, pair], th_m[:, pair], 1.0, proj[:, b + e, :].rearrange("p (b t) -> p b t", b=2), ALU.add, ALU.mult)
                    (freed if e else B.run)(ins)
                    B.post(tt(yr[:, pair], yr[:, pair], th_m[:, pair], ALU.add), "merged")
                for j in (2 * c, 2 * c + 1):
                    pair = slice(2 * j, 2 * j + 2)
                    eng.wait_ge(sems["merged_hi"], j + 1)
                    B.post(stt(v[:, 1, pair, :], yr[:, pair], 0.5, hi32(v[:, 0, pair, :]), ALU.mult, ALU.subtract), "merged_ready")

            def add_blocks(name, gain, norm_no):
                for c in range(4):
                    b = arrive(f"{name}{c}")
                    t = x2[:, 2 * c:2 * c + 2, :]
                    freed(tt(t, t, proj[:, b:b + 2, 0:S], ALU.add))
                    pump(index[f"{name}{min(c + 1, 3)}"])
                    lo_pair(c, gain, norm_no)

            rms = r_all[:, 0, 0:S]

            def token_factors(no):
                eng.wait_ge(sems["r_turned"], no)
                B.post(ve.tensor_copy(r_tok, aux[:, 0, 0:2]), "r_tok_ready")

            def norm_scale(norm_no):
                eng.wait_ge(sems["root_ready"], norm_no + 3)
                B.post(ve.reciprocal(rms, rms), "rms_ready")

            def hidden_layer(d, no, gain=None, norm_no=None):
                tag, n_h, k0 = d["tag"], d["n"], d["k0"]
                g = loop_first[tag]

                def step(n, k, i=None):
                    if i is not None:
                        split(n + AHEAD, i)
                    elif k != n_h - 1:
                        pump(n)
                    if k is None:
                        return
                    kk = (lambda c: k0 + k + c if i is None else i * 2 + (k0 + k + c))
                    eng.wait_ge(sems["chunk_used"], at(lambda m: m + 1, n, i))
                    b, slot = 2 * (k % 2), 2 * (k % 2)
                    if tag == "ffn":
                        g0, hid = f("f1", 0, S), f("f1", 256, S)
                        B.post(tt(g0, proj[:, b, 0:S], rms, ALU.mult), "ffn_gate_scaled")
                        eng.wait_ge(sems["ffn_gate_tanh"], kk(1))
                        B.run(stt(g0, proj[:, b, 0:S], 1.0, g0, ALU.add, ALU.mult))
                        B.post(tt(hid, g0, proj[:, b + 1, 0:S], ALU.mult), "hidden_val")
                        eng.wait_ge(sems["hidden_hi"], kk(1))
                        B.post(tt(v[:, 1, slot, :], hid, hi32(v[:, 0, slot, :]), ALU.subtract), "hidden_ready")
                    else:
                        rl, hid = f("f1", 0, 2, S), f("f1", 512, 2, S)
                        B.run(ts(rl, proj[:, b:b + 2, 0:S], 0.0, ALU.max))
                        B.post(tt(hid, rl, rl, ALU.mult), "hidden_val")
                        eng.wait_ge(sems["hidden_hi"], kk(1))
                        B.post(tt(v[:, 1, slot:slot + 2, :], hid, hi32(v[:, 0, slot:slot + 2, :]), ALU.subtract), "hidden_ready")

                step(g, 0)
                turns = (n_h - 2) // 2
                with eng.Fori(0, turns) as i:
                    B.enter(i, {"lo_ready": 4, "hidden_val": 2, "hidden_ready": 2, "dve_step": 2,
                                "ffn_gate_scaled": 2 if tag == "ffn" else 0})
                    step(g + 1, 1, i)
                    step(g + 2, None, i)
                    step(g + 3, 2, i)
                    step(g + 4, None, i)
                B.leave(turns)
                done[0] += 4 * turns
                step(g + 2 * n_h - 3, n_h - 1)
                pump(g + 2 * n_h - 3)
                if tag != "ffn":
                    B.run(tt(rms, rms, rms, ALU.mult))
                for c in range(4):
                    if c < 3:
                        eng.wait_ge(sems["down_bank"], 3 * no + c + 1)
                    else:
                        eng.wait_ge(sems["chunk_used"], g + 2 * n_h)
                    t = f("f1", 512 * (c % 2), 2, S)
                    B.run(stt(t, auxh[:, 2 * c:2 * c + 2, :], 0.5 if tag == "ffn" else 1.0, bc(rms, 2), ALU.mult, ALU.mult))
                    pair = x2[:, 2 * c:2 * c + 2, :]
                    B.post(tt(pair, pair, t, ALU.add), "final_ready" if tag == "m1" else "x_new")
                    if gain and c:
                        lo_pair(c - 1, gain, norm_no)
                if gain:
                    lo_pair(3, gain, norm_no)
                    pump(loop_last[no] - 1)

            add_blocks("wo", lambda k: V("ffn", k), 1)
            norm_scale(1)
            hidden_layer(FFN, 0, lambda k: both_gains[:, k:k + 1], 2)

            rf, rm = r_all[:, 1, 0:S], r_all[:, 2, 0:S]
            eng.wait_ge(sems["root_ready"], 5)
            B.run(ve.reciprocal(rf, rms))
            B.run(tt(rm, rf, rf, ALU.mult))
            B.post(tt(rm, rm, aux[:, 1, 0:S], ALU.mult), "second_mean")
            eng.wait_ge(sems["second_root"], 1)
            B.run(ve.reciprocal(rm, rm))
            B.post(tt(rms, rf, rm, ALU.mult), "rms_ready")
            pre = (f("f1", 0, 4, S), f("f1", 1024, 4, S))
            fin = (f("f3", 0, 4, S), f("f3", 1024, 4, S))
            B.run(ts(qg8, V("sb_q"), 0.125, ALU.mult))
            for j, name in enumerate(("sq", "sk")):
                for c in range(2):
                    b = arrive(f"{name}{c}", urgent=j == c == 0)
                    freed(tt(pre[j][:, 2 * c:2 * c + 2, :], proj[:, b:b + 2, 0:S], bc(rms, 2), ALU.mult))
                    if j == 0:
                        for k in range(4 * c, 4 * c + 4):
                            B.run(stt(x2[:, k, :], x2[:, k, :], V("final", k), rf, ALU.mult, ALU.mult))
            def per_token(name, dst, width=256):
                b = arrive(name)
                for j in range(2):
                    ins = ts(dst(j), proj[:, b + j, 0:width], r_tok[:, j:j + 1], ALU.mult)
                    if j == 0:
                        B.run(ins)
                freed(ins)

            token_factors(1)
            eng.wait_ge(sems["late_in"], 16)
            eng.wait_ge(sems["sg_turned"], 1)
            causal = LC("mask_causal")[:, 0:P]
            B.post(tt(f("f6", 0, 8, P), aux[:, 2:4, :].rearrange("p a (g t) -> p (a g) t", g=4), bc(causal, 8), ALU.mult), "sg_t_ready")
            sb_v, za, vg = f("f5", 0, 2, 512), f("f4", 0, 2, D), f("f5", 1024, 2, 512)
            strict = bc(LC("mask_strict"), 2)

            def za_part(a):
                per_token(f"za{a}", lambda j: za[:, j, a * 256:(a + 1) * 256])

            za_part(0)
            B.run(ve.tensor_copy(f("f5", 0, 16, 64)[0:16], C("ident")[0:16, 0:16][:, :, None].to_broadcast([16, 16, 64])))
            eng.wait_ge(sems["sb_root"], 1)
            B.post(ve.reciprocal(rows16, rows16), "sb_factor")
            za_part(1)
            for j in range(2):
                eng.wait_ge(sems["sb_spread"], j + 1)
                ins = stt(fin[j], pre[j], qg8 if j == 0 else V("sb_k"), auxh[:, 4 * j:4 * j + 4], ALU.mult, ALU.mult)
                if j == 0:
                    B.run(ins)
            B.post(ins, "sb_qk_ready")
            za_part(2)

            def sb_z(a):
                eng.wait_ge(sems["sb_scores"], a + 1)
                if a >= 2:
                    eng.wait_ge(sems["sb_exp"], a - 1)
                B.post(tt(f("f2", 768 * (a % 2), 2, 384), aux[:, 2 * (a % 2):2 * (a % 2) + 2, 0:384], strict, ALU.mult), "sb_z")

            def sb_soft(a):
                zm, soft = f("f2", 768 * (a % 2), 2, 384), f("f1", 768 * a, 2, 384)
                eng.wait_ge(sems["sb_log"], a + 1)
                B.run(stt(soft, zm, 0.0, soft, ALU.max, ALU.add))
                B.post(tt(soft, soft, strict, ALU.mult), "sb_soft")

            def sb_arg(a):
                zm = f("f2", 768 * (a % 2), 2, 384)
                eng.wait_ge(sems["sb_suffix"], a + 1)
                B.post(tt(zm, zm, aux[:, 2 * (a % 2):2 * (a % 2) + 2, 0:384], ALU.add), "sb_arg")

            def sb_attn(a):
                attn = f("f1", 768 * a, 2, 384)
                eng.wait_ge(sems["sb_exp"], a + 1)
                B.post(tt(attn, attn, strict, ALU.mult), "sb_attn")

            def value_part(c):
                per_token(f"sv{c}", lambda j: sb_v[:, j, c * 256:(c + 1) * 256])

            sb_z(0)
            sb_z(1)
            sb_soft(0)
            sb_soft(1)
            za_part(3)
            sb_arg(0)
            sb_arg(1)
            eng.wait_ge(sems["gelu_ready"], 1)
            B.run(ve.reduce_sum(stat[:, 0:2], za[:, :, 512:1024], AX_X))
            B.run(ts(stat[:, 0:2], stat[:, 0:2], 1.0 / 512, ALU.mult))
            for b in range(2):
                ins = ts(vg[:, b, :], za[:, b, 512:1024], stat[:, b:b + 1], ALU.subtract)
                if b == 0:
                    B.run(ins)
            B.post(ins, "vg_centred")
            value_part(0)
            sb_z(2)
            sb_z(3)
            sb_attn(0)
            sb_attn(1)
            eng.wait_ge(sems["vg_root"], 1)
            B.run(ve.reciprocal(stat[:, 4:6], stat[:, 4:6]))
            ln = f("f6", 1024, 2, 512)
            for b in range(2):
                B.run(stt(vg[:, b, :], vg[:, b, :], stat[:, 4 + b:5 + b], ln[:, 0, :], ALU.mult, ALU.mult))
            B.post(tt(vg, vg, bc(ln[:, 1, :], 2), ALU.add), "vg_ready")
            value_part(1)
            sb_soft(2)
            sb_soft(3)
            eng.wait_ge(sems["mixed"], 1)
            pb = 2 * (order["mixed"] % 2)
            for g in range(8):
                c = slice(g * 64, (g + 1) * 64)
                m = proj[:, pb + g // 4, (g % 4) * P:(g % 4 + 1) * P].rearrange("p (b c) -> p b c", b=2)
                ins = stt(vg[:, :, c], m, V("sg_b", g), za[:, :, c], ALU.add, ALU.mult)
                if g < 7:
                    B.run(ins)
            freed(ins)
            sb_arg(2)
            sb_arg(3)
            sb_attn(2)
            sb_attn(3)
            eng.wait_ge(sems["sb_out"], 2)
            B.post(ve.tensor_copy(f("f2", 0, 2, S), aux[:, 0, :].rearrange("p (b t) -> p b t", b=2)), "sb_out_ready")
            eng.wait_ge(sems["ya_turned"], 1)
            pb = 2 * (order["ya_turn"] % 2)
            freed(ve.tensor_copy(f("f4", 0, 4, S), proj[:, pb:pb + 2, :].rearrange("p a (b t) -> p (a b) t", b=2)))
            eng.wait_ge(sems["sb_out"], 4)
            B.post(ve.tensor_copy(f("f2", 512, 2, S), aux[:, 1, :].rearrange("p (b t) -> p b t", b=2)), "sb_out_ready")
            eng.wait_ge(sems["y_even_hi"], 1)
            B.post(tt(v[:, 1, 0:4, :], f("f4", 0, 4, S), hi32(v[:, 0, 0:4, :]), ALU.subtract), "y_even_ready")
            eng.wait_ge(sems["y_even_hi"], 2)
            B.post(tt(v[:, 1, 4:8, :], f("f2", 0, 4, S), hi32(v[:, 0, 4:8, :]), ALU.subtract), "y_even_ready")
            add_blocks("eo", lambda k: V("mlp2", k), 3)
            norm_scale(3)
            hidden_layer(M0, 1, lambda k: V("mix2", 8 + k), 4)

            norm_scale(4)
            b = arrive("gates")
            token_factors(2)
            B.run(ts(gat[:, 0:8], proj[:, b, 0:8], r_tok[:, 0:1], ALU.mult))
            freed(ts(gat[:, 8:16], proj[:, b + 1, 0:8], r_tok[:, 1:2], ALU.mult))
            ga = gat.rearrange("p (b c) -> p b c", b=2)
            ib = PAR_COLS["i_b"][0]
            B.post(tt(ga, ga, bc(par[:, ib:ib + 8], 2), ALU.add), "gates_raw")
            eng.wait_ge(sems["gates_log"], 1)
            ab = f("f6", 0, 8).rearrange("p (b c) -> p b c", b=2)
            B.post(stt(ga[:, :, 4:8], ga[:, :, 4:8], 0.0, ab, ALU.min, ALU.subtract), "gates_ready")
            rows, cum, ones_row = f("f6", 1536, 3, S)[0:4], f("f6", 1280, S)[0:4], f("f6", 1024, S)[0:4]
            conv_in, conv_out = f("f1", 0, 8, S + 3), f("f3", 0, 8, S)
            B.run(ve.memset(ones_row, 1.0))
            B.run(ve.memset(conv_in[:, :, 0:3], 0.0))
            b = arrive("qk0")
            freed(tt(conv_in[:, 0:2, 3:S + 3], proj[:, b:b + 2, 0:S], bc(rms, 2), ALU.mult))
            eng.wait_ge(sems["gates_turned"], 1)
            B.run(ve.tensor_copy(rows[:, 1, :], aux[0:4, 2, 0:S]))
            B.run(ve.tensor_tensor_scan(cum, ones_row, rows[:, 1, :], 0.0, ALU.mult, ALU.add))
            B.run(tt(rows[:, 0, :], aux[0:4, 1, 0:S], cum, ALU.subtract))
            B.run(ve.tensor_tensor_scan(rows[:, 1, :], rows[:, 0, :], rows[:, 0, :], 0.0, ALU.max, ALU.max))
            B.post(tt(rows[:, 2, :], cum, rows[:, 1, :], ALU.add), "rows_ready")

            def conv(c):
                for k in (2 * c, 2 * c + 1):
                    o = conv_out[:, k, :]
                    ins = ts(o, conv_in[:, k, 0:S], V("conv_w", k), ALU.mult, V("conv_b", k), ALU.add)
                    for q in range(1, 4):
                        B.run(ins)
                        ins = stt(o, conv_in[:, k, q:q + S], V("conv_w", 8 * q + k), o, ALU.mult, ALU.add)
                    if k % 2 == 0:
                        B.run(ins)
                B.post(ins, "conv_ready")

            def conv_silu(c):
                t = conv_out[:, 2 * c:2 * c + 2, :]
                eng.wait_ge(sems["conv_tanh"], c + 1)
                B.post(stt(t, f("f2", 0, 8, S)[:, 2 * c:2 * c + 2, :], 1.0, t, ALU.add, ALU.mult), "conv_done")

            def qk_part(c):
                b = arrive(f"qk{c}")
                freed(tt(conv_in[:, 2 * c:2 * c + 2, 3:S + 3], proj[:, b:b + 2, 0:S], bc(rms, 2), ALU.mult))

            ov, osd_of = f("f5", 0, 2, D), lambda h: f("f6", 1536 + 384 * (h % 2), 384)
            ow = lambda h: f("f6", 384 * h, 384)
            oh, og = f("f1", 0, 8, S), f("f4", 0, 8, S)
            dmax, mean = r_all[:, 1, 0:S], r_all[:, 2, 0:S]
            a_cols = small[:, 54:62]

            def v_part(c):
                per_token(f"ov{c}", lambda j: ov[:, j, c * 256:(c + 1) * 256])

            def og_part(h):
                b = arrive(f"og{h}")
                freed(tt(og[:, 2 * h:2 * h + 2, :], proj[:, b:b + 2, 0:S], bc(rms, 2), ALU.mult))

            def o_weights(h):
                eng.wait_ge(sems["o_scores"], h + 1)
                if h >= 2:
                    eng.wait_ge(sems["o_num"], h - 1)
                B.post(stt(osd_of(h), aux[:, h % 2, 0:384], 0.25 * 128.0 ** -0.5, ow(h), ALU.mult, ALU.mult), "osd_ready")

            def o_denominator(h):
                eng.wait_ge(sems["o_den"], h + 1)
                B.run(stt(dmax, aux[:, 2, 0:S], -1.0, f("f1", 2072, 4, S)[:, h, :], ALU.mult, ALU.max))
                B.run(tt(dmax, aux[:, 2, 0:S], dmax, ALU.max))
                B.post(stt(dmax, dmax, EPS, dmax, ALU.mult, ALU.mult), "o_max")

            def o_mean(h):
                eng.wait_ge(sems["o_sum"], h + 1)
                B.post(stt(mean, aux[:, h % 2, 0:S], 1.0 / 256, dmax, ALU.mult, ALU.add), "o_mean")

            def o_norm(h):
                eng.wait_ge(sems["o_root"], h + 1)
                B.run(ve.reciprocal(mean, mean))
                t = oh[:, 2 * h:2 * h + 2, :]
                B.run(tt(t, t, bc(mean, 2), ALU.mult))

            def y_value(h):
                t = oh[:, 2 * h:2 * h + 2, :]
                eng.wait_ge(sems["gate_tanh"], 13 + h)
                B.post(stt(t, og[:, 2 * h:2 * h + 2, :], 1.0, t, ALU.add, ALU.mult), "y_odd_val")

            def y_lo(h):
                eng.wait_ge(sems["y_odd_hi"], h + 1)
                pair = slice(2 * h, 2 * h + 2)
                B.post(stt(v[:, 1, pair, :], oh[:, pair, :], 0.5, hi32(v[:, 0, pair, :]), ALU.mult, ALU.subtract), "y_odd_ready")

            conv(0)
            qk_part(1)
            eng.wait_ge(sems["a_turned"], 1)
            B.post(ve.tensor_copy(a_cols, aux[:, 0, 0:8]), "a_cols_ready")
            conv(1)
            conv_silu(0)
            qk_part(2)
            eng.wait_ge(sems["o_spread"], 1)
            for h in range(4):
                B.run(ts(ow(h)[:, 0:S], aux[:, h, 0:S], a_cols[:, h:h + 1], ALU.subtract, 0.0, ALU.max))
                ins = ts(ow(h)[:, S:384], aux[:, h, P:S], a_cols[:, 4 + h:5 + h], ALU.subtract, 0.0, ALU.max)
                if h < 3:
                    B.run(ins)
            B.post(ins, "ow_arg")
            conv(2)
            conv_silu(1)
            qk_part(3)
            conv(3)
            conv_silu(2)
            eng.wait_ge(sems["ow_exp"], 1)
            ow4 = f("f6", 0, 4, 384)
            B.run(tt(ow4, ow4, bc(LC("mask_causal"), 4), ALU.mult))
            conv_silu(3)
            v_part(0)
            v_part(1)
            o_weights(0)
            v_part(2)
            o_denominator(0)
            o_weights(1)
            v_part(3)
            o_mean(0)
            o_denominator(1)
            o_weights(2)
            o_norm(0)
            og_part(0)
            o_mean(1)
            o_denominator(2)
            o_weights(3)
            o_norm(1)
            og_part(1)
            o_mean(2)
            o_denominator(3)
            o_norm(2)
            og_part(2)
            o_mean(3)
            o_norm(3)
            for h in range(3):
                y_value(h)
            for h in range(3):
                y_lo(h)
            og_part(3)
            y_value(3)
            y_lo(3)
            add_blocks("oo", lambda k: V("mlp2", 8 + k), 5)
            norm_scale(5)
            hidden_layer(M1, 2)


def host_constants():
    import numpy as np

    def rope(half, rows):
        inv = np.float32(10000.0) ** (-np.arange(half, dtype=np.float32) / np.float32(half))
        ang = np.arange(L, dtype=np.float32)[None, :] * inv[rows % half][:, None]
        return np.cos(ang), np.sin(ang)

    def rotation(size, starts, half):
        m = np.zeros((P, size), np.float32)
        for s in starts:
            for j in range(half):
                m[s + half + j, s + j] = -1.0
                m[s + j, s + half + j] = 1.0
        return m

    p = np.arange(P)
    one = np.ones((P, P), np.float32)
    cr, sr = rope(32, p)
    cm, sm = rope(16, p[:32])
    cos_m, sin_m = np.ones((P, L), np.float32), np.zeros((P, L), np.float32)
    cos_m[64:96], sin_m[64:96] = cm, sm
    pair = (p[:, None] // 64 + 14 == np.arange(30)[None, :]).astype(np.float32)
    rel = np.stack([META + np.arange(S)[None, :] - (p[:, None] + t) for t, _ in KEY_BLOCKS], 1)
    parts = {"ident": np.eye(P), "ones": one, "pick16": pair, "neg_tri": -np.tril(one), "neg_ones": -one,
             "rot_ret": rotation(P, (0, 64), 32), "rot_mla": rotation(96, (64,), 16), "cos_ret": cr, "sin_ret": sr,
             "cos_mla": cos_m, "sin_mla": sin_m, "rel": rel.reshape(P, 3 * S), "pick8": np.repeat(np.arange(16)[None] == 7, P, 0)}
    consts = np.concatenate([np.asarray(parts[k], np.float32) for k in CONST_COLS], 1)
    t = np.concatenate([np.arange(S), np.arange(P)])[None, :]
    pick = np.zeros((P, 4, P), np.float32)
    for h in range(4):
        pick[h, h] = 1.0
    lates = {"mask_strict": p[:, None] < t, "mask_causal": p[:, None] <= t, "pick_head": pick.reshape(P, 512)}
    late = np.concatenate([np.asarray(lates[k], np.float32) for k in LATE_COLS], 1)
    return np.ascontiguousarray(consts), np.ascontiguousarray(late)


def packed_vectors(a):
    import numpy as np

    def col(x):
        return np.reshape(x, (-1, P)).T

    def rows(x):
        return np.broadcast_to(np.reshape(x, (1, -1)), (P, np.size(x)))

    parts = {"norm_mix": col(a["norm_mix_w"]), "gn": col(a["ret_gn_w"]), "q_norm": col(a["mla_q_norm_w"]),
             "kv_norm": col(a["mla_kv_norm_w"]), "ffn": col(a["norm_ffn_w"]), "final": col(a["norm_final_w"]),
             "mix2": col(a["mix_norm_g_2"]), "mlp2": col(a["mlp_norm_g_2"]), "conv_w": col(a["od_conv_w_2"]),
             "conv_b": col(a["od_conv_b_2"]), "on": col(a["od_out_norm_g_2"]),
             "sb_q": col(np.tile(np.ravel(a["sb_q_norm_g_2"]), 2)), "sb_k": col(np.tile(np.ravel(a["sb_k_norm_g_2"]), 2)),
             "sg_b": col(a["sg_b_2"]), "decay_f": rows(a["ret_decay_fwd"]), "decay_b": rows(a["ret_decay_bwd"]),
             "i_b": rows(a["od_i_b_2"]), "f_b": rows(a["od_f_b_2"])}
    params = np.ascontiguousarray(np.concatenate([parts[k] for k in PAR_COLS], 1))
    ln_gb = np.ascontiguousarray(np.stack([rows(a["sg_ln_g_2"]), rows(a["sg_ln_b_2"])], 1))
    return params, ln_gb


_WHOLE = ["x", "meta_tokens", "w_in", "w_ret_out", "w_uq", "w_uk", "w_uv", "w_mla_out", "w_o", "w_ffn_gate", "w_ffn_up",
          "w_ffn_down", "mlp_w1_2", "mlp_w2_2", "ev_w_in_2", "ev_w_out_2", "sg_w_2", "od_w_in_2", "od_w_out_2"]


def kernel(**inputs):
    import numpy as _np
    import concourse.bacc as _bacc
    from concourse import mybir as _mybir
    from concourse.bass_utils import run_bass_kernel_spmd as _run

    nc = _bacc.Bacc("TRN2", target_bir_lowering=False, num_devices=1)
    host = {k: _np.asarray(v) for k, v in inputs.items()}
    arrays, w = {}, {}

    def give(name, a):
        a = _np.ascontiguousarray(a)
        arrays[f"in_{name}_dram"] = a
        return nc.dram_tensor(f"in_{name}_dram", a.shape, _mybir.dt.from_np(a.dtype), kind="ExternalInput").ap()

    for name in _WHOLE:
        w[name] = give(name, host[name])
    params, ln_gb = packed_vectors(host)
    consts, late = host_constants()
    extra = [give(n, a) for n, a in (("params", params), ("consts", consts), ("late", late), ("ln_gb", ln_gb))]
    out = nc.dram_tensor("out_0_dram", (1, S, D), _mybir.dt.float32, kind="ExternalOutput").ap()
    build(nc, w, *extra, out)
    r = _run(nc, [arrays], core_ids=[0])
    return r.results[0]["out_0_dram"]
```
